# Optimizing a Trainium2 kernel written in Bass

```python
import jax, jax.numpy as jnp
from jax import lax
import numpy as np

D_MODEL = 1024
BATCH = 1
SEQ = 512
DEPTH = 2

GRID_W = 64
CTX_LEN = 256
HEAD_DIM = 64
N_MIXERS = 4
GROUP_HEADS = D_MODEL // (N_MIXERS * HEAD_DIM)
GROUP_WIDTH = GROUP_HEADS * HEAD_DIM
KV_HEADS = GROUP_HEADS // 2
KV_WIDTH = KV_HEADS * HEAD_DIM
Q_BLOCK = 128
WINDOW = 128
ROPE_THETA = 10000.0
GLA_DK = HEAD_DIM // 2
GLA_KW = GROUP_HEADS * GLA_DK
GLA_GATE_RANK = 16
GLA_GATE_TAU = 16.0
GLA_CHUNK = 64
MLSTM_CHUNK = 64
D_FF = 4 * D_MODEL
N_MOD = 6
EPS = 1e-6
NEG = -1e30
IN_SPLITS = (GROUP_WIDTH, KV_WIDTH, KV_WIDTH,
             GROUP_WIDTH, KV_WIDTH, KV_WIDTH,
             GLA_KW, GLA_KW, GROUP_WIDTH, GROUP_WIDTH, 2 * GLA_GATE_RANK,
             GROUP_WIDTH, GROUP_WIDTH, GROUP_WIDTH, GROUP_WIDTH,
             2 * GROUP_HEADS, 2 * GROUP_HEADS)
IN_WIDTH = sum(IN_SPLITS)

kernel_name = 'hybrid_parallel_heads_dit_block'

def rms_norm(x, g):
    xf = x.astype(jnp.float32)
    y = xf * lax.rsqrt(jnp.mean(xf * xf, axis=-1, keepdims=True) + EPS)
    return (y * g.astype(jnp.float32)).astype(x.dtype)

def heads(a, dim=HEAD_DIM):
    return a.reshape(a.shape[:-1] + (-1, dim))

def _flip(a):
    return jnp.flip(a, axis=1)

def _ident(a):
    return a

def axial_rope(n_tokens):
    rows = n_tokens // GRID_W
    row = jnp.repeat(jnp.arange(rows, dtype=jnp.float32), GRID_W)
    col = jnp.tile(jnp.arange(GRID_W, dtype=jnp.float32), rows)
    n_freq = HEAD_DIM // 4
    inv = ROPE_THETA ** (-jnp.arange(n_freq, dtype=jnp.float32) / n_freq)
    ang = jnp.concatenate([row[:, None] * inv, col[:, None] * inv], axis=-1)
    return jnp.cos(ang), jnp.sin(ang)

def apply_rope(x, cos, sin):
    xf = x.astype(jnp.float32)
    x1, x2 = xf[..., 0::2], xf[..., 1::2]
    c, s = cos[:, None, :], sin[:, None, :]
    y = jnp.stack([x1 * c - x2 * s, x1 * s + x2 * c], axis=-1).reshape(x.shape)
    return y.astype(x.dtype)

def context_attention(q, k, v, sink):
    B_, L, H, d = q.shape
    G = k.shape[2]
    R = H // G
    qg = q.reshape(B_, L, G, R, d)
    s = jnp.einsum('blgrd,bmgd->bgrlm', qg, k, preferred_element_type=jnp.float32) * d ** -0.5
    if sink is not None:
        s_sink = jnp.broadcast_to(sink.astype(jnp.float32).reshape(1, G, R, 1, 1), s.shape[:-1] + (1,))
        s = jnp.concatenate([s, s_sink], axis=-1)
    w = jax.nn.softmax(s, axis=-1)[..., :L]
    o = jnp.einsum('bgrlm,bmgd->blgrd', w.astype(v.dtype), v)
    return o.reshape(B_, L, H * d)

def global_block_attention(q, k, v, k_c, v_c):
    B_, S, H, d = q.shape
    G = k.shape[2]
    R = H // G
    nb = S // Q_BLOCK
    scale = d ** -0.5
    qb = q.reshape(B_, nb, Q_BLOCK, G, R, d).transpose(1, 0, 2, 3, 4, 5)

    def one_block(qi):
        s_lat = jnp.einsum('bqgrd,bkgd->bgrqk', qi, k, preferred_element_type=jnp.float32) * scale
        s_ctx = jnp.einsum('bqgrd,bcgd->bgrqc', qi, k_c, preferred_element_type=jnp.float32) * scale
        w = jax.nn.softmax(jnp.concatenate([s_lat, s_ctx], axis=-1), axis=-1).astype(v.dtype)
        return (jnp.einsum('bgrqk,bkgd->bqgrd', w[..., :S], v)
                + jnp.einsum('bgrqc,bcgd->bqgrd', w[..., S:], v_c))

    o = lax.map(one_block, qb)
    return o.transpose(1, 0, 2, 3, 4, 5).reshape(B_, S, H * d)

def window_block_attention(q, k, v, k_c, v_c, sink):
    B_, S, H, d = q.shape
    G = k.shape[2]
    R = H // G
    L = k_c.shape[1]
    nb = S // Q_BLOCK
    scale = d ** -0.5
    pad = ((0, 0), (Q_BLOCK, Q_BLOCK), (0, 0), (0, 0))
    kp = jnp.pad(k, pad).reshape(B_, nb + 2, Q_BLOCK, G, d)
    vp = jnp.pad(v, pad).reshape(B_, nb + 2, Q_BLOCK, G, d)
    kw = jnp.concatenate([kp[:, :-2], kp[:, 1:-1], kp[:, 2:]], axis=2)
    vw = jnp.concatenate([vp[:, :-2], vp[:, 1:-1], vp[:, 2:]], axis=2)
    qb = q.reshape(B_, nb, Q_BLOCK, G, R, d)
    s_win = jnp.einsum('bnqgrd,bnkgd->bngrqk', qb, kw, preferred_element_type=jnp.float32) * scale
    qpos = jnp.arange(nb)[:, None] * Q_BLOCK + jnp.arange(Q_BLOCK)[None, :]
    kpos = jnp.arange(nb)[:, None] * Q_BLOCK - Q_BLOCK + jnp.arange(3 * Q_BLOCK)[None, :]
    ok = ((jnp.abs(qpos[:, :, None] - kpos[:, None, :]) <= WINDOW)
          & (kpos >= 0)[:, None, :] & (kpos < S)[:, None, :])
    s_win = jnp.where(ok[None, :, None, None], s_win, NEG)
    s_ctx = jnp.einsum('bnqgrd,bcgd->bngrqc', qb, k_c, preferred_element_type=jnp.float32) * scale
    s_sink = jnp.broadcast_to(sink.astype(jnp.float32).reshape(1, 1, G, R, 1, 1), s_ctx.shape[:-1] + (1,))
    w = jax.nn.softmax(jnp.concatenate([s_win, s_ctx, s_sink], axis=-1), axis=-1).astype(v.dtype)
    K3 = 3 * Q_BLOCK
    o = (jnp.einsum('bngrqk,bnkgd->bnqgrd', w[..., :K3], vw)
         + jnp.einsum('bngrqc,bcgd->bnqgrd', w[..., K3:K3 + L], v_c))
    return o.reshape(B_, S, H * d)

def gla_scan(q, k, v, log_a, state):
    B_, T, H, _ = q.shape
    dv = v.shape[-1]
    nc = T // GLA_CHUNK
    tri = jnp.tril(jnp.ones((GLA_CHUNK, GLA_CHUNK), dtype=bool))

    def chunks(a):
        return a.astype(jnp.float32).reshape(B_, nc, GLA_CHUNK, H, a.shape[-1]).transpose(1, 0, 3, 2, 4)

    def step(S, inp):
        qc, kc, vc, la = inp
        b = jnp.cumsum(la, axis=2)
        rel = jnp.where(tri[:, :, None], b[:, :, :, None, :] - b[:, :, None, :, :], -jnp.inf)
        scores = jnp.einsum('bhtd,bhsd,bhtsd->bhts', qc, kc, jnp.exp(rel))
        o = (jnp.einsum('bhts,bhsv->bhtv', scores, vc)
             + jnp.einsum('bhtd,bhdv->bhtv', qc * jnp.exp(b), S))
        b_end = b[:, :, -1:, :]
        S = (jnp.exp(b_end[:, :, 0, :])[..., None] * S
             + jnp.einsum('bhsd,bhsv->bhdv', kc * jnp.exp(b_end - b), vc))
        return S, o

    S, o = lax.scan(step, state, (chunks(q), chunks(k), chunks(v), chunks(log_a)))
    return o.transpose(1, 0, 3, 2, 4).reshape(B_, T, H, dv), S

def mlstm_scan(q, k, v, i_pre, log_f, state):
    B_, T, H, _ = q.shape
    dv = v.shape[-1]
    nc = T // MLSTM_CHUNK
    tri = jnp.tril(jnp.ones((MLSTM_CHUNK, MLSTM_CHUNK), dtype=bool))

    def chunks4(a):
        return a.astype(jnp.float32).reshape(B_, nc, MLSTM_CHUNK, H, a.shape[-1]).transpose(1, 0, 3, 2, 4)

    def chunks3(a):
        return a.astype(jnp.float32).reshape(B_, nc, MLSTM_CHUNK, H).transpose(1, 0, 3, 2)

    def step(carry, inp):
        C, n, m = carry
        qc, kc, vc, ic, fc = inp
        F = jnp.cumsum(fc, axis=-1)
        logw = jnp.where(tri, F[..., :, None] - F[..., None, :] + ic[..., None, :], -jnp.inf)
        log_inter = F + m[..., None]
        m_t = jnp.maximum(log_inter, jnp.max(logw, axis=-1))
        w = jnp.exp(logw - m_t[..., None])
        w_inter = jnp.exp(log_inter - m_t)
        qk = jnp.einsum('bhtd,bhsd->bhts', qc, kc) * w
        num = (jnp.einsum('bhts,bhsv->bhtv', qk, vc)
               + w_inter[..., None] * jnp.einsum('bhtd,bhdv->bhtv', qc, C))
        den = jnp.sum(qk, axis=-1) + w_inter * jnp.einsum('bhtd,bhd->bht', qc, n)
        h = num / jnp.maximum(jnp.abs(den), jnp.exp(-m_t))[..., None]
        F_end = F[..., -1]
        log_end = F_end[..., None] - F + ic
        m_new = jnp.maximum(F_end + m, jnp.max(log_end, axis=-1))
        w_end = jnp.exp(log_end - m_new[..., None])
        decay = jnp.exp(F_end + m - m_new)
        C = decay[..., None, None] * C + jnp.einsum('bhs,bhsd,bhsv->bhdv', w_end, kc, vc)
        n = decay[..., None] * n + jnp.einsum('bhs,bhsd->bhd', w_end, kc)
        return (C, n, m_new), h

    state, h = lax.scan(step, state, (chunks4(q), chunks4(k), chunks4(v), chunks3(i_pre), chunks3(log_f)))
    return h.transpose(1, 0, 3, 2, 4).reshape(B_, T, H, dv), state

def mixer_global_gqa(z, zc, p, cos, sin, ctx_out):
    q = apply_rope(rms_norm(heads(z[0]), p['g_q_a']), cos, sin)
    k = apply_rope(rms_norm(heads(z[1]), p['g_k_a']), cos, sin)
    v = heads(z[2])
    k_c = rms_norm(heads(zc[1]), p['g_k_a'])
    v_c = heads(zc[2])
    o = global_block_attention(q, k, v, k_c, v_c)
    o_c = context_attention(rms_norm(heads(zc[0]), p['g_q_a']), k_c, v_c, None) if ctx_out else None
    return o, o_c

def mixer_window_gqa(z, zc, p, cos, sin, ctx_out):
    q = apply_rope(rms_norm(heads(z[0]), p['g_q_b']), cos, sin)
    k = apply_rope(rms_norm(heads(z[1]), p['g_k_b']), cos, sin)
    v = heads(z[2])
    k_c = rms_norm(heads(zc[1]), p['g_k_b'])
    v_c = heads(zc[2])
    o = window_block_attention(q, k, v, k_c, v_c, p['sink_b'])
    o_c = context_attention(rms_norm(heads(zc[0]), p['g_q_b']), k_c, v_c, p['sink_b']) if ctx_out else None
    return o, o_c

def mixer_gla(z, zc, p):
    def prep(parts):
        q, k, v, r, g = parts
        return (heads(q, GLA_DK) * GLA_DK ** -0.5, heads(k, GLA_DK), heads(v), heads(r), g)

    lat, ctx = prep(z), prep(zc)

    def log_decay(g, d):
        g_d = g[..., d * GLA_GATE_RANK:(d + 1) * GLA_GATE_RANK]
        pre = g_d @ p['w_gla_gate'][d] + p['b_gla_gate'][d]
        return heads(jax.nn.log_sigmoid(pre.astype(jnp.float32)) / GLA_GATE_TAU, GLA_DK)

    B_ = lat[0].shape[0]
    outs, outs_c = [], []
    for d in range(2):
        fl = _flip if d == 1 else _ident
        s0 = jnp.zeros((B_, GROUP_HEADS, GLA_DK, HEAD_DIM), jnp.float32)
        o_c, s_ctx = gla_scan(fl(ctx[0]), fl(ctx[1]), fl(ctx[2]), fl(log_decay(ctx[4], d)), s0)
        o_l, _ = gla_scan(fl(lat[0]), fl(lat[1]), fl(lat[2]), fl(log_decay(lat[4], d)), s_ctx)
        outs.append(fl(o_l))
        outs_c.append(fl(o_c))

    def finish(o, r):
        y = rms_norm(o, p['g_gla_out']) * jax.nn.silu(r.astype(jnp.float32))
        return y.reshape(y.shape[:2] + (GROUP_WIDTH,)).astype(r.dtype)

    return finish(outs[0] + outs[1], lat[3]), finish(outs_c[0] + outs_c[1], ctx[3])

def mixer_mlstm(z, zc, p):
    def prep(parts):
        q, k, v, o, i_pre, f_pre = parts
        return (heads(q), heads(k) * HEAD_DIM ** -0.5, heads(v), heads(o), i_pre, f_pre)

    lat, ctx = prep(z), prep(zc)

    def gates(parts, d):
        sl = slice(d * GROUP_HEADS, (d + 1) * GROUP_HEADS)
        ig = parts[4][..., sl].astype(jnp.float32) + p['b_mlstm_i'][d].astype(jnp.float32)
        lf = jax.nn.log_sigmoid(parts[5][..., sl].astype(jnp.float32) + p['b_mlstm_f'][d].astype(jnp.float32))
        return ig, lf

    B_ = lat[0].shape[0]
    outs, outs_c = [], []
    for d in range(2):
        fl = _flip if d == 1 else _ident
        st0 = (jnp.zeros((B_, GROUP_HEADS, HEAD_DIM, HEAD_DIM), jnp.float32),
               jnp.zeros((B_, GROUP_HEADS, HEAD_DIM), jnp.float32),
               jnp.zeros((B_, GROUP_HEADS), jnp.float32))
        ig_c, lf_c = gates(ctx, d)
        ig_l, lf_l = gates(lat, d)
        h_c, st_ctx = mlstm_scan(fl(ctx[0]), fl(ctx[1]), fl(ctx[2]), fl(ig_c), fl(lf_c), st0)
        h_l, _ = mlstm_scan(fl(lat[0]), fl(lat[1]), fl(lat[2]), fl(ig_l), fl(lf_l), st_ctx)
        outs.append(fl(h_l))
        outs_c.append(fl(h_c))

    def finish(h, o):
        y = jax.nn.sigmoid(o.astype(jnp.float32)) * rms_norm(h, p['g_mlstm_out'])
        return y.reshape(y.shape[:2] + (GROUP_WIDTH,)).astype(o.dtype)

    return finish(outs[0] + outs[1], lat[3]), finish(outs_c[0] + outs_c[1], ctx[3])

def squared_relu_mlp(h, w1, w2):
    return jnp.square(jax.nn.relu(h @ w1)) @ w2

def hybrid_layer(x, xc, mod, mod_c, p, cos, sin, ctx_out):
    sh1, sc1, ga1, sh2, sc2, ga2 = jnp.split(mod[:, None, :], N_MOD, axis=-1)
    sh1c, sc1c, ga1c, sh2c, sc2c, ga2c = jnp.split(mod_c, N_MOD, axis=-1)
    offs = np.cumsum(IN_SPLITS)[:-1].tolist()
    h = rms_norm(x, p['g_norm1']) * (1.0 + sc1) + sh1
    hc = rms_norm(xc, p['g_norm1']) * (1.0 + sc1c) + sh1c
    z = jnp.split(h @ p['w_in'], offs, axis=-1)
    zc = jnp.split(hc @ p['w_in'], offs, axis=-1)
    o_a, oc_a = mixer_global_gqa(z[0:3], zc[0:3], p, cos, sin, ctx_out)
    o_b, oc_b = mixer_window_gqa(z[3:6], zc[3:6], p, cos, sin, ctx_out)
    o_c, oc_c = mixer_gla(z[6:11], zc[6:11], p)
    o_d, oc_d = mixer_mlstm(z[11:17], zc[11:17], p)
    y = jnp.concatenate([o_a, o_b, o_c, o_d], axis=-1) @ p['w_out']
    x = x + ga1 * y
    x = x + ga2 * squared_relu_mlp(rms_norm(x, p['g_norm2']) * (1.0 + sc2) + sh2, p['w_mlp1'], p['w_mlp2'])
    if ctx_out:
        yc = jnp.concatenate([oc_a, oc_b, oc_c, oc_d], axis=-1) @ p['w_out']
        xc = xc + ga1c * yc
        xc = xc + ga2c * squared_relu_mlp(rms_norm(xc, p['g_norm2']) * (1.0 + sc2c) + sh2c, p['w_mlp1'], p['w_mlp2'])
    return x, xc

def setup_inputs(seed: int = 0) -> dict:
    key = jax.random.key(seed)
    ks = jax.random.split(key, 24)
    f32 = jnp.float32
    nrm = lambda k, shape, s: jax.random.normal(k, shape, f32) * s
    D = D_MODEL
    return {
        'x': nrm(ks[0], (BATCH, SEQ, D), 1.0),
        'c': nrm(ks[1], (BATCH, D), 1.0),
        'ctx': nrm(ks[2], (BATCH, CTX_LEN, D), 1.0),
        'c_ctx': nrm(ks[3], (D,), 1.0),
        'w_mod': nrm(ks[4], (DEPTH, D, N_MOD * D), 0.5 * D ** -0.5),
        'b_mod': nrm(ks[5], (DEPTH, N_MOD * D), 0.02),
        'g_norm1': 1.0 + nrm(ks[6], (DEPTH, D), 0.02),
        'g_norm2': 1.0 + nrm(ks[7], (DEPTH, D), 0.02),
        'w_in': nrm(ks[8], (DEPTH, D, IN_WIDTH), D ** -0.5),
        'g_q_a': 1.0 + nrm(ks[9], (DEPTH, HEAD_DIM), 0.02),
        'g_k_a': 1.0 + nrm(ks[10], (DEPTH, HEAD_DIM), 0.02),
        'g_q_b': 1.0 + nrm(ks[11], (DEPTH, HEAD_DIM), 0.02),
        'g_k_b': 1.0 + nrm(ks[12], (DEPTH, HEAD_DIM), 0.02),
        'sink_b': nrm(ks[13], (DEPTH, GROUP_HEADS), 0.5),
        'w_gla_gate': nrm(ks[14], (DEPTH, 2, GLA_GATE_RANK, GLA_KW), GLA_GATE_RANK ** -0.5),
        'b_gla_gate': nrm(ks[15], (DEPTH, 2, GLA_KW), 0.1),
        'g_gla_out': 1.0 + nrm(ks[16], (DEPTH, HEAD_DIM), 0.02),
        'b_mlstm_i': nrm(ks[17], (DEPTH, 2, GROUP_HEADS), 0.1),
        'b_mlstm_f': 3.0 + nrm(ks[18], (DEPTH, 2, GROUP_HEADS), 0.5),
        'g_mlstm_out': 1.0 + nrm(ks[19], (DEPTH, HEAD_DIM), 0.02),
        'w_out': nrm(ks[20], (DEPTH, D, D), D ** -0.5),
        'w_mlp1': nrm(ks[21], (DEPTH, D, D_FF), D ** -0.5),
        'w_mlp2': nrm(ks[22], (DEPTH, D_FF, D), D_FF ** -0.5),
    }

def reference(x, c, ctx, c_ctx, w_mod, b_mod, g_norm1, g_norm2, w_in, g_q_a, g_k_a, g_q_b, g_k_b, sink_b,
              w_gla_gate, b_gla_gate, g_gla_out, b_mlstm_i, b_mlstm_f, g_mlstm_out, w_out, w_mlp1, w_mlp2):
    cos, sin = axial_rope(x.shape[1])
    s_c = jax.nn.silu(c)
    s_cc = jax.nn.silu(c_ctx)
    xc = ctx
    for l in range(DEPTH):
        mod = s_c @ w_mod[l] + b_mod[l]
        mod_c = s_cc @ w_mod[l] + b_mod[l]
        p = {'g_norm1': g_norm1[l], 'g_norm2': g_norm2[l], 'w_in': w_in[l],
             'g_q_a': g_q_a[l], 'g_k_a': g_k_a[l], 'g_q_b': g_q_b[l], 'g_k_b': g_k_b[l], 'sink_b': sink_b[l],
             'w_gla_gate': w_gla_gate[l], 'b_gla_gate': b_gla_gate[l], 'g_gla_out': g_gla_out[l],
             'b_mlstm_i': b_mlstm_i[l], 'b_mlstm_f': b_mlstm_f[l], 'g_mlstm_out': g_mlstm_out[l],
             'w_out': w_out[l], 'w_mlp1': w_mlp1[l], 'w_mlp2': w_mlp2[l]}
        x, xc = hybrid_layer(x, xc, mod, mod_c, p, cos, sin, l < DEPTH - 1)
    return x


_drawn_inputs = setup_inputs


def setup_inputs(seed=0):
    import zlib

    import numpy as np

    out = dict(_drawn_inputs(seed))
    spreads = {}
    factors = {'g_norm1': 6.718,
     'g_norm2': 4.381,
     'g_q_a': 8.0,
     'g_k_a': 8.0,
     'g_q_b': 8.0,
     'g_k_b': 8.0,
     'sink_b': 8.0,
     'b_gla_gate': 8.0,
     'g_gla_out': 8.0,
     'b_mlstm_i': 64.0,
     'g_mlstm_out': 64.0}
    for name, (base, spread) in spreads.items():
        noise = np.random.default_rng([zlib.crc32(name.encode()), seed]).standard_normal(out[name].shape)
        drawn = base * np.exp(spread * noise) if base else spread * noise
        out[name] = __import__('jax').numpy.asarray(drawn.astype(out[name].dtype))
    for name, factor in factors.items():
        out[name] = (out[name] * factor).astype(out[name].dtype)
    return out
```

```python
import numpy as np
import concourse.bass as bass
from concourse import mybir

F32 = mybir.dt.float32
F32R = mybir.dt.float32r
BF16 = mybir.dt.bfloat16
U8 = mybir.dt.uint8
ALU = mybir.AluOpType
ACT = mybir.ActivationFunctionType
AX_X = mybir.AxisListType.X

P = 128
D_MODEL = 1024
SEQ = 512
CTX = 256
T = SEQ + CTX
DEPTH = 2
GRID_W = 64
HD = 64
KD = D_MODEL // P
TILES = T // P
LAT_TILES = SEQ // P
GLA_DK = 32
GATE_RANK = 16
GLA_TAU = 16.0
ROPE_THETA = 10000.0
EPS = 1e-6
BIG = 1e30
N_MOD = 6
WC = 256
MOD_SLOTS = N_MOD * D_MODEL // WC
IN_SLOTS = 12
OUT_SLOTS = D_MODEL // WC
QUARTERS = 4
QW1 = 4
QW2 = 4
LAYER_SLOTS = IN_SLOTS + OUT_SLOTS + QUARTERS * (QW1 + QW2)
FIRST_MODS = 8
FEATS = 13
ORDER = ((4, 5, 0, 1, 2, 3), (5, 4, 3, 2, 1, 0))
LEVELS = (64, 32, 16, 8, 4, 2, 1)

C_IDENT, C_BLOCK, C_SWAP = 0, P, 2 * P
C_COS = 3 * P
C_SIN = C_COS + SEQ
C_SEL = C_SIN + SEQ
C_HM = C_SEL + 8
C_KEEP = C_HM + 8
C_LEVEL = C_KEEP
C_LEFT = C_LEVEL + 8 * P
C_RIGHT = C_LEFT + P
C_ALL = C_RIGHT + P

V_C = 0
V_CC = KD
V_L = 2 * KD
LV_BMOD, LV_G1, LV_G2, LV_GB = 0, 48, 56, 64
LV_GQK = 65
LV_BG = 69
LV = 71
V_ALL = V_L + LV


class Tally:

    def __init__(self):
        self.n = 0
        self.term = None

    def add(self, k=1):
        self.n += k
        return self.at(0)

    def at(self, back):
        v = self.n + back
        return v if self.term is None else self.term + v

    def enter(self, i, per):
        self.start, self.per = self.n, per
        if i is not None:
            self.term = i * per

    def leave(self, times):
        assert self.n - self.start == self.per, (self.n, self.start, self.per)
        self.n = self.start + self.per * times
        self.term = None


def build(nc, x_in, ctx_in, w_big, w_mod, vecs, consts, gla_gate, rows, out):
    def place(name, off, shape, dt=F32):
        return nc.alloc_sbuf_tensor_at(name, [P] + list(shape), dt, offset=off)

    base = (nc.sbuf_base + 63) // 64 * 64
    cur = [base]

    def keep(name, shape, dt=F32):
        size = int(np.prod(shape)) * {F32: 4, F32R: 4, BF16: 2, U8: 1}[dt]
        off = cur[0]
        cur[0] += (size + 31) // 32 * 32
        return place(name, off, shape, dt)

    xT = keep("xT", [KD, T])
    raw = [keep(f"raw{r}", [KD, WC]) for r in range(2)]
    w_hi = [keep(f"w_hi{r}", [KD, WC], F32R) for r in range(2)]
    w_lo = [keep(f"w_lo{r}", [KD, WC], F32R) for r in range(2)]
    cst = keep("cst", [C_KEEP])
    ones = keep("ones", [P])
    lmask = keep("lmask", [8, P], U8)
    ident_b = keep("ident_b", [P], BF16)
    m_left = keep("m_left", [P], BF16)
    m_right = keep("m_right", [P], BF16)
    p_after = keep("p_after", [P], BF16)
    p_before = keep("p_before", [P], BF16)
    vcol = [keep("vcol0", [V_ALL]), keep("vcol1", [LV])]
    cs = keep("cs", [KD, 2])
    modt = [keep(f"modt{l}", [2 * 48]) for l in range(DEPTH)]
    bmod2 = keep("bmod2", [DEPTH * 48 * 2])
    gs = keep("gs", [KD, 2])
    gswap = keep("gswap", [P])
    wg = keep("wg", [2, P])
    rowc = keep("rowc", [4 + 2 * 256])
    nsink = keep("nsink", [4])
    eps = keep("eps", [1])
    mx = keep("mx", [2])
    nb = keep("nb", [2, 4])
    se = keep("se", [2, 4])
    es = keep("es", [2, 4])
    psum_e = keep("psum_e", [2, 4])
    rs = keep("rs", [2, 4])
    dex = keep("dex", [2, TILES])
    mp = keep("mp", [TILES])
    mend = keep("mend", [TILES])
    dec = keep("dec", [TILES])
    dcb = keep("dcb", [4, TILES])
    ms8 = keep("ms8", [TILES * 8])
    ident = cst[:, C_IDENT:C_IDENT + P]
    block = cst[:, C_BLOCK:C_BLOCK + P]
    swap = cst[:, C_SWAP:C_SWAP + P]
    cos = cst[:, C_COS:C_COS + SEQ]
    sin = cst[:, C_SIN:C_SIN + SEQ]
    sel = cst[:, C_SEL:C_SEL + 8]
    hm8 = cst[:, C_HM:C_HM + 8]

    TB = T * 4
    RH = cur[0]
    RS = RH + KD * TB
    RU = RS + KD * TB
    RV = RU + 16 * TB
    END = RV + 6 * 260 * 4 + 6 * 256 * 4 + 6 * 512 * 4
    assert END <= nc.sbuf_usable_end, (END, nc.sbuf_usable_end)

    h_hi = place("h_hi", RH, [KD, T], F32R)
    h_lo = place("h_lo", RS, [KD, T], F32R)
    y = place("y", RH, [TILES, 4 * 256])
    xin = [place(f"xin{i}", RH + i * 4096, [D_MODEL]) for i in range(2)]
    vin = place("vin", RH + 8192, [P])
    vin1 = place("vin1", RH + 8192 + 512, [P])
    cload = place("cload", RH + 16384, [C_ALL - C_KEEP])
    xout = [place(f"xout{i}", RH + i * 4096, [D_MODEL]) for i in range(2)]
    tmp = [place(f"tmp{i}", RV + i * TB, [T]) for i in range(8)]
    ft = [None] * FEATS
    v_ab = place("v_ab", RU + 6 * TB, [TILES, 256])
    for i in range(6):
        ft[i] = place(f"ft{i}", RU + i * TB, [T])
    for i in range(6, FEATS):
        ft[i] = place(f"ft{i}", RU + (i + 2) * TB, [T])
    SPARE = RU + 15 * TB
    vd1 = place("vd1", RV, [TILES, 4, 65])
    vc = place("vc", RV + 6 * 260 * 4, [TILES, 256])
    ro = place("ro", RV + 6 * 516 * 4, [TILES, 512])
    yT_hi = place("yT_hi", RU, [KD, T], F32R)
    yT_lo = place("yT_lo", RU + KD * TB, [KD, T], F32R)
    hid_hi = place("hid_hi", RU, [KD, T], F32R)
    hid_lo = place("hid_lo", RU + KD * TB, [KD, T], F32R)
    rab = place("rab", RS, [6, T])
    kb1 = [place(f"kb1_{m}", RS + (6 + m) * TB, [T]) for m in range(2)]
    rt = [place(f"rt{i}", RH + i * 2048, [SEQ]) for i in range(2)]
    prob = [place(f"prob{i}", RS + i * TB, [T]) for i in range(2)]
    probT = [place(f"probT{i}", RS + (2 + i) * TB, [T]) for i in range(2)]
    bb = [place(f"bb{d}", RS + d * TB, [T]) for d in range(2)]
    snap = place("snap", RS + 2 * TB, [2, TILES, 256])
    qe = [place(f"qe{d}", RS + (6 + d) * TB, [T]) for d in range(2)]
    ls = place("ls", RU, [3, T])
    pre = [place(f"pre{d}", RU + (3 + d) * TB, [T]) for d in range(2)]
    ex = place("ex", RU + 5 * TB, [2, T])
    kdec = [place(f"kdec{d}", RU + d * TB, [T]) for d in range(2)]
    ktc = [place(f"ktc{d}", RU + (2 + d) * TB, [T]) for d in range(2)]
    umask = place("umask", RU + 7 * TB, [2, 256])
    HT = 3 * P
    sacc = place("sacc", RU, [3, 4, P])
    eqk = [place(f"eqk{b}", RU + (2 + b) * TB, [2, HT]) for b in range(2)]
    qbd = [place(f"qbd{b}", RU + (4 + 2 * b) * TB, [3, 4, P]) for b in range(2)]
    kl = [place(f"kl{b}", SPARE + b * HT * 4, [HT]) for b in range(2)]
    qdb = place("qdb", RS, [4, T])
    ktd = place("ktd", RS + 4 * TB, [TILES, 256])
    fcum = place("fcum", RS + 6 * TB, [T])
    mrun = place("mrun", RS + 7 * TB, [T])
    arow = place("arow", RU, [T])
    r1 = place("r1", RU + TB, [T])
    r2 = place("r2", RU + 2 * TB, [T])
    o = RU + 3 * TB
    wb = [place(f"wb{b}", o + b * 4096, [2, 4, P]) for b in range(2)]
    o += 8192
    vw = place("vw", o, [2, 4, 65])
    o += 2080
    t1 = place("t1", o, [2, 4, 65])
    t2 = place("t2", o + 2080, [2, 4, 65])
    hh = place("hh", o + 4160, [2, 4, 64])
    cst_d = place("cst_d", o + 6208, [2, 2, 2, 65])
    col = place("col", o + 8288, [TILES, 2, 4, 4])
    dd = place("dd", o + 9056, [2, 4])
    rd = place("rd", o + 9088, [2, 4])
    assert o + 9120 <= RU + 10 * TB
    sqy = place("sqy", RS, [TILES, 512])
    sig = place("sig", RS + 4 * TB, [TILES, 512])

    ps = nc.alloc_psum_tensor("ps", [P, 4096], F32)

    def bank(b, a=0, n=512):
        return ps[:, b * 512 + a:b * 512 + a + n]

    def pair(g, a=0, n=1024):
        return bank(2 * (g % 2), a, n)

    S = {}

    def sem(name):
        if name not in S:
            S[name] = nc.alloc_semaphore(name)
        return S[name]

    def cols(j, n=1):
        return slice(j * P, (j + n) * P)

    def bc(ap, n):
        return ap.unsqueeze(2).to_broadcast([ap.shape[0], ap.shape[1], n])

    def mod_after(l, s):
        if l == 0 and s < IN_SLOTS + OUT_SLOTS:
            return FIRST_MODS + s
        return None

    Q_MODS = MOD_SLOTS // QUARTERS
    N_W = DEPTH * LAYER_SLOTS

    def lvec(l, i, n=1):
        b = (V_L if l == 0 else 0) + i
        return vcol[l][:, b:b + n]

    def att_units(l):
        js = range(TILES) if l == 0 else range(LAT_TILES)
        return [(m, j, h) for m in range(2) for j in js for h in range(4)]

    def key_span(m, j):
        if j >= LAT_TILES:
            return 512, [4, 5], []
        if m == 0:
            return 0, [0, 1, 2, 3, 4, 5], []
        k0, k1 = max(0, j - 1), min(LAT_TILES - 1, j + 1)
        n = k1 - k0 + 1
        lo = 512 - n * P
        masks = []
        if j > 0:
            masks.append((m_left, lo))
        if j < LAT_TILES - 1:
            masks.append((m_right, 512 - P))
        return lo, list(range(k0, k1 + 1)) + [4, 5], masks

    def halves(l):
        return [(0, 3), (3, 3 if l == 0 else 1)]

    blk = nc.Block()
    with blk:
        @blk.sync
        def _(sp):
            sp.dma_start(cst[:], consts[:, 0:C_KEEP]).then_inc(sem("c_landed"), 16)
            sp.dma_start(vin[0:V_ALL, :], vecs[0:V_ALL, :]).then_inc(sem("c_landed"), 16)
            sp.dma_start(vin1[0:LV, :], vecs[V_ALL:V_ALL + LV, :]).then_inc(sem("c_landed"), 16)
            sp.dma_start(cload[:], consts[:, C_KEEP:C_ALL]).then_inc(sem("c_landed"), 16)
            mods = Tally()
            wts = Tally()

            def load_mod(j, idx):
                r = j % 2 if isinstance(j, int) and j < FIRST_MODS else 1
                if isinstance(j, int) and j < FIRST_MODS:
                    if j >= 2:
                        sp.wait_ge(sem("mod_used"), j - 1)
                else:
                    sp.wait_ge(sem("mod_used"), mods.at(0))
                sp.dma_start(raw[r][:], idx).then_inc(sem(f"mod_landed{r}"), 16)
                mods.add()

            def load_w(idx, first=False):
                if first:
                    sp.wait_ge(sem("mod_used"), FIRST_MODS - 1)
                else:
                    sp.wait_ge(sem("lo_ready"), wts.at(0))
                sp.dma_start(raw[0][:], idx).then_inc(sem("w_landed"), 16)
                wts.add()

            def wslot(n):
                return w_big[n].rearrange("p (k m) -> p k m", k=KD)

            def mslot(n):
                return w_mod[n].rearrange("p (k m) -> p k m", k=KD)

            for j in range(FIRST_MODS):
                load_mod(j, mslot(j))
                if j < TILES:
                    if j >= 2:
                        sp.wait_ge(sem("x_in"), j - 1)
                    src = x_in[cols(j), :] if j < LAT_TILES else ctx_in[cols(j - LAT_TILES), :]
                    sp.dma_start(xin[j % 2][:], src).then_inc(sem(f"x_landed{j % 2}"), 16)
            load_w(wslot(0), first=True)
            load_w(wslot(1))
            for l in range(DEPTH):
                sp.dma_start(rowc[:], rows[l:l + 1, :].to_broadcast([P, rows.shape[1]])).then_inc(sem("lay_landed"), 16)
                sp.dma_start(wg[:], gla_gate[l]).then_inc(sem("lay_landed"), 16)
                w0 = l * LAYER_SLOTS
                for s in range(IN_SLOTS + OUT_SLOTS):
                    load_w(wslot(w0 + s + 2))
                    if mod_after(l, s) is not None:
                        load_mod(mod_after(l, s), mslot(mod_after(l, s)))
                q0 = w0 + IN_SLOTS + OUT_SLOTS
                n_loop = QUARTERS if l < DEPTH - 1 else QUARTERS - 1
                mods_per = Q_MODS if l == 0 else 0
                with sp.Fori(0, n_loop) as i:
                    wts.enter(i, 8)
                    mods.enter(i, mods_per)
                    for s in range(QW1 + QW2):
                        load_w(w_big[bass.ds(i * 8 + (q0 + s + 2), 1)].rearrange("o p (k m) -> p (o k) m", k=KD))
                        if s < mods_per:
                            load_mod(None, w_mod[bass.ds(i * Q_MODS + (MOD_SLOTS + s), 1)]
                                     .rearrange("o p (k m) -> p (o k) m", k=KD))
                wts.leave(n_loop)
                mods.leave(n_loop)
                if l == DEPTH - 1:
                    for s in range(QW1 + QW2 - 2):
                        load_w(wslot(q0 + 8 * n_loop + s + 2))
                if l == 0:
                    sp.wait_ge(sem("x_done"), 8 * (1 + QUARTERS))
            for j in range(LAT_TILES):
                sp.wait_ge(sem("out_ready"), j + 1)
                sp.dma_start(out[cols(j), :], xout[j % 2][:]).then_inc(sem(f"out_stored{j % 2}"), 16)
            for r in range(2):
                sp.wait_ge(sem(f"out_stored{r}"), 16 * (LAT_TILES // 2))

        @blk.gpsimd
        def _(gp):
            def low(n, r):
                gp.wait_ge(sem("hi_ready"), n)
                nc.gpsimd.tensor_tensor(w_lo[r][:], raw[0][:], w_hi[r][:].bitcast(F32),
                                        ALU.subtract).then_inc(sem("lo_ready"), 1)
            with gp.Fori(0, N_W // 2) as i:
                low(i * 2 + 1, 0)
                low(i * 2 + 2, 1)

        @blk.scalar
        def _(act):
            big = Tally()
            w_n = Tally()
            c = {}

            def T_(name):
                return c.setdefault(name, Tally())

            w_groups = []
            for l in range(DEPTH):
                for s in range(LAYER_SLOTS):
                    w_groups.append((w_groups[-1] if w_groups else 0) + (1 if s == 6 else 2))

            def split_hi(w, i=None, per=0):
                if w >= N_W:
                    return
                if i is None:
                    act.wait_ge(sem("w_landed"), 16 * (w + 1))
                    if w >= 2:
                        act.wait_ge(sem("big_done"), w_groups[w - 2])
                else:
                    act.wait_ge(sem("w_landed"), i * 128 + 16 * (w + 1))
                    act.wait_ge(sem("big_done"), i * 16 + w_groups[w - 2])
                nc.scalar.activation(w_hi[w % 2][:], raw[0][:], ACT.Copy).then_inc(sem("hi_ready"), 1)

            stage_n = [0]

            def stage_end():
                act.drain().then_inc(sem("stage_done"), 1)
                stage_n[0] += 3
                act.wait_ge(sem("stage_done"), stage_n[0])

            own = Tally()

            def step(ins):
                ins.then_inc(sem("act_step"), 1)
                act.wait_ge(sem("act_step"), own.add())

            act.wait_ge(sem("v_cols"), 1)
            nc.scalar.activation(cs[:, :, 0], vcol[0][:, V_C:V_C + KD], ACT.Exp, scale=-1.0)
            nc.scalar.activation(cs[:, :, 1], vcol[0][:, V_CC:V_CC + KD], ACT.Exp,
                                 scale=-1.0).then_inc(sem("c_exp"), 1)
            for j in range(TILES):
                act.wait_ge(sem("x_trans"), j + 1)
                nc.scalar.activation(xT[:, :, cols(j)], pair(j).rearrange("p (k t) -> p k t", k=KD),
                                     ACT.Copy).then_inc(sem("x_in"), 1)

            def norm(l, which, n_t, x_total):
                parts = [(0, 0, SEQ)] + ([(1, SEQ, T)] if n_t == T else [])
                sqn, accn, hn = T_("sq"), T_("acc"), T_("h")
                t_n, hh_n = T_("t"), T_("h_hi")
                for k in range(KD):
                    act.wait_ge(sem("x_done"), x_total - KD + k + 1) if x_total else \
                        act.wait_ge(sem("x_in"), TILES)
                    if k >= 2:
                        act.wait_ge(sem("acc_added"), accn.n + max(1, k - 2))
                    nc.scalar.activation(tmp[k % 2][:, 0:n_t], xT[:, k, 0:n_t],
                                         ACT.Square).then_inc(sem("sq_ready"), 1)
                accn.add(KD - 1)
                act.wait_ge(sem("ms_ready"), T_("ms").add())
                step(nc.scalar.activation(tmp[3][:, 0:n_t], bank(4, 0, n_t), ACT.Ln, bias=eps[:, 0:1],
                                          scale=1.0 / D_MODEL))
                nc.scalar.activation(tmp[3][:, 0:n_t], tmp[3][:, 0:n_t], ACT.Exp,
                                     scale=-0.5).then_inc(sem("rstd_ready"), 1)
                sh = modt[l][:].rearrange("p (m c) -> p m c", c=2)
                m0 = 0 if which == 1 else 24
                for k in range(KD):
                    act.wait_ge(sem("t_ready"), t_n.add())
                    if k >= 2:
                        act.wait_ge(sem("h_ready"), hn.n + k - 1)
                    for c_i, a, b in parts:
                        ins = nc.scalar.activation(tmp[4 + k % 2][:, a:b], tmp[k % 2][:, a:b], ACT.Identity,
                                                   bias=sh[:, m0 + k, c_i:c_i + 1], scale=gs[:, k, c_i:c_i + 1])
                    ins.then_inc(sem("h_full"), 1)
                    act.wait_ge(sem("h_full"), hh_n.add())
                    nc.scalar.activation(h_hi[:, k, 0:n_t], tmp[4 + k % 2][:, 0:n_t],
                                         ACT.Copy).then_inc(sem("h_hi_ready"), 1)
                hn.add(KD)

            def in_proj(l):
                scale = {6: GLA_DK ** -0.5, 10: HD ** -0.5, 11: HD ** -0.5}
                for s in range(IN_SLOTS):
                    w = l * LAYER_SLOTS + s
                    for m in range(2):
                        g = 2 * s + m
                        if g < FEATS:
                            act.wait_ge(sem("big_done"), big.add())
                            if g == 12:
                                ins = nc.scalar.activation(ft[g][:], pair(g, 0, T), ACT.Identity,
                                                           bias=lvec(l, LV_GB), scale=1.0)
                            else:
                                ins = nc.scalar.activation(ft[g][:], pair(g, 0, T), ACT.Copy,
                                                           scale=scale.get(g, 1.0))
                            ins.then_inc(sem("ft_ready"), 1)
                        elif g > FEATS:
                            big.add()
                    split_hi(w + 2)

            def prep_ab():
                for i in range(6):
                    nc.scalar.activation(rab[:, i, :], ft[i][:], ACT.Square).then_inc(sem("sqab_ready"), 1)
                for i in range(6):
                    act.wait_ge(sem("msab_ready"), T_("msab").add())
                    nc.scalar.activation(rab[:, i, :], pair(i, 0, T), ACT.Ln, bias=eps[:, 0:1],
                                         scale=1.0 / HD).then_inc(sem("lnab_done"), 1)
                act.wait_ge(sem("lnab_done"), T_("lnab").add(6))
                nc.scalar.activation(rab[:], rab[:], ACT.Exp, scale=-0.5).then_inc(sem("rab_ready"), 1)

            def attention(l):
                units = att_units(l)
                n = len(units)
                e0, t0, p0 = T_("nb").n, T_("tr").n, T_("pv").n

                def evac(u):
                    _, j, _ = units[u]
                    m = units[u][0]
                    _, keys, _ = key_span(m, j)
                    act.wait_ge(sem("tr_done"), t0 + u + 1)
                    if u >= 2:
                        act.wait_ge(sem("pv_done"), p0 + u - 1)
                    nc.scalar.activation(probT[u % 2][:, 0:len(keys) * P], bank(4, 0, len(keys) * P),
                                         ACT.Copy).then_inc(sem("pt_ready"), 1)

                for u, (m, j, h) in enumerate(units):
                    lo, keys, _ = key_span(m, j)
                    jj = u // 4
                    act.wait_ge(sem("nb_ready"), e0 + u + 1)
                    if u >= 2:
                        act.wait_ge(sem("tr_done"), t0 + u - 1)
                    nc.scalar.activation(prob[u % 2][:, 0:T - lo], pair(u, lo, T - lo), ACT.Exp,
                                         bias=nb[:, jj % 2, h:h + 1], scale=HD ** -0.5,
                                         accum_out=psum_e[:, jj % 2, h:h + 1]).then_inc(sem("exp_done"), 1)
                    if m == 1 and h == 3:
                        nc.scalar.activation(es[:, jj % 2, :], se[:, jj % 2, :],
                                             ACT.Exp).then_inc(sem("es_ready"), 1)
                    if u >= 1:
                        evac(u - 1)
                evac(n - 1)
                T_("nb").add(n), T_("tr").add(n), T_("pv").add(n)

            def gla(l):
                for d in range(2):
                    act.wait_ge(sem("pre_done"), T_("pre").add())
                    nc.scalar.activation(pre[d][:], pair(d, 0, T), ACT.Identity, bias=lvec(l, LV_BG + d),
                                         scale=1.0).then_inc(sem("pre_ready"), 1)
                act.wait_ge(sem("abs_ready"), T_("abs").add(3))
                step(nc.scalar.activation(ls[:], ls[:], ACT.Exp))
                nc.scalar.activation(ls[:], ls[:], ACT.Ln, bias=1.0).then_inc(sem("softplus_ready"), 1)
                act.wait_ge(sem("ex_raw"), T_("exr").add())
                nc.scalar.activation(ex[:], ex[:], ACT.Exp, scale=1.0 / GLA_TAU).then_inc(sem("ex_ready"), 1)
                nc.scalar.activation(dex[:], dex[:], ACT.Exp, scale=1.0 / GLA_TAU).then_inc(sem("ex_ready"), 1)
                for d in range(2):
                    act.wait_ge(sem("kt_done"), T_("kt").add())
                    nc.scalar.activation(ktc[d][:], pair(d, 0, T), ACT.Copy).then_inc(sem("ktc_ready"), 1)
                act.wait_ge(sem("kdec_ready"), T_("kdec").add(2))
                for d in range(2):
                    nc.scalar.activation(ex[:, d, :], bb[d][:], ACT.Exp,
                                         scale=1.0 / GLA_TAU).then_inc(sem("ex_ready"), 1)
                for hf, (j0, nt) in enumerate(halves(l)):
                    for li in range(len(LEVELS)):
                        b = (hf * 8 + li + 1) % 2
                        act.wait_ge(sem("e_raw"), T_("er").add())
                        nc.scalar.activation(eqk[b][:, :, 0:nt * P], eqk[b][:, :, 0:nt * P], ACT.Exp,
                                             scale=1.0 / GLA_TAU).then_inc(sem("e_ready"), 1)
                    for t in range(nt):
                        act.wait_ge(sem("oc_done"), T_("oc").add())
                        nc.scalar.activation(y[:, j0 + t, 512:768], bank(4 + (j0 + t) % 2, 0, 256),
                                             ACT.Copy).then_inc(sem("yc_ready"), 1)

            def mlstm(l):
                act.wait_ge(sem("qdb_zero"), T_("qz").add())
                for p_ in range(2):
                    for hf in range(2):
                        rr = slice(64 * hf, 64 * hf + 64)
                        nc.scalar.activation(qdb[rr, 2 * p_ + hf, :], ft[8 + p_][rr, :],
                                             ACT.Copy).then_inc(sem("qdb_ready"), 1)
                for a, n in ((0, 4), (4, 2)):
                    act.wait_ge(sem("kd_done"), T_("kd").add())
                    nc.scalar.activation(ktd[:, a:a + n, :], pair(a // 4, 0, n * 256).rearrange(
                        "p (j c) -> p j c", j=n), ACT.Copy).then_inc(sem("ktd_ready"), 1)
                act.wait_ge(sem("r_raw"), T_("rr").add())
                nc.scalar.activation(r1[64:128, :], r1[64:128, :], ACT.Exp).then_inc(sem("r_ready"), 1)
                nc.scalar.activation(r2[:], r2[:], ACT.Exp).then_inc(sem("r_ready"), 1)
                nc.scalar.activation(dec[:], dec[:], ACT.Exp).then_inc(sem("r_ready"), 1)
                act.wait_ge(sem("col_ready"), T_("col").add())
                k = 0
                for s in range(TILES):
                    for d in range(2):
                        j = ORDER[d][s]
                        if l == DEPTH - 1 and j >= LAT_TILES:
                            continue
                        act.wait_ge(sem("mb_done"), T_("mb").add())
                        if k >= 4:
                            act.wait_ge(sem("num_done"), T_("num").n + k - 3)
                        for h in range(4):
                            ins = nc.scalar.activation(wb[s % 2][:, d, h, :], bank(d, h * P, P), ACT.Exp,
                                                       bias=col[:, j, 0, d, h:h + 1], scale=-1.0)
                        ins.then_inc(sem("w_ready"), 1)
                        k += 1
                T_("num").add(k)

            def finish(l):
                nj = TILES if l == 0 else LAT_TILES
                nc.scalar.activation(sqy[:, 0:nj, :], y[:, 0:nj, 512:1024], ACT.Square).then_inc(sem("sqy_ready"), 1)
                nc.scalar.activation(sig[:, 0:nj, :], ro[:, 0:nj, :], ACT.Exp, scale=-1.0).then_inc(sem("sig_raw"), 1)
                act.wait_ge(sem("ms8_ready"), T_("ms8").add())
                step(nc.scalar.activation(ms8[:, 0:nj * 8], ms8[:, 0:nj * 8], ACT.Ln, bias=eps[:, 0:1],
                                          scale=1.0 / HD))
                nc.scalar.activation(ms8[:, 0:nj * 8], ms8[:, 0:nj * 8], ACT.Exp,
                                     scale=-0.5).then_inc(sem("rstd8_ready"), 1)
                for j in range(nj):
                    act.wait_ge(sem("yt_done"), T_("yt").add())
                    nc.scalar.activation(yT_hi[:, :, cols(j)], pair(j).rearrange("p (k t) -> p k t", k=KD),
                                         ACT.Copy).then_inc(sem("yt_hi"), 1)

            def mlp_quarter(l, n_t, w0, i, last):
                def hid_high(m):
                    act.wait_ge(sem("sq2_ready"), T_("sq2").add())
                    nc.scalar.activation(hid_hi[:, m, 0:n_t], tmp[2 + m % 2][:, 0:n_t],
                                         ACT.Copy).then_inc(sem("hid_hi_ready"), 1)
                for s in range(QW1 + QW2):
                    for m in range(2):
                        g = 2 * s + m
                        big.add()
                        if s < QW1:
                            act.wait_ge(sem("big_done"), big.at(0))
                            if g >= 2:
                                act.wait_ge(sem("sq2_ready"), T_("sq2").at(0))
                            nc.scalar.activation(tmp[6 + g % 2][:, 0:n_t], pair(g, 0, n_t),
                                                 ACT.Relu).then_inc(sem("relu_done"), 1)
                            if g >= 1:
                                hid_high(g - 1)
                    if s == QW1 - 1:
                        hid_high(2 * QW1 - 1)
                    if not (last and s >= QW1 + QW2 - 2):
                        split_hi(w0 + s + 2, i)

            split_hi(0)
            split_hi(1)
            x_total = 0
            for l in range(DEPTH):
                n_t = T if l == 0 else SEQ
                w0 = l * LAYER_SLOTS
                norm(l, 1, T, x_total)
                in_proj(l)
                stage_end()
                prep_ab()
                attention(l)
                stage_end()
                gla(l)
                stage_end()
                mlstm(l)
                stage_end()
                finish(l)
                for s in range(OUT_SLOTS):
                    big.add(2)
                    split_hi(w0 + IN_SLOTS + s + 2)
                x_total += KD
                norm(l, 2, n_t, x_total)
                n_loop = QUARTERS if l < DEPTH - 1 else QUARTERS - 1
                q0 = w0 + IN_SLOTS + OUT_SLOTS
                with act.Fori(0, n_loop) as i:
                    big.enter(i, 16)
                    T_("sq2").enter(i, 8)
                    mlp_quarter(l, n_t, q0, i, False)
                big.leave(n_loop)
                T_("sq2").leave(n_loop)
                if l == DEPTH - 1:
                    mlp_quarter(l, n_t, q0 + 8 * n_loop, None, True)
                x_total += KD * QUARTERS

        @blk.vector
        def _(dve):
            c = {}

            def T_(name):
                return c.setdefault(name, Tally())

            big = Tally()
            own = Tally()

            def step(ins):
                ins.then_inc(sem("dve_step"), 1)
                dve.wait_ge(sem("dve_step"), own.add())

            stage_n = [0]

            def stage_end():
                dve.drain().then_inc(sem("stage_done"), 1)
                stage_n[0] += 3
                dve.wait_ge(sem("stage_done"), stage_n[0])

            v = nc.vector

            v.memset(ones[:], 1.0)
            v.memset(eps[:], EPS).then_inc(sem("ones_ready"), 1)
            dve.wait_ge(sem("c_landed"), 64)
            v.tensor_copy(lmask[:], cload[:, 0:8 * P].rearrange("p (a b) -> p a b", a=8))
            v.tensor_copy(ident_b[:], ident)
            v.tensor_scalar(m_left[:], cload[:, C_LEFT - C_KEEP:C_LEFT - C_KEEP + P], -BIG, None, ALU.mult)
            v.tensor_scalar(m_right[:], cload[:, C_RIGHT - C_KEEP:C_RIGHT - C_KEEP + P], -BIG, None, ALU.mult)
            v.tensor_scalar(p_after[:], cload[:, C_LEFT - C_KEEP:C_LEFT - C_KEEP + P], BIG, None, ALU.mult)
            v.tensor_scalar(p_before[:], cload[:, C_RIGHT - C_KEEP:C_RIGHT - C_KEEP + P], BIG, None,
                            ALU.mult).then_inc(sem("masks_ready"), 1)
            dve.wait_ge(sem("v_trans"), 1)
            v.tensor_copy(vcol[1][:], bank(7, P, LV))
            v.tensor_copy(vcol[0][:], bank(7, 0, V_ALL)).then_inc(sem("v_cols"), 1)
            dve.wait_ge(sem("v_cols"), 1)
            for l in range(DEPTH):
                last = v.tensor_copy(bmod2[:, l * 96:(l + 1) * 96].rearrange("p (m c) -> p m c", c=2),
                                     bc(lvec(l, LV_BMOD, 48), 2))
            step(last)
            dve.wait_ge(sem("c_exp"), 1)
            step(v.tensor_scalar(cs[:], cs[:], 1.0, None, ALU.add))
            step(v.reciprocal(cs[:], cs[:]))
            v.tensor_tensor(cs[:, :, 0], cs[:, :, 0], vcol[0][:, V_C:V_C + KD], ALU.mult)
            v.tensor_tensor(cs[:, :, 1], cs[:, :, 1], vcol[0][:, V_CC:V_CC + KD], ALU.mult).then_inc(sem("cs_ready"), 1)

            mod_n = Tally()

            def mod_out(l, s, i=None):
                dve.wait_ge(sem("mod_used"), mod_n.add())
                if i is None:
                    a, b = modt[l][:, 4 * s:4 * s + 4], bmod2[:, l * 96 + 4 * s:l * 96 + 4 * s + 4]
                else:
                    a = modt[l][:, bass.ds(i * (4 * Q_MODS) + 4 * s, 4)]
                    b = bmod2[:, bass.ds(i * (4 * Q_MODS) + (l * 96 + 4 * s), 4)]
                v.tensor_tensor(a, bank(6, 0, 4), b, ALU.add).then_inc(sem("mod_out"), 1)

            for s in range(FIRST_MODS):
                mod_out(0, s)

            def norm(l, which, n_t):
                sqn = T_("sq")
                mt = modt[l][:].rearrange("p (m c) -> p m c", c=2)
                m0 = 8 if which == 1 else 32
                dve.wait_ge(sem("mod_out"), mod_n.at(0))
                step(v.scalar_tensor_tensor(gs[:], mt[:, m0:m0 + KD, :], 1.0,
                                            bc(lvec(l, LV_G1 if which == 1 else LV_G2, KD), 2), ALU.add, ALU.mult))
                for k in range(1, KD):
                    dve.wait_ge(sem("sq_ready"), sqn.n + k + 1)
                    if k >= 2:
                        dve.wait_ge(sem("acc_added"), T_("acc").n + k - 1)
                    v.tensor_tensor(tmp[2][:, 0:n_t], tmp[0][:, 0:n_t] if k == 1 else tmp[2][:, 0:n_t],
                                    tmp[k % 2][:, 0:n_t], ALU.add).then_inc(sem("acc_added"), 1)
                sqn.add(KD)
                T_("acc").add(KD - 1)
                dve.wait_ge(sem("rstd_ready"), T_("rstd").add())

                def low(k):
                    dve.wait_ge(sem("h_hi_ready"), T_("hhi").add())
                    v.tensor_tensor(h_lo[:, k, 0:n_t], tmp[4 + k % 2][:, 0:n_t], h_hi[:, k, 0:n_t].bitcast(F32),
                                    ALU.subtract).then_inc(sem("h_ready"), 1)
                for k in range(KD):
                    if k >= 2:
                        dve.wait_ge(sem("h_full"), T_("hf").n + k - 1)
                    v.tensor_tensor(tmp[k % 2][:, 0:n_t], xT[:, k, 0:n_t], tmp[3][:, 0:n_t],
                                    ALU.mult).then_inc(sem("t_ready"), 1)
                    if k >= 1:
                        low(k - 1)
                low(KD - 1)
                T_("hf").add(KD)

            def in_proj(l):
                for s in range(IN_SLOTS):
                    for m in range(2):
                        g = 2 * s + m
                        if g == FEATS:
                            continue
                        big.add()
                        if g < FEATS:
                            continue
                        dve.wait_ge(sem("big_done"), big.at(0))
                        j0, n = (0, 4) if m == 0 else (4, 2)
                        src = pair(g, 0, n * 256).rearrange("p (j c) -> p j c", j=n)
                        if s == 7:
                            dst = v_ab[:, j0:j0 + n, :]
                        elif s == 8:
                            dst = vc[:, j0:j0 + n, :]
                        elif s == 9:
                            dst = vd1[:, j0:j0 + n, :, 0:64]
                            src = pair(g, 0, n * 256).rearrange("p (j h c) -> p j h c", j=n, h=4)
                        else:
                            dst = ro[:, j0:j0 + n, (s - 10) * 256:(s - 9) * 256]
                        v.tensor_copy(dst, src).then_inc(sem("vt_ready"), 1)
                    if mod_after(l, s) is not None:
                        mod_out(0, mod_after(l, s))
                v.memset(vd1[:, :, :, 64:65], 1.0)

            def prep_ab(l):
                dve.wait_ge(sem("lay_landed"), 32 * (l + 1))
                v.tensor_scalar(nsink[:], rowc[:, 0:4], -1.0, None, ALU.mult)
                for i in range(6):
                    gi = LV_GQK + (0, 0, 1, 2, 2, 3)[i]
                    if i >= 1:
                        dve.wait_ge(sem("rot_done"), T_("rot").n + i)
                    v.tensor_scalar(gswap[:], swap, lvec(l, gi), None, ALU.mult).then_inc(sem("gswap_ready"), 1)
                T_("rot").add(6)
                dve.wait_ge(sem("rab_ready"), T_("rab").add())
                dve.wait_ge(sem("rot_done"), T_("rot").n)
                lat, ctx_ = slice(0, SEQ), slice(SEQ, T)
                for i in range(6):
                    g = lvec(l, LV_GQK + (0, 0, 1, 2, 2, 3)[i])
                    rot = bank(4 + i % 4) if i < 4 else bank(i - 4)
                    step(v.scalar_tensor_tensor(rt[0][:], ft[i][:, lat], g, cos, ALU.mult, ALU.mult))
                    step(v.tensor_tensor(rt[1][:], rot, sin, ALU.mult))
                    step(v.tensor_tensor(rt[0][:], rt[0][:], rt[1][:], ALU.add))
                    if i in (2, 5):
                        k1 = kb1[i // 3]
                        a, b = slice(0, 64), slice(64, 128)
                        v.memset(k1[a, :], 0.0)
                        v.tensor_tensor(k1[b, lat], rt[0][b, :], rab[b, i, lat], ALU.mult)
                        step(v.scalar_tensor_tensor(k1[b, ctx_], ft[i][b, ctx_], g[b, :], rab[b, i, ctx_],
                                                    ALU.mult, ALU.mult))
                        v.tensor_tensor(ft[i][a, lat], rt[0][a, :], rab[a, i, lat], ALU.mult)
                        v.scalar_tensor_tensor(ft[i][a, ctx_], ft[i][a, ctx_], g[a, :], rab[a, i, ctx_],
                                               ALU.mult, ALU.mult)
                        v.memset(ft[i][b, :], 0.0).then_inc(sem("qk_ready"), 1)
                    else:
                        v.tensor_tensor(ft[i][:, lat], rt[0][:], rab[:, i, lat], ALU.mult)
                        v.scalar_tensor_tensor(ft[i][:, ctx_], ft[i][:, ctx_], g, rab[:, i, ctx_],
                                               ALU.mult, ALU.mult).then_inc(sem("qk_ready"), 1)
                    dve.wait_ge(sem("qk_ready"), T_("qk").add())

            def attention(l):
                units = att_units(l)
                s0, p0 = T_("sc").n, T_("pv").n
                e0 = T_("exp").n

                def tile_out(jj):
                    m, j, _ = units[4 * jj]
                    jp = jj % 2
                    dve.wait_ge(sem("pv_done"), p0 + 4 * jj + 4)
                    dve.wait_ge(sem("exp_done"), e0 + 4 * jj + 4)
                    if m == 1:
                        dve.wait_ge(sem("es_ready"), T_("es").add())
                        step(v.tensor_tensor(psum_e[:, jp, :], psum_e[:, jp, :], es[:, jp, :], ALU.add))
                    step(v.reciprocal(rs[:, jp, :], psum_e[:, jp, :]))
                    v.tensor_tensor(y[:, j, m * 256:m * 256 + 256].rearrange("p (h c) -> p h c", h=4),
                                    bank(6 + jp, 0, 256).rearrange("p (h c) -> p h c", h=4),
                                    bc(rs[:, jp, :], 64), ALU.mult).then_inc(sem("yab_ready"), 1)

                for u, (m, j, h) in enumerate(units):
                    lo, keys, _ = key_span(m, j)
                    jp = u // 4 % 2
                    dve.wait_ge(sem("sc_done"), s0 + u + 1)
                    step(v.tensor_reduce(mx[:, u % 2:u % 2 + 1], pair(u, lo, T - lo), AX_X, ALU.max))
                    if m == 0:
                        v.tensor_scalar(nb[:, jp, h:h + 1], mx[:, u % 2:u % 2 + 1], -HD ** -0.5, None,
                                        ALU.mult).then_inc(sem("nb_ready"), 1)
                    else:
                        step(v.tensor_scalar(nb[:, jp, h:h + 1], mx[:, u % 2:u % 2 + 1], -HD ** -0.5,
                                             nsink[:, h:h + 1], ALU.mult, ALU.min))
                        v.tensor_tensor(se[:, jp, h:h + 1], nb[:, jp, h:h + 1], rowc[:, h:h + 1],
                                        ALU.add).then_inc(sem("nb_ready"), 1)
                    if h == 2 and u >= 4:
                        tile_out(u // 4 - 1)
                tile_out(len(units) // 4 - 1)
                T_("sc").add(len(units)), T_("pv").add(len(units)), T_("exp").add(len(units))

            def gla(l):
                qc, kc, gates = ft[6], ft[7], ft[12]
                for d in range(2):
                    dve.wait_ge(sem("pre_ready"), T_("pre").add())
                    v.scalar_tensor_tensor(ls[:, d, :], pre[d][:], -1.0, pre[d][:], ALU.mult,
                                           ALU.min).then_inc(sem("abs_ready"), 1)
                v.scalar_tensor_tensor(ls[:, 2, :], gates[:], -1.0, gates[:], ALU.mult,
                                       ALU.min).then_inc(sem("abs_ready"), 1)
                v.memset(snap[:, 0, ORDER[0][0], :], 0.0)
                v.memset(snap[:, 1, ORDER[1][0], :], 0.0)
                dve.wait_ge(sem("softplus_ready"), T_("sp").add())
                for d in range(2):
                    step(v.scalar_tensor_tensor(pre[d][:], pre[d][:], 0.0, ls[:, d, :], ALU.min, ALU.subtract))
                step(v.scalar_tensor_tensor(gates[64:128, :], gates[64:128, :], 0.0, ls[64:128, 2, :],
                                            ALU.min, ALU.subtract))
                one = ones[:, 0:1].to_broadcast([P, P])
                for j in range(TILES):
                    v.tensor_tensor_scan(bb[0][:, cols(j)], one, pre[0][:, cols(j)], 0.0, ALU.mult, ALU.add)
                    last = v.tensor_tensor_scan(bb[1][:, cols(j)][:, ::-1], one, pre[1][:, cols(j)][:, ::-1], 0.0,
                                                ALU.mult, ALU.add)
                step(last)
                ends = [bb[0][:].rearrange("p (j t) -> p j t", t=P)[:, :, P - 1],
                        bb[1][:].rearrange("p (j t) -> p j t", t=P)[:, :, 0]]
                for d in range(2):
                    v.tensor_copy(dex[:, d, :], ends[d])
                    last = v.tensor_tensor(ex[:, d, :].rearrange("p (j t) -> p j t", t=P), bc(ends[d], P),
                                           bb[d][:].rearrange("p (j t) -> p j t", t=P), ALU.subtract)
                last.then_inc(sem("ex_raw"), 1)
                dve.wait_ge(sem("ex_ready"), T_("ex").add(2))
                for d in range(2):
                    v.tensor_tensor(kdec[d][:], kc[:], ex[:, d, :], ALU.mult).then_inc(sem("kdec_ready"), 1)
                for s in range(TILES - 1):
                    dve.wait_ge(sem("u_done"), T_("u").add())
                    step(v.tensor_tensor(umask[:].rearrange("p d (h c) -> p (d h) c", c=64),
                                         bank(4 + s % 2).rearrange("p (h c) -> p h c", c=64), bc(hm8, 64), ALU.mult))
                    for d in range(2):
                        a, b = ORDER[d][s], ORDER[d][s + 1]
                        last = v.scalar_tensor_tensor(snap[:, d, b, :], snap[:, d, a, :], dex[:, d, a:a + 1],
                                                      umask[:, d, :], ALU.mult, ALU.add)
                    last.then_inc(sem("snap_ready"), 1)
                    dve.wait_ge(sem("snap_ready"), T_("snap").add())
                dve.wait_ge(sem("ex_ready"), T_("ex").add(2))
                for d in range(2):
                    v.tensor_tensor(qe[d][:], qc[:], ex[:, d, :], ALU.mult).then_inc(sem("qe_ready"), 1)
                dve.wait_ge(sem("qe_ready"), T_("qe").add(2))
                v.memset(qbd[0][:], 0.0)
                v.memset(qbd[1][:], 0.0)
                step(v.memset(sacc[:], 0.0))

                seq = [(hf, li, j0, nt) for hf, (j0, nt) in enumerate(halves(l)) for li in range(8)]

                def exponents(it):
                    hf, li, j0, nt = seq[it]
                    if li == 0:
                        return
                    h = LEVELS[li - 1]
                    b = it % 2
                    tok = slice(j0 * P, (j0 + nt) * P)
                    b0 = bb[0][:, tok].rearrange("p (n w h) -> p n w h", w=2, h=h)
                    b1 = bb[1][:, tok].rearrange("p (n w h) -> p n w h", w=2, h=h)
                    eq = eqk[b][:, 0, 0:nt * P].rearrange("p (n w h) -> p n w h", w=2, h=h)
                    ek = eqk[b][:, 1, 0:nt * P].rearrange("p (n w h) -> p n w h", w=2, h=h)
                    ref0, ref1 = bc(b0[:, :, 0, h - 1], h), bc(b1[:, :, 1, 0], h)
                    v.tensor_tensor(eq[:, :, 1, :], b0[:, :, 1, :], ref0, ALU.subtract)
                    v.tensor_tensor(eq[:, :, 0, :], b1[:, :, 0, :], ref1, ALU.subtract)
                    v.tensor_tensor(ek[:, :, 0, :], ref0, b0[:, :, 0, :], ALU.subtract)
                    v.tensor_tensor(ek[:, :, 1, :], ref1, b1[:, :, 1, :], ALU.subtract).then_inc(sem("e_raw"), 1)

                def factors(it):
                    hf, li, j0, nt = seq[it]
                    b = it % 2
                    tok = slice(j0 * P, (j0 + nt) * P)
                    if it >= 2:
                        done = sum(q[3] for q in seq[:it - 1])
                        dve.wait_ge(sem("lev_done"), T_("lev").n + done)
                    if li > 0:
                        dve.wait_ge(sem("e_ready"), T_("er").add())
                        v.tensor_tensor(kl[b][:, 0:nt * P], kc[:, tok], eqk[b][:, 1, 0:nt * P], ALU.mult)
                    for h in range(4):
                        r = slice(32 * h, 32 * h + 32)
                        src = qc[r, tok].rearrange("p (j t) -> p j t", t=P)
                        if li > 0:
                            last = v.tensor_tensor(qbd[b][r, 0:nt, h, :], src,
                                                   eqk[b][r, 0, 0:nt * P].rearrange("p (j t) -> p j t", t=P), ALU.mult)
                        else:
                            last = v.tensor_scalar(qbd[b][r, 0:nt, h, :], src, 2.0, None, ALU.mult)
                    last.then_inc(sem("lev_factors"), 1)
                    dve.wait_ge(sem("lev_factors"), T_("lf").add())

                def merge(it):
                    hf, li, j0, nt = seq[it]
                    if li == 0 and hf == 1:
                        dve.wait_ge(sem("oc_done"), T_("oc").n + 3)
                    if it >= 1:
                        dve.wait_ge(sem("lev_merged"), T_("mm").n)
                    for t in range(nt):
                        k = T_("mm").n
                        dve.wait_ge(sem("lev_done"), T_("lev").n + T_("mm").add() - T_("mm0").n)
                        v.copy_predicated(sacc[:, t], lmask[:, li, :].unsqueeze(1).to_broadcast([P, 4, P]),
                                          bank(k % 4).rearrange("p (h t) -> p h t", h=4)).then_inc(sem("lev_merged"), 1)

                T_("mm0").n = T_("mm").n
                exponents(0)
                for it in range(len(seq)):
                    if it + 1 < len(seq):
                        exponents(it + 1)
                    factors(it)
                    if it >= 1:
                        merge(it - 1)
                merge(len(seq) - 1)
                n_mm = sum(q[3] for q in seq)
                T_("lev").add(n_mm)
                T_("oc").add(sum(nt for _, nt in halves(l)))

            def mlstm(l):
                gates = ft[12]
                v.memset(qdb[:], 0.0).then_inc(sem("qdb_zero"), 1)
                v.memset(cst_d[:], 0.0)
                v.memset(mrun[:], 0.0)
                v.memset(r1[:], 0.0)
                v.memset(r2[:], 0.0)
                v.memset(mp[:], 0.0)
                v.memset(mend[:], 0.0)
                v.memset(dec[:], 0.0)
                step(v.memset(fcum[:], 0.0))
                one = ones[64:68, 0:1].to_broadcast([4, P])
                one1 = ones[96:100, 0:1].to_broadcast([4, P])
                for j in range(TILES):
                    v.tensor_tensor_scan(fcum[0:4, cols(j)], one, gates[64:68, cols(j)], 0.0, ALU.mult, ALU.add)
                    last = v.tensor_tensor_scan(fcum[32:36, cols(j)][:, ::-1], one1, gates[96:100, cols(j)][:, ::-1],
                                                0.0, ALU.mult, ALU.add)
                step(last)
                R = slice(0, 36)
                step(v.tensor_tensor(arow[R, :], gates[R, :], fcum[R, :], ALU.subtract))
                for s in range(TILES):
                    for d in range(2):
                        j = ORDER[d][s]
                        r = slice(32 * d, 32 * d + 4)
                        a_, m_ = arow[r, cols(j)], mrun[r, cols(j)]
                        if d == 1:
                            a_, m_ = a_[:, ::-1], m_[:, ::-1]
                        last = v.tensor_tensor_scan(m_, a_, a_, mp[r, j:j + 1], ALU.max, ALU.max)
                    step(last)
                    if s < TILES - 1:
                        for d in range(2):
                            j, jn = ORDER[d][s], ORDER[d][s + 1]
                            r = slice(32 * d, 32 * d + 4)
                            e = j * P + (P - 1 if d == 0 else 0)
                            last = v.tensor_tensor(mp[r, jn:jn + 1], fcum[r, e:e + 1], mrun[r, e:e + 1], ALU.add)
                        step(last)
                mr = mrun[:].rearrange("p (j t) -> p j t", t=P)
                v.tensor_copy(mend[0:4, :], mr[0:4, :, P - 1])
                step(v.tensor_copy(mend[32:36, :], mr[32:36, :, 0]))

                def tt(ap):
                    return ap.rearrange("p (j t) -> p j t", t=P)
                v.tensor_copy(r1[R, :], arow[R, :])
                v.tensor_tensor(tt(r1[64:100, :]), tt(arow[R, :]), bc(mend[R, :], P), ALU.subtract)
                v.tensor_tensor(tt(r2[R, :]), bc(mp[R, :], P), tt(mrun[R, :]), ALU.subtract)
                v.scalar_tensor_tensor(r2[64:100, :], fcum[R, :], -1.0, mrun[R, :], ALU.mult, ALU.subtract)
                v.tensor_tensor(dec[R, :], mp[R, :], mend[R, :], ALU.subtract).then_inc(sem("r_raw"), 1)
                for q in range(2):
                    dve.wait_ge(sem("r_trans"), T_("rtr").add())
                    last = v.tensor_copy(col[:, :, q, :, :], pair(q, 0, T).rearrange(
                        "p (j a b) -> p j a b", j=TILES, a=4)[:, :, :, 0:4])
                last.then_inc(sem("col_ready"), 1)
                dve.wait_ge(sem("dec_done"), T_("decd").add())
                v.tensor_copy(dcb[:], bank(4, 0, 24).rearrange("p (a j) -> p a j", a=4)).then_inc(sem("dcb_ready"), 1)
                dve.wait_ge(sem("dcb_ready"), T_("dcb").add())
                dve.wait_ge(sem("col_ready"), T_("col").add())
                seen = set()
                for s in range(TILES):
                    cur_, nxt = s % 2, (s + 1) % 2
                    for d in range(2):
                        j = ORDER[d][s]
                        if s < TILES - 1:
                            if s >= 1:
                                dve.wait_ge(sem("ud_done"), T_("udv").add())
                            v.tensor_tensor(vw[:, d], vd1[:, j], bc(col[:, j, 0, 2 + d, :], 65),
                                            ALU.mult).then_inc(sem("vw_ready"), 1)
                    if s == TILES - 1:
                        T_("udv").add(2)
                    outs = [d for d in range(2) if not (l == DEPTH - 1 and ORDER[d][s] >= LAT_TILES)]
                    for d in outs:
                        dve.wait_ge(sem("w_ready"), T_("w").add())
                        dve.wait_ge(sem("qk_done"), T_("qkd").add())
                        v.tensor_tensor(wb[s % 2][:, d], wb[s % 2][:, d],
                                        bank(2 + d).rearrange("p (h t) -> p h t", h=4),
                                        ALU.mult).then_inc(sem("p_ready"), 1)
                    for d in range(2):
                        j = ORDER[d][s]
                        if s < TILES - 1:
                            dve.wait_ge(sem("ud_done"), T_("ud").add())
                            for p_ in range(2):
                                last = v.scalar_tensor_tensor(
                                    cst_d[:, d, nxt, p_, :], cst_d[:, d, cur_, p_, :], dcb[:, 2 * d + p_, j:j + 1],
                                    bank(d, p_ * 65, 65), ALU.mult, ALU.add)
                            last.then_inc(sem("state_ready"), 1)
                            dve.wait_ge(sem("state_ready"), T_("st").add())
                    for d in outs:
                        j = ORDER[d][s]
                        dve.wait_ge(sem("num_done"), T_("num").add())
                        inter = bank(6 + d, 0, 260).rearrange("p (h c) -> p h c", h=4)
                        intra = bank(4 + d, 0, 260).rearrange("p (h c) -> p h c", h=4)
                        step(v.tensor_tensor(t1[:, d], inter, bc(col[:, j, 1, d, :], 65), ALU.mult))
                        step(v.tensor_tensor(t2[:, d], t1[:, d], intra, ALU.add))
                        step(v.scalar_tensor_tensor(dd[:, d, :], t2[:, d, :, 64], -1.0, t2[:, d, :, 64],
                                                    ALU.mult, ALU.max))
                        step(v.tensor_tensor(dd[:, d, :], dd[:, d, :], col[:, j, 1, 2 + d, :], ALU.max))
                        step(v.reciprocal(rd[:, d, :], dd[:, d, :]))
                        dst = y[:, j, 768:1024].rearrange("p (h c) -> p h c", h=4)
                        if j in seen:
                            step(v.tensor_tensor(hh[:, d], t2[:, d, :, 0:64], bc(rd[:, d, :], 64), ALU.mult))
                            v.tensor_tensor(dst, dst, hh[:, d], ALU.add).then_inc(sem("yd_ready"), 1)
                        else:
                            seen.add(j)
                            v.tensor_tensor(dst, t2[:, d, :, 0:64], bc(rd[:, d, :], 64),
                                            ALU.mult).then_inc(sem("yd_ready"), 1)
                        dve.wait_ge(sem("yd_ready"), T_("yd").add())

            def finish(l):
                nj = TILES if l == 0 else LAT_TILES
                dve.wait_ge(sem("sqy_ready"), T_("sqy").add())
                v.tensor_reduce(ms8[:, 0:nj * 8], sqy[:, 0:nj, :].rearrange("p j (h c) -> p (j h) c", c=64),
                                AX_X, ALU.add).then_inc(sem("ms8_ready"), 1)
                dve.wait_ge(sem("sig_raw"), T_("sigr").add())
                sg = sig[:, 0:nj, :]
                step(v.tensor_scalar(sg, sg, 1.0, None, ALU.add))
                step(v.reciprocal(sg, sg))
                step(v.tensor_tensor(sig[:, 0:nj, 0:256], sig[:, 0:nj, 0:256], ro[:, 0:nj, 0:256], ALU.mult))
                yg = y[:, 0:nj, 512:1024]
                step(v.tensor_tensor(sg, sg, rowc[:, 4:516].unsqueeze(1).to_broadcast([P, nj, 512]), ALU.mult))
                step(v.tensor_tensor(yg, yg, sg, ALU.mult))
                dve.wait_ge(sem("rstd8_ready"), T_("r8").add())
                for j in range(nj):
                    yj = y[:, j, 512:1024].rearrange("p (h c) -> p h c", c=64)
                    v.tensor_tensor(yj, yj, bc(ms8[:, 8 * j:8 * j + 8], 64), ALU.mult).then_inc(sem("y_ready"), 1)
                for j in range(nj):
                    dve.wait_ge(sem("yt_hi"), T_("yth").add())
                    v.tensor_tensor(yT_lo[:, :, cols(j)], pair(j).rearrange("p (k t) -> p k t", k=KD),
                                    yT_hi[:, :, cols(j)].bitcast(F32), ALU.subtract).then_inc(sem("yt_ready"), 1)

            def residual(l, n_t, k, ga):
                mt = modt[l][:].rearrange("p (m c) -> p m c", c=2)
                dve.wait_ge(sem("big_done"), big.add())
                v_ = T_("xd")
                for c_i, a, b in [(0, 0, SEQ)] + ([(1, SEQ, T)] if n_t == T else []):
                    ins = v.scalar_tensor_tensor(xT[:, k, a:b], pair(k, a, b - a), mt[:, ga + k, c_i:c_i + 1],
                                                 xT[:, k, a:b], ALU.mult, ALU.add)
                ins.then_inc(sem("x_done"), 1)
                v_.add()

            def mlp_quarter(l, n_t, i):
                def hid_low(m):
                    dve.wait_ge(sem("hid_hi_ready"), T_("hh2").add())
                    v.tensor_tensor(hid_lo[:, m, 0:n_t], tmp[2 + m % 2][:, 0:n_t],
                                    hid_hi[:, m, 0:n_t].bitcast(F32), ALU.subtract).then_inc(sem("hid_ready"), 1)
                dve.wait_ge(sem("x_done"), T_("xd").at(0))
                for s in range(QW1 + QW2):
                    for m in range(2):
                        g = 2 * s + m
                        if s < QW1:
                            big.add()
                            dve.wait_ge(sem("relu_done"), T_("relu").add())
                            if g >= 2:
                                dve.wait_ge(sem("hid_ready"), T_("hh2").at(0))
                            v.tensor_tensor(tmp[2 + g % 2][:, 0:n_t], tmp[6 + g % 2][:, 0:n_t],
                                            tmp[6 + g % 2][:, 0:n_t], ALU.mult).then_inc(sem("sq2_ready"), 1)
                            if g >= 1:
                                hid_low(g - 1)
                        else:
                            residual(l, n_t, g - 2 * QW1, 40)
                    if s == QW1 - 1:
                        hid_low(2 * QW1 - 1)
                    if l == 0 and s < Q_MODS:
                        mod_out(1, s, i)

            for l in range(DEPTH):
                n_t = T if l == 0 else SEQ
                norm(l, 1, T)
                in_proj(l)
                stage_end()
                prep_ab(l)
                attention(l)
                stage_end()
                gla(l)
                stage_end()
                mlstm(l)
                stage_end()
                finish(l)
                for s in range(OUT_SLOTS):
                    for m in range(2):
                        if s == 0 and m == 0:
                            dve.wait_ge(sem("mod_out"), mod_n.at(0))
                        residual(l, n_t, 2 * s + m, 16)
                    if mod_after(l, IN_SLOTS + s) is not None:
                        mod_out(0, mod_after(l, IN_SLOTS + s))
                norm(l, 2, n_t)
                n_loop = QUARTERS if l < DEPTH - 1 else QUARTERS - 1
                looped = [(big, 16), (T_("relu"), 8), (T_("hh2"), 8), (T_("xd"), 8),
                          (mod_n, Q_MODS if l == 0 else 0)]
                with dve.Fori(0, n_loop) as i:
                    for t, per in looped:
                        t.enter(i, per)
                    mlp_quarter(l, n_t, i)
                for t, per in looped:
                    t.leave(n_loop)
                if l == DEPTH - 1:
                    mlp_quarter(l, n_t, None)
            for j in range(LAT_TILES):
                dve.wait_ge(sem("out_trans"), j + 1)
                if j >= 2:
                    dve.wait_ge(sem(f"out_stored{j % 2}"), 16 * (j // 2))
                v.tensor_copy(xout[j % 2][:], pair(j)).then_inc(sem("out_ready"), 1)

        @blk.tensor
        def _(pe):
            c = {}

            def T_(name):
                return c.setdefault(name, Tally())

            mm = nc.tensor.matmul
            stage_n = [0]

            def stage_end():
                pe.drain().then_inc(sem("stage_done"), 1)
                stage_n[0] += 3
                pe.wait_ge(sem("stage_done"), stage_n[0])

            pe.wait_ge(sem("c_landed"), 64)
            nc.tensor.transpose(bank(7, P, LV), vin1[0:LV, :], ident[0:LV, 0:LV])
            nc.tensor.transpose(bank(7, 0, V_ALL), vin[0:V_ALL, :], ident[0:V_ALL, 0:V_ALL]).then_inc(sem("v_trans"), 1)

            def x_tile(j):
                pe.wait_ge(sem(f"x_landed{j % 2}"), 16 * (j // 2 + 1))
                if j >= 2:
                    pe.wait_ge(sem("x_in"), j - 1)
                for k in range(KD):
                    ins = nc.tensor.transpose(pair(j, k * P, P), xin[j % 2][:, k * P:(k + 1) * P], ident)
                ins.then_inc(sem("x_trans"), 1)

            mods, wts = Tally(), Tally()
            mod_l = [0, 0]

            def mod_slot(r):
                if mods.term is None and mods.n < FIRST_MODS:
                    pe.wait_ge(sem(f"mod_landed{r}"), 16 * (mods.n // 2 + 1))
                else:
                    pe.wait_ge(sem("mod_landed1"), 16 * (mods.at(-FIRST_MODS // 2) + 1)
                               if mods.term is None else (mods.term + (mods.n + 1 - FIRST_MODS // 2)) * 16)
                if not (mods.term is None and mods.n == 0):
                    pe.wait_ge(sem("mod_out"), mods.at(0))
                for m in range(2):
                    for k in range(KD):
                        ins = mm(bank(6, 2 * m, 2), raw[r][:, k, m * P:(m + 1) * P], cs[:, k, :],
                                 start=(k == 0), stop=(k == KD - 1))
                ins.then_inc(sem("mod_used"), 1)
                mods.add()

            pe.wait_ge(sem("cs_ready"), 1)
            for s in range(FIRST_MODS):
                if s < TILES:
                    x_tile(s)
                mod_slot(s % 2)

            def passes(r):
                return ((w_hi[r], 0), (w_hi[r], 1), (w_lo[r], 0))

            def feature_group(g, r, m, mov, n_t, ready=None):
                spans = [(0, SEQ)] + ([(SEQ, T)] if n_t == T else [])
                for k in range(KD):
                    if ready is not None:
                        pe.wait_ge(ready[0], ready[1] + k + 1)
                    for q, (w, hl) in enumerate(passes(r)):
                        for a, b in spans:
                            ins = mm(pair(g, a, b - a), w[:, k, m * P:(m + 1) * P], mov[hl][:, k, a:b],
                                     start=(k == 0 and q == 0), stop=(k == KD - 1 and q == 2))
                ins.then_inc(sem("big_done"), 1)

            def norm_sum(n_t):
                pe.wait_ge(sem("acc_added"), T_("acc").add(KD - 1))
                ins = mm(bank(4), ones[:], tmp[2][:, 0:SEQ], start=True, stop=True)
                if n_t == T:
                    ins = mm(bank(5, 0, CTX), ones[:], tmp[2][:, SEQ:T], start=True, stop=True)
                ins.then_inc(sem("ms_ready"), 1)

            def in_proj(l):
                ft0, vt0, h0 = T_("ft").n, T_("vt").n, T_("h").n
                for s in range(IN_SLOTS):
                    r = wts.n % 2
                    pe.wait_ge(sem("lo_ready"), wts.add())
                    for m in range(2):
                        g = 2 * s + m
                        if g == FEATS:
                            continue
                        if 2 <= g <= FEATS + 1:
                            pe.wait_ge(sem("ft_ready"), ft0 + min(g - 1, FEATS))
                        elif g > FEATS + 1:
                            n = g - FEATS - 2
                            if n >= 1:
                                pe.wait_ge(sem("vt_ready"), vt0 + n)
                        if g < FEATS:
                            feature_group(g, r, m, (h_hi, h_lo), T, (sem("h_ready"), h0) if g == 0 else None)
                        else:
                            j0, n = (0, 4) if m == 0 else (4, 2)
                            for j in range(j0, j0 + n):
                                for k in range(KD):
                                    for q, (w, hl) in enumerate(passes(r)):
                                        ins = mm(pair(g, (j - j0) * 256, 256), (h_hi, h_lo)[hl][:, k, cols(j)],
                                                 w[:, k, :], start=(k == 0 and q == 0),
                                                 stop=(k == KD - 1 and q == 2))
                            ins.then_inc(sem("big_done"), 1)
                    if mod_after(l, s) is not None:
                        mod_slot(1)
                T_("ft").add(FEATS), T_("vt").add(10), T_("h").add(KD)

            def prep_ab():
                for i in range(6):
                    pe.wait_ge(sem("sqab_ready"), T_("sqab").add())
                    if i >= 2:
                        pe.wait_ge(sem("lnab_done"), T_("lnab").n + i - 1)
                    mm(pair(i, 0, SEQ), block, rab[:, i, 0:SEQ], start=True, stop=True)
                    mm(pair(i, SEQ, CTX), block, rab[:, i, SEQ:T], start=True, stop=True).then_inc(sem("msab_ready"), 1)
                T_("lnab").add(6)
                pe.wait_ge(sem("lnab_done"), T_("lnab").n)
                for i in range(6):
                    pe.wait_ge(sem("gswap_ready"), T_("gsw").add())
                    mm(bank(4 + i % 4) if i < 4 else bank(i - 4), gswap[:], ft[i][:, 0:SEQ], start=True,
                       stop=True).then_inc(sem("rot_done"), 1)

            def attention(l):
                units = att_units(l)
                n = len(units)
                e0, q0, y0, pt0 = T_("exp").n, T_("qk").n, T_("yab").n, T_("pt").n
                pe.wait_ge(sem("qk_ready"), T_("qk").add(6))

                def scores(u):
                    m, j, h = units[u]
                    lo, keys, masks = key_span(m, j)
                    if u >= 2:
                        pe.wait_ge(sem("exp_done"), e0 + u - 1)
                    q = ft[3 * m + h % 2][:, cols(j)]
                    k_ = ft[3 * m + 2] if h < 2 else kb1[m]
                    if lo < 512:
                        mm(pair(u, lo, 512 - lo), q, k_[:, keys[0] * P:keys[0] * P + 512 - lo], start=True,
                           stop=not masks)
                        for x_, (mk, at) in enumerate(masks):
                            mm(pair(u, at, P), ident_b[:], mk[:], start=False, stop=(x_ == len(masks) - 1))
                    mm(pair(u, 512, CTX), q, k_[:, SEQ:T], start=True, stop=True).then_inc(sem("sc_done"), 1)

                def transposes(u):
                    m, j, h = units[u]
                    _, keys, _ = key_span(m, j)
                    pe.wait_ge(sem("exp_done"), e0 + u + 1)
                    if u >= 1:
                        pe.wait_ge(sem("pt_ready"), pt0 + u)
                    for t in range(len(keys)):
                        ins = nc.tensor.transpose(bank(4, t * P, P), prob[u % 2][:, cols(t)], ident)
                    ins.then_inc(sem("tr_done"), 1)

                def values(u):
                    m, j, h = units[u]
                    _, keys, _ = key_span(m, j)
                    jj = u // 4
                    pe.wait_ge(sem("pt_ready"), pt0 + u + 1)
                    if h == 0 and jj >= 2:
                        pe.wait_ge(sem("yab_ready"), y0 + jj - 1)
                    for t, kt in enumerate(keys):
                        ins = mm(bank(6 + jj % 2, h * 64, 64), probT[u % 2][:, cols(t)],
                                 v_ab[:, kt, m * P + (h // 2) * 64:m * P + (h // 2) * 64 + 64],
                                 start=(t == 0), stop=(t == len(keys) - 1))
                    ins.then_inc(sem("pv_done"), 1)

                scores(0)
                for u in range(n):
                    if u + 1 < n:
                        scores(u + 1)
                    if u >= 1:
                        values(u - 1)
                    transposes(u)
                values(n - 1)
                T_("exp").add(n), T_("yab").add(n // 4), T_("pt").add(n)

            def gla(l):
                for d in range(2):
                    pe.wait_ge(sem("lay_landed"), 32 * (l + 1))
                    mm(pair(d, 0, SEQ), wg[:, d, :], ft[12][:, 0:SEQ], start=True, stop=True)
                    mm(pair(d, SEQ, CTX), wg[:, d, :], ft[12][:, SEQ:T], start=True, stop=True)\
                        .then_inc(sem("pre_done"), 1)
                for d in range(2):
                    pe.wait_ge(sem("kdec_ready"), T_("kdec").add())
                    for j in range(TILES):
                        ins = nc.tensor.transpose(pair(d, j * P, P), kdec[d][:, cols(j)], ident)
                    ins.then_inc(sem("kt_done"), 1)
                pe.wait_ge(sem("ktc_ready"), T_("ktc").add(2))
                for s in range(TILES - 1):
                    if s >= 2:
                        pe.wait_ge(sem("snap_ready"), T_("snap").n + s - 1)
                    for d in range(2):
                        j = ORDER[d][s]
                        ins = mm(bank(4 + s % 2, d * 256, 256), ktc[d][:, cols(j)], vc[:, j, :], start=True, stop=True)
                    ins.then_inc(sem("u_done"), 1)
                T_("snap").add(TILES - 1)
                n_oc = 0
                for hf, (j0, nt) in enumerate(halves(l)):
                    for li in range(8):
                        b = (hf * 8 + li) % 2
                        pe.wait_ge(sem("lev_factors"), T_("lf").add())
                        for t in range(nt):
                            k = T_("mm").n
                            if k - T_("mm0").n >= 4:
                                pe.wait_ge(sem("lev_merged"), T_("mg").n + k - T_("mm0").n - 3)
                            kk = ft[7][:, cols(j0 + t)] if li == 0 else kl[b][:, cols(t)]
                            mm(bank(k % 4), kk, qbd[b][:, t], start=True, stop=True).then_inc(sem("lev_done"), 1)
                            T_("mm").add()
                    pe.wait_ge(sem("lev_merged"), T_("mg").n + T_("mm").n - T_("mm0").n)
                    if hf == 0:
                        pe.wait_ge(sem("qe_ready"), T_("qe").add(2))
                        pe.wait_ge(sem("snap_ready"), T_("snap").n)
                    for t in range(nt):
                        j = j0 + t
                        if n_oc >= 2:
                            pe.wait_ge(sem("yc_ready"), T_("yc").n + n_oc - 1)
                        ob = 4 + j % 2
                        mm(bank(ob, 0, 256), qe[0][:, cols(j)], snap[:, 0, j, :], start=True, stop=False)
                        mm(bank(ob, 0, 256), qe[1][:, cols(j)], snap[:, 1, j, :], start=False, stop=False)
                        for h in range(4):
                            ins = mm(bank(ob, h * 64, 64), sacc[:, t, h, :], vc[:, j, h * 64:h * 64 + 64],
                                     start=False, stop=(h == 3))
                        ins.then_inc(sem("oc_done"), 1)
                        n_oc += 1
                T_("mg").add(T_("mm").n - T_("mm0").n)
                T_("mm0").n = T_("mm").n
                T_("yc").add(n_oc)

            def mlstm(l):
                for a, n in ((0, 4), (4, 2)):
                    for j in range(a, a + n):
                        for p_ in range(2):
                            ins = nc.tensor.transpose(pair(a // 4, (j - a) * 256 + p_ * P, P),
                                                      ft[10 + p_][:, cols(j)], ident)
                    ins.then_inc(sem("kd_done"), 1)
                pe.wait_ge(sem("ktd_ready"), T_("ktd").add(2))
                pe.wait_ge(sem("r_ready"), T_("r").add(3))
                for q in range(2):
                    for j in range(TILES):
                        ins = nc.tensor.transpose(pair(q, j * P, P), (r1, r2)[q][:, cols(j)], ident)
                    ins.then_inc(sem("r_trans"), 1)
                for d in range(2):
                    for p_ in range(2):
                        for hf in range(2):
                            h = 4 * d + 2 * p_ + hf
                            a = 4 * 512 + (2 * d + p_) * TILES
                            ins = mm(ps[64 * hf:64 * hf + 64, a:a + TILES], sel[:, h:h + 1].to_broadcast([P, 64]),
                                     dec[:], start=True, stop=True)
                ins.then_inc(sem("dec_done"), 1)
                pe.wait_ge(sem("qdb_ready"), T_("qdb").add(4))
                pe.wait_ge(sem("col_ready"), T_("col").add())
                pe.wait_ge(sem("dcb_ready"), T_("dcb").add())
                st0 = T_("st").n
                for s in range(TILES):
                    cur_ = s % 2
                    outs = [d for d in range(2) if not (l == DEPTH - 1 and ORDER[d][s] >= LAT_TILES)]
                    if s >= 1:
                        pe.wait_ge(sem("state_ready"), st0 + 2 * s)
                    for d in outs:
                        j = ORDER[d][s]
                        mk = (p_after, p_before)[d]
                        mm(bank(d), ident_b[:], mk[:].unsqueeze(1).to_broadcast([P, 4, P]), start=True, stop=False)
                        for h in range(4):
                            ins = mm(bank(d, h * P, P), sel[:, 4 * d + h:4 * d + h + 1].to_broadcast([P, P]),
                                     mrun[:, cols(j)], start=False, stop=(h == 3))
                        ins.then_inc(sem("mb_done"), 1)
                        if T_("pk").n >= 1:
                            pe.wait_ge(sem("p_ready"), T_("pr").n)
                        for p_ in range(2):
                            ins = mm(bank(2 + d, p_ * 256, 256), ft[10 + p_][:, cols(j)],
                                     qdb[:, 2 * p_:2 * p_ + 2, cols(j)], start=True, stop=True)
                        ins.then_inc(sem("qk_done"), 1)
                    if s < TILES - 1:
                        for d in range(2):
                            j = ORDER[d][s]
                            pe.wait_ge(sem("vw_ready"), T_("vw").add())
                            if d in outs:
                                pe.wait_ge(sem("w_ready"), T_("w").add())
                            for h in range(4):
                                hf = h % 2
                                a = d * 512 + (h // 2) * 65
                                ins = mm(ps[64 * hf:64 * hf + 64, a:a + 65], ktd[:, j, h * 64:h * 64 + 64],
                                         vw[:, d, h, :], start=True, stop=True)
                            ins.then_inc(sem("ud_done"), 1)
                    else:
                        T_("w").add(len(outs))
                    for d in outs:
                        j = ORDER[d][s]
                        pe.wait_ge(sem("p_ready"), T_("pr").add())
                        if T_("ydn").n >= 2:
                            pe.wait_ge(sem("yd_ready"), T_("ydn").n - 1)
                        T_("ydn").add()
                        T_("pk").add()
                        for h in range(4):
                            mm(bank(6 + d, h * 65, 65), qdb[:, h, cols(j)], cst_d[:, d, cur_, h // 2, :],
                               start=True, stop=True)
                        for h in range(4):
                            ins = mm(bank(4 + d, h * 65, 65), wb[s % 2][:, d, h, :], vd1[:, j, h, :],
                                     start=True, stop=True)
                        ins.then_inc(sem("num_done"), 1)
                T_("st").add(2 * (TILES - 1))

            def finish(l):
                nj = TILES if l == 0 else LAT_TILES
                lo0 = T_("ytl").n
                for j in range(nj):
                    pe.wait_ge(sem("y_ready"), T_("y").add())
                    if j >= 2:
                        pe.wait_ge(sem("yt_ready"), lo0 + j - 1)
                    for k in range(KD):
                        ins = nc.tensor.transpose(pair(j, k * P, P), y[:, j, k * P:(k + 1) * P], ident)
                    ins.then_inc(sem("yt_done"), 1)
                T_("ytl").add(nj)
                pe.wait_ge(sem("yt_ready"), T_("ytl").n)

            def out_proj(l, n_t):
                for s in range(OUT_SLOTS):
                    r = wts.n % 2
                    pe.wait_ge(sem("lo_ready"), wts.add())
                    for m in range(2):
                        k = 2 * s + m
                        if k >= 2:
                            pe.wait_ge(sem("x_done"), T_("xd").n - 1)
                        feature_group(k, r, m, (yT_hi, yT_lo), n_t)
                        T_("xd").add()
                    if mod_after(l, IN_SLOTS + s) is not None:
                        mod_slot(1)

            def mlp_quarter(l, n_t, i, first):
                for s in range(QW1 + QW2):
                    r = s % 2
                    pe.wait_ge(sem("lo_ready"), wts.add())
                    for m in range(2):
                        g = 2 * s + m
                        if g < 2:
                            pe.wait_ge(sem("x_done"), T_("xd").at(g - 1))
                        elif g < 10:
                            pe.wait_ge(sem("relu_done"), T_("relu").at(g - 9 if s >= QW1 else -1))
                        else:
                            pe.wait_ge(sem("x_done"), T_("xd").at(-1))
                        if s < QW1:
                            feature_group(g, r, m, (h_hi, h_lo), n_t,
                                          (sem("h_ready"), T_("h").n - KD) if first and g == 0 else None)
                            T_("relu").add()
                        else:
                            if g == 2 * QW1:
                                feature_group(g, r, m, (hid_hi, hid_lo), n_t, (sem("hid_ready"), T_("hid").at(0)))
                                T_("hid").add(8)
                            else:
                                feature_group(g, r, m, (hid_hi, hid_lo), n_t)
                            T_("xd").add()
                    if l == 0 and s < Q_MODS:
                        mod_slot(1)

            for l in range(DEPTH):
                n_t = T if l == 0 else SEQ
                norm_sum(T)
                in_proj(l)
                stage_end()
                prep_ab()
                attention(l)
                stage_end()
                gla(l)
                stage_end()
                mlstm(l)
                stage_end()
                finish(l)
                out_proj(l, n_t)
                norm_sum(n_t)
                T_("h").add(KD)
                n_loop = QUARTERS if l < DEPTH - 1 else QUARTERS - 1
                pe.wait_ge(sem("h_ready"), T_("h").n)
                looped = [(wts, 8), (T_("relu"), 8), (T_("hid"), 8), (T_("xd"), 8), (mods, Q_MODS if l == 0 else 0)]
                with pe.Fori(0, n_loop) as i:
                    for t, per in looped:
                        t.enter(i, per)
                    mlp_quarter(l, n_t, i, False)
                for t, per in looped:
                    t.leave(n_loop)
                if l == DEPTH - 1:
                    mlp_quarter(l, n_t, None, False)
            pe.wait_ge(sem("x_done"), T_("xd").n)
            for j in range(LAT_TILES):
                if j >= 2:
                    pe.wait_ge(sem("out_ready"), j - 1)
                for k in range(KD):
                    ins = nc.tensor.transpose(pair(j, k * P, P), xT[:, k, cols(j)], ident)
                ins.then_inc(sem("out_trans"), 1)


def _slots(w, widths=WC):
    k, m = w.shape
    return w.reshape(k // P, P, m // widths, widths).transpose(2, 1, 0, 3).reshape(m // widths, P, -1)


def _in_columns():
    gw, kw, gk = 256, 128, 128
    names = [("qa", gw), ("ka", kw), ("va", kw), ("qb", gw), ("kb", kw), ("vb", kw), ("qc", gk), ("kc", gk),
             ("vc", gw), ("rc", gw), ("gc", 32), ("qd", gw), ("kd", gw), ("vd", gw), ("od", gw), ("id", 8), ("fd", 8)]
    at, c = {}, 0
    for n, w in names:
        at[n] = np.arange(c, c + w)
        c += w

    def q_pair(n, p):
        return np.concatenate([at[n][64 * p:64 * p + 64], at[n][64 * (p + 2):64 * (p + 2) + 64]])
    gates = -np.ones(P, dtype=np.int64)
    gates[0:4] = at["id"][0:4]
    gates[32:36] = at["id"][4:8]
    gates[16:32] = at["gc"][0:16]
    gates[48:64] = at["gc"][16:32]
    gates[64:68] = at["fd"][0:4]
    gates[96:100] = at["fd"][4:8]
    return np.concatenate([q_pair("qa", 0), q_pair("qa", 1), at["ka"], q_pair("qb", 0), q_pair("qb", 1), at["kb"],
                           at["qc"], at["kc"], at["qd"], at["kd"], gates, -np.ones(P, dtype=np.int64),
                           at["va"], at["vb"], at["vc"], at["vd"], at["rc"], at["od"]])


def _constants():
    c = np.zeros((P, C_ALL), np.float32)
    p = np.arange(P)
    c[:, C_IDENT:C_IDENT + P] = np.eye(P)
    c[:, C_BLOCK:C_BLOCK + P] = (p[:, None] // HD == p[None, :] // HD)
    sw = np.zeros((P, P), np.float32)
    e = np.arange(0, P, 2)
    sw[e + 1, e] = -1.0
    sw[e, e + 1] = 1.0
    c[:, C_SWAP:C_SWAP + P] = sw
    t = np.arange(SEQ)
    n_freq = HD // 4
    inv = np.float32(ROPE_THETA) ** (-np.arange(n_freq, dtype=np.float32) / np.float32(n_freq))
    row = (t // GRID_W).astype(np.float32)
    col = (t % GRID_W).astype(np.float32)
    ang = np.concatenate([row[:, None] * inv, col[:, None] * inv], axis=-1).astype(np.float32)
    idx = (p % HD) // 2
    c[:, C_COS:C_COS + SEQ] = np.cos(ang).T[idx]
    c[:, C_SIN:C_SIN + SEQ] = np.sin(ang).T[idx]
    for d in range(2):
        for h in range(4):
            c[32 * d + h, C_SEL + 4 * d + h] = 1.0
            c[32 * h:32 * h + 32, C_HM + 4 * d + h] = 1.0
    s_, t_ = p[:, None], p[None, :]
    c[:, C_LEVEL:C_LEVEL + P] = np.eye(P)
    for i, h in enumerate(LEVELS):
        same = (s_ // (2 * h)) == (t_ // (2 * h))
        c[:, C_LEVEL + (i + 1) * P:C_LEVEL + (i + 2) * P] = same & ((s_ // h) != (t_ // h))
    c[:, C_LEFT:C_LEFT + P] = t_ < s_
    c[:, C_RIGHT:C_RIGHT + P] = t_ > s_
    return c


def kernel(**inputs):
    import concourse.bacc as _bacc
    from concourse.bass_utils import run_bass_kernel_spmd as _run

    a = {k: np.ascontiguousarray(v) for k, v in inputs.items()}
    cols_ = _in_columns()
    slots, mods, vrows, gate, row_list = [], [], [a["c"][0].reshape(KD, P), a["c_ctx"].reshape(KD, P)], [], []
    for l in range(DEPTH):
        mods.append(_slots(a["w_mod"][l]))
        w_in = np.zeros((D_MODEL, len(cols_)), a["w_in"].dtype)
        w_in[:, cols_ >= 0] = a["w_in"][l][:, cols_[cols_ >= 0]]
        slots.append(_slots(w_in))
        slots.append(_slots(a["w_out"][l]))
        for q in range(QUARTERS):
            w = D_MODEL
            slots.append(_slots(a["w_mlp1"][l][:, q * w:(q + 1) * w]))
            slots.append(_slots(a["w_mlp2"][l][q * w:(q + 1) * w, :]))
        gb = np.zeros((1, P), np.float32)
        gb[0, 0:4], gb[0, 32:36] = a["b_mlstm_i"][l]
        gb[0, 64:68], gb[0, 96:100] = a["b_mlstm_f"][l]
        vrows += [a["b_mod"][l].reshape(48, P), a["g_norm1"][l].reshape(KD, P), a["g_norm2"][l].reshape(KD, P), gb]
        vrows += [np.tile(a[n][l], 2)[None] for n in ("g_q_a", "g_k_a", "g_q_b", "g_k_b")]
        vrows.append(a["b_gla_gate"][l])
        g = np.zeros((P, 2, P), np.float32)
        g[16:32, 0] = a["w_gla_gate"][l, 0]
        g[48:64, 1] = a["w_gla_gate"][l, 1]
        gate.append(g)
        row_list.append(np.concatenate([a["sink_b"][l], np.tile(a["g_gla_out"][l], 4), np.tile(a["g_mlstm_out"][l], 4)]))
    arrays = {
        "x_in": a["x"][0], "ctx_in": a["ctx"][0], "w_big": np.concatenate(slots), "w_modl": np.concatenate(mods),
        "vecs": np.concatenate(vrows), "consts": _constants(), "gla_gate": np.stack(gate), "rows": np.stack(row_list),
    }
    nc = _bacc.Bacc("TRN2", target_bir_lowering=False, num_devices=1)
    args = [nc.dram_tensor(n, v.shape, F32, kind="ExternalInput").ap() for n, v in arrays.items()]
    out = nc.dram_tensor("out", (SEQ, D_MODEL), F32, kind="ExternalOutput").ap()
    build(nc, *args, out)
    r = _run(nc, [arrays], core_ids=[0])
    return r.results[0]["out"][None]
```

```python
import numpy as np
import concourse.bass as bass
from concourse import mybir

F32 = mybir.dt.float32
F32R = mybir.dt.float32r
BF16 = mybir.dt.bfloat16
U8 = mybir.dt.uint8
ALU = mybir.AluOpType
ACT = mybir.ActivationFunctionType
AX_X = mybir.AxisListType.X

P = 128
D_MODEL = 1024
SEQ = 512
CTX = 256
T = SEQ + CTX
DEPTH = 2
GRID_W = 64
HD = 64
KD = D_MODEL // P
TILES = T // P
LAT_TILES = SEQ // P
GLA_DK = 32
GATE_RANK = 16
GLA_TAU = 16.0
ROPE_THETA = 10000.0
EPS = 1e-6
BIG = 1e30
N_MOD = 6
WC = 256
MOD_SLOTS = N_MOD * D_MODEL // WC
IN_SLOTS = 12
OUT_SLOTS = D_MODEL // WC
QUARTERS = 4
QW1 = 4
QW2 = 4
LAYER_SLOTS = IN_SLOTS + OUT_SLOTS + QUARTERS * (QW1 + QW2)
FIRST_MODS = 8
FEATS = 13
ONE_RAW = LAYER_SLOTS + 2
Q_FEATS = (0, 1, 3, 4, 6, 8, 9)
ORDER = ((4, 5, 0, 1, 2, 3), (5, 4, 3, 2, 1, 0))
LEVELS = (64, 32, 16, 8, 4, 2, 1)

C_IDENT, C_BLOCK, C_SWAP = 0, P, 2 * P
C_COS = 3 * P
C_SIN = C_COS + SEQ
C_SEL = C_SIN + SEQ
C_HM = C_SEL + 8
C_KEEP = C_HM + 8
C_LEVEL = C_KEEP
C_LEFT = C_LEVEL + 8 * P
C_RIGHT = C_LEFT + P
C_ALL = C_RIGHT + P

V_C = 0
V_CC = KD
V_L = 2 * KD
LV_BMOD, LV_G1, LV_G2, LV_GB = 0, 48, 56, 64
LV_GQK = 65
LV_BG = 69
LV = 71
V_ALL = V_L + LV


class Tally:

    def __init__(self):
        self.n = 0
        self.term = None

    def add(self, k=1):
        self.n += k
        return self.at(0)

    def at(self, back):
        v = self.n + back
        return v if self.term is None else self.term + v

    def enter(self, i, per):
        self.start, self.per = self.n, per
        if i is not None:
            self.term = i * per

    def leave(self, times):
        assert self.n - self.start == self.per, (self.n, self.start, self.per)
        self.n = self.start + self.per * times
        self.term = None


def build(nc, x_in, ctx_in, w_big, w_mod, vecs, consts, gla_gate, rows, out):
    def place(name, off, shape, dt=F32):
        return nc.alloc_sbuf_tensor_at(name, [P] + list(shape), dt, offset=off)

    base = (nc.sbuf_base + 63) // 64 * 64
    cur = [base]

    def keep(name, shape, dt=F32):
        size = int(np.prod(shape)) * {F32: 4, F32R: 4, BF16: 2, U8: 1}[dt]
        off = cur[0]
        cur[0] += (size + 31) // 32 * 32
        return place(name, off, shape, dt)

    xT = keep("xT", [KD, T])
    raw = [keep(f"raw{r}", [KD, WC]) for r in range(2)]
    w_hi = [keep(f"w_hi{r}", [KD, WC], F32R) for r in range(2)]
    w_lo = [keep(f"w_lo{r}", [KD, WC], F32R) for r in range(2)]
    cst = keep("cst", [C_KEEP])
    ones = keep("ones", [P])
    lmask = keep("lmask", [8, P], U8)
    ident_b = keep("ident_b", [P], BF16)
    m_left = keep("m_left", [P], BF16)
    m_right = keep("m_right", [P], BF16)
    p_after = keep("p_after", [P], BF16)
    p_before = keep("p_before", [P], BF16)
    vcol = [keep("vcol0", [V_ALL]), keep("vcol1", [LV])]
    cs = keep("cs", [KD, 2])
    modt = [keep(f"modt{l}", [2 * 48]) for l in range(DEPTH)]
    gs = keep("gs", [KD, 2])
    mod_acc_at = cur[0]
    mod_acc = keep("mod_acc", [2, WC])
    wg = keep("wg", [2, P])
    rowc = keep("rowc", [4 + 2 * 256])
    nsink = keep("nsink", [4])
    eps = keep("eps", [1])
    mx = keep("mx", [2])
    nb = keep("nb", [2, 4])
    se = keep("se", [2, 4])
    es = keep("es", [2, 4])
    psum_e = keep("psum_e", [2, 4])
    rs = keep("rs", [2, 4])
    dex = keep("dex", [2, TILES])
    mp = keep("mp", [TILES])
    mend = keep("mend", [TILES])
    dec = keep("dec", [TILES])
    dcb = keep("dcb", [4, TILES])
    ms8 = keep("ms8", [TILES * 8])
    ident = cst[:, C_IDENT:C_IDENT + P]
    block = cst[:, C_BLOCK:C_BLOCK + P]
    swap = cst[:, C_SWAP:C_SWAP + P]
    cos = cst[:, C_COS:C_COS + SEQ]
    sin = cst[:, C_SIN:C_SIN + SEQ]
    sel = cst[:, C_SEL:C_SEL + 8]
    hm8 = cst[:, C_HM:C_HM + 8]

    TB = T * 4
    RH = cur[0]
    RS = RH + KD * TB
    RU = RS + KD * TB
    RV = RU + 16 * TB
    END = RV + 6 * 260 * 4 + 6 * 256 * 4 + 6 * 512 * 4
    assert END <= nc.sbuf_usable_end, (END, nc.sbuf_usable_end)

    h_hi = place("h_hi", RH, [KD, T], F32R)
    h_lo = place("h_lo", RS, [KD, T], F32R)
    y = place("y", RH, [TILES, 4 * 256])
    SLOT = KD * WC * 4
    xin = [place(f"xin{j}", RU + j * D_MODEL * 4, [D_MODEL]) for j in range(TILES)]
    first_at = [RS + j * SLOT for j in range(3)] + [RU + (3 + j) * SLOT for j in range(3)] + [RH, RH + SLOT]
    first_mod = [place(f"first_mod{j}", a, [KD, WC]) for j, a in enumerate(first_at)]
    mod_rows = place("mod_rows", RV + 5 * T * 4, [FIRST_MODS * WC])
    cload = place("cload", RH + 2 * SLOT, [C_ALL - C_KEEP])
    vin = place("vin", RH + 2 * SLOT + (C_ALL - C_KEEP) * 4, [P])
    vin1 = place("vin1", RH + 2 * SLOT + (C_ALL - C_KEEP) * 4 + P * 4, [P])
    xout = [place(f"xout{i}", RH + i * 4096, [D_MODEL]) for i in range(2)]
    tmp = [place(f"tmp{i}", RV + i * TB, [T]) for i in range(8)]
    ft = [None] * FEATS
    v_ab = place("v_ab", RU + 6 * TB, [TILES, 256])
    for i in range(6):
        ft[i] = place(f"ft{i}", RU + i * TB, [T])
    for i in range(6, FEATS):
        ft[i] = place(f"ft{i}", RU + (i + 2) * TB, [T])
    SPARE = RU + 15 * TB
    vd1 = place("vd1", RV, [TILES, 4, 65])
    vc = place("vc", RV + 6 * 260 * 4, [TILES, 256])
    ro = place("ro", RV + 6 * 516 * 4, [TILES, 512])
    yT_hi = place("yT_hi", RU, [KD, T], F32R)
    yT_lo = place("yT_lo", RU + KD * TB, [KD, T], F32R)
    hid_hi = place("hid_hi", RU, [KD, T], F32R)
    hid_lo = place("hid_lo", RU + KD * TB, [KD, T], F32R)
    gswap = place("gswap", mod_acc_at, [P])
    rab = place("rab", RS, [6, T])
    kb1 = [place(f"kb1_{m}", RS + (6 + m) * TB, [T]) for m in range(2)]
    rt = [place(f"rt{i}", RH + i * 2048, [SEQ]) for i in range(2)]
    prob = [place(f"prob{i}", RS + i * TB, [T]) for i in range(2)]
    probT = [place(f"probT{i}", RS + (2 + i) * TB, [T]) for i in range(2)]
    bb = [place(f"bb{d}", RS + d * TB, [T]) for d in range(2)]
    snap = place("snap", RS + 2 * TB, [2, TILES, 256])
    qe = [place(f"qe{d}", RS + (6 + d) * TB, [T]) for d in range(2)]
    ls = place("ls", RU, [3, T])
    pre = [place(f"pre{d}", RU + (3 + d) * TB, [T]) for d in range(2)]
    ex = place("ex", RU + 5 * TB, [2, T])
    kdec = [place(f"kdec{d}", RU + d * TB, [T]) for d in range(2)]
    ktc = [place(f"ktc{d}", RU + (2 + d) * TB, [T]) for d in range(2)]
    umask = place("umask", RU + 7 * TB, [2, 256])
    HT = 3 * P
    sacc = place("sacc", RU, [3, 4, P])
    eqk = [place(f"eqk{b}", RU + (2 + b) * TB, [2, HT]) for b in range(2)]
    qbd = [place(f"qbd{b}", RU + (4 + 2 * b) * TB, [3, 4, P]) for b in range(2)]
    kl = [place(f"kl{b}", SPARE + b * HT * 4, [HT]) for b in range(2)]
    qdb = place("qdb", RS, [4, T])
    ktd = place("ktd", RS + 4 * TB, [TILES, 256])
    fcum = place("fcum", RS + 6 * TB, [T])
    mrun = place("mrun", RS + 7 * TB, [T])
    arow = place("arow", RU, [T])
    r1 = place("r1", RU + TB, [T])
    r2 = place("r2", RU + 2 * TB, [T])
    o = RU + 3 * TB
    wb = [place(f"wb{b}", o + b * 4096, [2, 4, P]) for b in range(2)]
    o += 8192
    vw = place("vw", o, [2, 4, 65])
    o += 2080
    t1 = place("t1", o, [2, 4, 65])
    t2 = place("t2", o + 2080, [2, 4, 65])
    hh = place("hh", o + 4160, [2, 4, 64])
    cst_d = place("cst_d", o + 6208, [2, 2, 2, 65])
    col = place("col", o + 8288, [TILES, 2, 4, 4])
    dd = place("dd", o + 9056, [2, 4])
    rd = place("rd", o + 9088, [2, 4])
    assert o + 9120 <= RU + 10 * TB
    sqy = place("sqy", RS, [TILES, 512])
    sig = place("sig", RS + 4 * TB, [TILES, 512])

    ps = nc.alloc_psum_tensor("ps", [P, 4096], F32)

    def bank(b, a=0, n=512):
        return ps[:, b * 512 + a:b * 512 + a + n]

    def pair(g, a=0, n=1024):
        return bank(2 * (g % 2), a, n)

    S = {}

    def sem(name):
        if name not in S:
            S[name] = nc.alloc_semaphore(name)
        return S[name]

    def cols(j, n=1):
        return slice(j * P, (j + n) * P)

    def bc(ap, n):
        return ap.unsqueeze(2).to_broadcast([ap.shape[0], ap.shape[1], n])

    def mod_after(l, s):
        if l == 0 and s < IN_SLOTS + OUT_SLOTS:
            return FIRST_MODS + s
        return None

    Q_MODS = MOD_SLOTS // QUARTERS
    N_W = DEPTH * LAYER_SLOTS

    def lvec(l, i, n=1):
        b = (V_L if l == 0 else 0) + i
        return vcol[l][:, b:b + n]

    def att_units(l):
        js = range(TILES) if l == 0 else range(LAT_TILES)
        return [(m, j, h) for m in range(2) for j in js for h in range(4)]

    def key_span(m, j):
        if j >= LAT_TILES:
            return 512, [4, 5], []
        if m == 0:
            return 0, [0, 1, 2, 3, 4, 5], []
        k0, k1 = max(0, j - 1), min(LAT_TILES - 1, j + 1)
        n = k1 - k0 + 1
        lo = 512 - n * P
        masks = []
        if j > 0:
            masks.append((m_left, lo))
        if j < LAT_TILES - 1:
            masks.append((m_right, 512 - P))
        return lo, list(range(k0, k1 + 1)) + [4, 5], masks

    def raw_of(w):
        return 0 if w < ONE_RAW else 1 - w % 2

    def landed(w):
        if w < ONE_RAW:
            return sem("w_landed0"), 16 * (w + 1)
        n = (w - ONE_RAW) // 2 + 1
        return (sem("w_landed1"), 16 * n) if raw_of(w) else (sem("w_landed0"), 16 * (ONE_RAW + n))

    def n_q(l):
        return T if l < DEPTH - 1 else SEQ

    def token_tiles(l, s, m):
        if l == DEPTH - 1 and s >= 10:
            return 2 * m, 2
        return ((0, 4), (4, 2))[m]

    def halves(l):
        return [(0, 3), (3, 3 if l == 0 else 1)]

    blk = nc.Block()
    with blk:
        @blk.sync
        def _(sp):
            sp.dma_start(vin[0:V_ALL, :], vecs[0:V_ALL, :]).then_inc(sem("c_landed"), 16)
            sp.dma_start(vin1[0:LV, :], vecs[V_ALL:V_ALL + LV, :]).then_inc(sem("c_landed"), 16)
            sp.dma_start(cst[:], consts[:, 0:C_KEEP]).then_inc(sem("c_landed"), 16)
            for j in range(TILES):
                src = x_in[cols(j), :] if j < LAT_TILES else ctx_in[cols(j - LAT_TILES), :]
                sp.dma_start(xin[j][:], src).then_inc(sem(f"x_landed{j}"), 16)
            mods = Tally()
            wts = Tally()

            def load_mod(idx):
                if mods.term is not None or mods.n > 0:
                    sp.wait_ge(sem("mod_summed"), mods.at(0))
                sp.dma_start(raw[1][:], idx).then_inc(sem("mod_landed"), 16)
                mods.add(2)

            def load_w(idx, w):
                if w == ONE_RAW:
                    sp.wait_ge(sem("mod_summed"), 2 * (DEPTH * MOD_SLOTS - FIRST_MODS))
                elif w > 0:
                    sp.wait_ge(sem("lo_ready"), wts.at(0 if w < ONE_RAW else -1))
                sp.dma_start(raw[raw_of(w)][:], idx).then_inc(landed(w)[0], 16)
                wts.add()

            def wslot(n):
                return w_big[n].rearrange("p (k m) -> p k m", k=KD)

            def mslot(n):
                return w_mod[n].rearrange("p (k m) -> p k m", k=KD)

            for j in range(FIRST_MODS):
                sp.dma_start(first_mod[j][:], mslot(j)).then_inc(sem(f"first_mod_landed{j}"), 16)
            sp.dma_start(cload[:], consts[:, C_KEEP:C_ALL]).then_inc(sem("masks_landed"), 16)
            load_w(wslot(0), 0)
            load_mod(mslot(FIRST_MODS))
            load_w(wslot(1), 1)
            for l in range(DEPTH):
                sp.dma_start(rowc[:], rows[l:l + 1, :].to_broadcast([P, rows.shape[1]])).then_inc(sem("lay_landed"), 16)
                sp.dma_start(wg[:], gla_gate[l]).then_inc(sem("lay_landed"), 16)
                w0 = l * LAYER_SLOTS
                for s in range(IN_SLOTS + OUT_SLOTS):
                    if mod_after(l, s) is not None and s > 0:
                        load_mod(mslot(mod_after(l, s)))
                    load_w(wslot(w0 + s + 2), w0 + s + 2)
                q0 = w0 + IN_SLOTS + OUT_SLOTS
                n_loop = QUARTERS if l < DEPTH - 1 else QUARTERS - 1
                mods_per = Q_MODS if l == 0 else 0
                with sp.Fori(0, n_loop) as i:
                    wts.enter(i, 8)
                    mods.enter(i, 2 * mods_per)
                    for s in range(QW1 + QW2):
                        if s < mods_per:
                            load_mod(w_mod[bass.ds(i * Q_MODS + (MOD_SLOTS + s), 1)]
                                     .rearrange("o p (k m) -> p (o k) m", k=KD))
                        load_w(w_big[bass.ds(i * 8 + (q0 + s + 2), 1)].rearrange("o p (k m) -> p (o k) m", k=KD),
                               q0 + s + 2)
                wts.leave(n_loop)
                mods.leave(n_loop)
                if l == DEPTH - 1:
                    for s in range(QW1 + QW2 - 2):
                        load_w(wslot(q0 + 8 * n_loop + s + 2), q0 + 8 * n_loop + s + 2)
                if l == 0:
                    sp.wait_ge(sem("x_done"), 8 * (1 + QUARTERS))
            for j in range(LAT_TILES):
                sp.wait_ge(sem("out_ready"), j + 1)
                sp.dma_start(out[cols(j), :], xout[j % 2][:]).then_inc(sem(f"out_stored{j % 2}"), 16)
            for r in range(2):
                sp.wait_ge(sem(f"out_stored{r}"), 16 * (LAT_TILES // 2))

        @blk.gpsimd
        def _(gp):
            def low(n, r, raw_r):
                gp.wait_ge(sem("hi_ready"), n)
                nc.gpsimd.tensor_tensor(w_lo[r][:], raw[raw_r][:], w_hi[r][:].bitcast(F32),
                                        ALU.subtract).then_inc(sem("lo_ready"), 1)
            with gp.Fori(0, ONE_RAW // 2) as i:
                low(i * 2 + 1, 0, 0)
                low(i * 2 + 2, 1, 0)
            with gp.Fori(0, (N_W - ONE_RAW) // 2) as i:
                low(i * 2 + (ONE_RAW + 1), 0, raw_of(ONE_RAW))
                low(i * 2 + (ONE_RAW + 2), 1, raw_of(ONE_RAW + 1))

        @blk.scalar
        def _(act):
            big = Tally()
            w_n = Tally()
            c = {}

            def T_(name):
                return c.setdefault(name, Tally())

            w_groups = []
            for l in range(DEPTH):
                for s in range(LAYER_SLOTS):
                    w_groups.append((w_groups[-1] if w_groups else 0) + (1 if s == 6 else 2))

            def split_hi(w, i=None, per=0):
                if w >= N_W:
                    return
                land, n = landed(w)
                if i is None:
                    act.wait_ge(land, n)
                    if w >= 2:
                        act.wait_ge(sem("big_done"), w_groups[w - 2])
                else:
                    act.wait_ge(land, i * (128 if w < ONE_RAW else 64) + n)
                    act.wait_ge(sem("big_done"), i * 16 + w_groups[w - 2])
                nc.scalar.activation(w_hi[w % 2][:], raw[raw_of(w)][:], ACT.Copy).then_inc(sem("hi_ready"), 1)

            stage_n = [0]

            def stage_end():
                act.drain().then_inc(sem("stage_done"), 1)
                stage_n[0] += 3
                act.wait_ge(sem("stage_done"), stage_n[0])

            own = Tally()

            def step(ins):
                ins.then_inc(sem("act_step"), 1)
                act.wait_ge(sem("act_step"), own.add())

            act.wait_ge(sem("v_cols"), 1)
            nc.scalar.activation(cs[:, :, 0], vcol[0][:, V_C:V_C + KD], ACT.Exp, scale=-1.0)
            nc.scalar.activation(cs[:, :, 1], vcol[0][:, V_CC:V_CC + KD], ACT.Exp,
                                 scale=-1.0).then_inc(sem("c_exp"), 1)
            for j in range(TILES):
                act.wait_ge(sem("x_trans"), j + 1)
                nc.scalar.activation(xT[:, :, cols(j)], pair(j).rearrange("p (k t) -> p k t", k=KD),
                                     ACT.Copy).then_inc(sem("x_in"), 1)

            def norm(l, which, n_t, x_total):
                parts = [(0, 0, SEQ)] + ([(1, SEQ, T)] if n_t == T else [])
                sqn, accn, hn = T_("sq"), T_("acc"), T_("h")
                t_n, hh_n = T_("t"), T_("h_hi")
                for k in range(KD):
                    act.wait_ge(sem("x_done"), x_total - KD + k + 1) if x_total else \
                        act.wait_ge(sem("x_in"), TILES)
                    if k >= 2:
                        act.wait_ge(sem("acc_added"), accn.n + max(1, k - 2))
                    nc.scalar.activation(tmp[k % 2][:, 0:n_t], xT[:, k, 0:n_t],
                                         ACT.Square).then_inc(sem("sq_ready"), 1)
                accn.add(KD - 1)
                act.wait_ge(sem("ms_ready"), T_("ms").add())
                step(nc.scalar.activation(tmp[3][:, 0:n_t], bank(4, 0, n_t), ACT.Ln, bias=eps[:, 0:1],
                                          scale=1.0 / D_MODEL))
                nc.scalar.activation(tmp[3][:, 0:n_t], tmp[3][:, 0:n_t], ACT.Exp,
                                     scale=-0.5).then_inc(sem("rstd_ready"), 1)
                if x_total == 0:
                    split_hi(0)
                sh = modt[l][:].rearrange("p (m c) -> p m c", c=2)
                m0 = 0 if which == 1 else 24
                for k in range(KD):
                    act.wait_ge(sem("t_ready"), t_n.add())
                    if k >= 2:
                        act.wait_ge(sem("h_ready"), hn.n + k - 1)
                    for c_i, a, b in parts:
                        ins = nc.scalar.activation(tmp[4 + k % 2][:, a:b], tmp[k % 2][:, a:b], ACT.Identity,
                                                   bias=sh[:, m0 + k, c_i:c_i + 1], scale=gs[:, k, c_i:c_i + 1])
                    ins.then_inc(sem("h_full"), 1)
                    act.wait_ge(sem("h_full"), hh_n.add())
                    nc.scalar.activation(h_hi[:, k, 0:n_t], tmp[4 + k % 2][:, 0:n_t],
                                         ACT.Copy).then_inc(sem("h_hi_ready"), 1)
                if x_total == 0:
                    split_hi(1)
                hn.add(KD)

            def in_proj(l):
                scale = {6: GLA_DK ** -0.5, 10: HD ** -0.5, 11: HD ** -0.5}
                for s in range(IN_SLOTS):
                    w = l * LAYER_SLOTS + s
                    for m in range(2):
                        g = 2 * s + m
                        if g < FEATS:
                            n = n_q(l) if g in Q_FEATS else T
                            act.wait_ge(sem("big_done"), big.add())
                            if g == 12:
                                ins = nc.scalar.activation(ft[g][:], pair(g, 0, T), ACT.Identity,
                                                           bias=lvec(l, LV_GB), scale=1.0)
                            else:
                                ins = nc.scalar.activation(ft[g][:, 0:n], pair(g, 0, n), ACT.Copy,
                                                           scale=scale.get(g, 1.0))
                            ins.then_inc(sem("ft_ready"), 1)
                        elif g > FEATS:
                            big.add()
                    split_hi(w + 2)

            def prep_ab(l):
                n_i = [n_q(l) if i in Q_FEATS else T for i in range(6)]
                for i, n in enumerate(n_i):
                    nc.scalar.activation(rab[:, i, 0:n], ft[i][:, 0:n], ACT.Square).then_inc(sem("sqab_ready"), 1)
                for i, n in enumerate(n_i):
                    act.wait_ge(sem("msab_ready"), T_("msab").add())
                    nc.scalar.activation(rab[:, i, 0:n], pair(i, 0, n), ACT.Ln, bias=eps[:, 0:1],
                                         scale=1.0 / HD).then_inc(sem("lnab_done"), 1)
                for i, n in enumerate(n_i):
                    act.wait_ge(sem("lnab_done"), T_("lnab").add())
                    nc.scalar.activation(rab[:, i, 0:n], rab[:, i, 0:n], ACT.Exp,
                                         scale=-0.5).then_inc(sem("rab_ready"), 1)

            def attention(l):
                units = att_units(l)
                n = len(units)
                e0, t0, p0 = T_("nb").n, T_("tr").n, T_("pv").n

                def evac(u):
                    _, j, _ = units[u]
                    m = units[u][0]
                    _, keys, _ = key_span(m, j)
                    act.wait_ge(sem("tr_done"), t0 + u + 1)
                    if u >= 2:
                        act.wait_ge(sem("pv_done"), p0 + u - 1)
                    nc.scalar.activation(probT[u % 2][:, 0:len(keys) * P], bank(4, 0, len(keys) * P),
                                         ACT.Copy).then_inc(sem("pt_ready"), 1)

                for u, (m, j, h) in enumerate(units):
                    lo, keys, _ = key_span(m, j)
                    jj = u // 4
                    act.wait_ge(sem("nb_ready"), e0 + u + 1)
                    if u >= 2:
                        act.wait_ge(sem("tr_done"), t0 + u - 1)
                    nc.scalar.activation(prob[u % 2][:, 0:T - lo], pair(u, lo, T - lo), ACT.Exp,
                                         bias=nb[:, jj % 2, h:h + 1], scale=HD ** -0.5,
                                         accum_out=psum_e[:, jj % 2, h:h + 1]).then_inc(sem("exp_done"), 1)
                    if m == 1 and h == 3:
                        nc.scalar.activation(es[:, jj % 2, :], se[:, jj % 2, :],
                                             ACT.Exp).then_inc(sem("es_ready"), 1)
                    if u >= 1:
                        evac(u - 1)
                evac(n - 1)
                T_("nb").add(n), T_("tr").add(n), T_("pv").add(n)

            def gla(l):
                for d in range(2):
                    act.wait_ge(sem("pre_done"), T_("pre").add())
                    nc.scalar.activation(pre[d][:], pair(d, 0, T), ACT.Identity, bias=lvec(l, LV_BG + d),
                                         scale=1.0).then_inc(sem("pre_ready"), 1)
                act.wait_ge(sem("abs_ready"), T_("abs").add(3))
                step(nc.scalar.activation(ls[:], ls[:], ACT.Exp))
                nc.scalar.activation(ls[:], ls[:], ACT.Ln, bias=1.0).then_inc(sem("softplus_ready"), 1)
                act.wait_ge(sem("ex_raw"), T_("exr").add())
                nc.scalar.activation(ex[:], ex[:], ACT.Exp, scale=1.0 / GLA_TAU).then_inc(sem("ex_ready"), 1)
                nc.scalar.activation(dex[:], dex[:], ACT.Exp, scale=1.0 / GLA_TAU).then_inc(sem("ex_ready"), 1)
                for d in range(2):
                    act.wait_ge(sem("kt_done"), T_("kt").add())
                    nc.scalar.activation(ktc[d][:], pair(d, 0, T), ACT.Copy).then_inc(sem("ktc_ready"), 1)
                act.wait_ge(sem("kdec_ready"), T_("kdec").add(2))
                for d in range(2):
                    nc.scalar.activation(ex[:, d, :], bb[d][:], ACT.Exp,
                                         scale=1.0 / GLA_TAU).then_inc(sem("ex_ready"), 1)
                for hf, (j0, nt) in enumerate(halves(l)):
                    for li in range(len(LEVELS)):
                        b = (hf * 8 + li + 1) % 2
                        act.wait_ge(sem("e_raw"), T_("er").add())
                        nc.scalar.activation(eqk[b][:, :, 0:nt * P], eqk[b][:, :, 0:nt * P], ACT.Exp,
                                             scale=1.0 / GLA_TAU).then_inc(sem("e_ready"), 1)
                    for t in range(nt):
                        act.wait_ge(sem("oc_done"), T_("oc").add())
                        nc.scalar.activation(y[:, j0 + t, 512:768], bank(4 + (j0 + t) % 2, 0, 256),
                                             ACT.Copy).then_inc(sem("yc_ready"), 1)

            def mlstm(l):
                act.wait_ge(sem("qdb_zero"), T_("qz").add())
                for p_ in range(2):
                    for hf in range(2):
                        rr = slice(64 * hf, 64 * hf + 64)
                        nc.scalar.activation(qdb[rr, 2 * p_ + hf, 0:n_q(l)], ft[8 + p_][rr, 0:n_q(l)],
                                             ACT.Copy).then_inc(sem("qdb_ready"), 1)
                for a, n in ((0, 4), (4, 2)):
                    act.wait_ge(sem("kd_done"), T_("kd").add())
                    nc.scalar.activation(ktd[:, a:a + n, :], pair(a // 4, 0, n * 256).rearrange(
                        "p (j c) -> p j c", j=n), ACT.Copy).then_inc(sem("ktd_ready"), 1)
                act.wait_ge(sem("r_raw"), T_("rr").add())
                nc.scalar.activation(r1[64:128, :], r1[64:128, :], ACT.Exp).then_inc(sem("r_ready"), 1)
                nc.scalar.activation(r2[:], r2[:], ACT.Exp).then_inc(sem("r_ready"), 1)
                nc.scalar.activation(dec[:], dec[:], ACT.Exp).then_inc(sem("r_ready"), 1)
                act.wait_ge(sem("col_ready"), T_("col").add())
                k = 0
                for s in range(TILES):
                    for d in range(2):
                        j = ORDER[d][s]
                        if l == DEPTH - 1 and j >= LAT_TILES:
                            continue
                        act.wait_ge(sem("mb_done"), T_("mb").add())
                        if k >= 4:
                            act.wait_ge(sem("num_done"), T_("num").n + k - 3)
                        for h in range(4):
                            ins = nc.scalar.activation(wb[s % 2][:, d, h, :], bank(d, h * P, P), ACT.Exp,
                                                       bias=col[:, j, 0, d, h:h + 1], scale=-1.0)
                        ins.then_inc(sem("w_ready"), 1)
                        k += 1
                T_("num").add(k)

            def finish(l):
                nj = TILES if l == 0 else LAT_TILES
                nc.scalar.activation(sqy[:, 0:nj, :], y[:, 0:nj, 512:1024], ACT.Square).then_inc(sem("sqy_ready"), 1)
                nc.scalar.activation(sig[:, 0:nj, :], ro[:, 0:nj, :], ACT.Exp, scale=-1.0).then_inc(sem("sig_raw"), 1)
                act.wait_ge(sem("ms8_ready"), T_("ms8").add())
                step(nc.scalar.activation(ms8[:, 0:nj * 8], ms8[:, 0:nj * 8], ACT.Ln, bias=eps[:, 0:1],
                                          scale=1.0 / HD))
                nc.scalar.activation(ms8[:, 0:nj * 8], ms8[:, 0:nj * 8], ACT.Exp,
                                     scale=-0.5).then_inc(sem("rstd8_ready"), 1)
                for j in range(nj):
                    act.wait_ge(sem("yt_done"), T_("yt").add())
                    nc.scalar.activation(yT_hi[:, :, cols(j)], pair(j).rearrange("p (k t) -> p k t", k=KD),
                                         ACT.Copy).then_inc(sem("yt_hi"), 1)

            def mlp_quarter(l, n_t, w0, i, last):
                def hid_high(m):
                    act.wait_ge(sem("sq2_ready"), T_("sq2").add())
                    nc.scalar.activation(hid_hi[:, m, 0:n_t], tmp[2 + m % 2][:, 0:n_t],
                                         ACT.Copy).then_inc(sem("hid_hi_ready"), 1)
                for s in range(QW1 + QW2):
                    for m in range(2):
                        g = 2 * s + m
                        big.add()
                        if s < QW1:
                            act.wait_ge(sem("big_done"), big.at(0))
                            if g >= 2:
                                act.wait_ge(sem("sq2_ready"), T_("sq2").at(0))
                            nc.scalar.activation(tmp[6 + g % 2][:, 0:n_t], pair(g, 0, n_t),
                                                 ACT.Relu).then_inc(sem("relu_done"), 1)
                            if g >= 1:
                                hid_high(g - 1)
                    if s == QW1 - 1:
                        hid_high(2 * QW1 - 1)
                    if not (last and s >= QW1 + QW2 - 2):
                        split_hi(w0 + s + 2, i)

            x_total = 0
            for l in range(DEPTH):
                n_t = T if l == 0 else SEQ
                w0 = l * LAYER_SLOTS
                norm(l, 1, T, x_total)
                in_proj(l)
                stage_end()
                prep_ab(l)
                attention(l)
                stage_end()
                gla(l)
                stage_end()
                mlstm(l)
                stage_end()
                finish(l)
                for s in range(OUT_SLOTS):
                    big.add(2)
                    split_hi(w0 + IN_SLOTS + s + 2)
                x_total += KD
                norm(l, 2, n_t, x_total)
                n_loop = QUARTERS if l < DEPTH - 1 else QUARTERS - 1
                q0 = w0 + IN_SLOTS + OUT_SLOTS
                with act.Fori(0, n_loop) as i:
                    big.enter(i, 16)
                    T_("sq2").enter(i, 8)
                    mlp_quarter(l, n_t, q0, i, False)
                big.leave(n_loop)
                T_("sq2").leave(n_loop)
                if l == DEPTH - 1:
                    mlp_quarter(l, n_t, q0 + 8 * n_loop, None, True)
                x_total += KD * QUARTERS

        @blk.vector
        def _(dve):
            c = {}

            def T_(name):
                return c.setdefault(name, Tally())

            big = Tally()
            own = Tally()

            def step(ins):
                ins.then_inc(sem("dve_step"), 1)
                dve.wait_ge(sem("dve_step"), own.add())

            stage_n = [0]

            def stage_end():
                dve.drain().then_inc(sem("stage_done"), 1)
                stage_n[0] += 3
                dve.wait_ge(sem("stage_done"), stage_n[0])

            v = nc.vector

            v.memset(ones[:], 1.0)
            v.memset(eps[:], EPS).then_inc(sem("ones_ready"), 1)
            dve.wait_ge(sem("v_trans"), 1)
            v.tensor_copy(vcol[1][:], bank(7, P, LV))
            v.tensor_copy(vcol[0][:], bank(7, 0, V_ALL)).then_inc(sem("v_cols"), 1)
            dve.wait_ge(sem("v_cols"), 1)
            dve.wait_ge(sem("c_exp"), 1)
            step(v.tensor_scalar(cs[:], cs[:], 1.0, None, ALU.add))
            step(v.reciprocal(cs[:], cs[:]))
            v.tensor_tensor(cs[:, :, 0], cs[:, :, 0], vcol[0][:, V_C:V_C + KD], ALU.mult)
            v.tensor_tensor(cs[:, :, 1], cs[:, :, 1], vcol[0][:, V_CC:V_CC + KD], ALU.mult).then_inc(sem("cs_ready"), 1)

            def make_masks():
                dve.wait_ge(sem("masks_landed"), 16)
                dve.wait_ge(sem("c_landed"), 48)
                v.tensor_copy(lmask[:], cload[:, 0:8 * P].rearrange("p (a b) -> p a b", a=8))
                v.tensor_copy(ident_b[:], ident)
                v.tensor_scalar(m_left[:], cload[:, C_LEFT - C_KEEP:C_LEFT - C_KEEP + P], -BIG, None, ALU.mult)
                v.tensor_scalar(m_right[:], cload[:, C_RIGHT - C_KEEP:C_RIGHT - C_KEEP + P], -BIG, None, ALU.mult)
                v.tensor_scalar(p_after[:], cload[:, C_LEFT - C_KEEP:C_LEFT - C_KEEP + P], BIG, None, ALU.mult)
                v.tensor_scalar(p_before[:], cload[:, C_RIGHT - C_KEEP:C_RIGHT - C_KEEP + P], BIG, None,
                                ALU.mult).then_inc(sem("masks_ready"), 1)

            mod_n = Tally()
            sum_n = Tally()

            def mod_out(l, s, i=None):
                dve.wait_ge(sem("mod_used"), mod_n.at(FIRST_MODS + 1))
                mod_n.add()
                if i is None:
                    a, b = modt[l][:, 4 * s:4 * s + 4], lvec(l, LV_BMOD + 2 * s, 2)
                else:
                    a = modt[l][:, bass.ds(i * (4 * Q_MODS) + 4 * s, 4)]
                    b = vcol[l][:, bass.ds(i * (2 * Q_MODS) + (LV_BMOD + 2 * s), 2)]
                v.tensor_tensor(a.rearrange("p (m c) -> p m c", c=2), bank(6, 0, 4).rearrange("p (m c) -> p m c", c=2),
                                bc(b, 2), ALU.add).then_inc(sem("mod_out"), 1)

            def mod_sum(half):
                if half == 0:
                    dve.wait_ge(sem("mod_landed"), sum_n.at(1) * 16)
                    dve.wait_ge(sem("mod_used"), sum_n.at(FIRST_MODS))
                for k in range(4 * half, 4 * half + 4):
                    for c_i in range(2):
                        if k == 0:
                            ins = v.tensor_scalar(mod_acc[:, c_i, :], raw[1][:, k, :], cs[:, k, c_i:c_i + 1], None,
                                                  ALU.mult)
                        else:
                            dve.wait_ge(sem("dve_step"), own.at(0 if (k, c_i) == (KD - 1, 1) else -1))
                            ins = v.scalar_tensor_tensor(mod_acc[:, c_i, :], raw[1][:, k, :], cs[:, k, c_i:c_i + 1],
                                                         mod_acc[:, c_i, :], ALU.mult, ALU.add)
                        if k < KD - 1:
                            ins.then_inc(sem("dve_step"), 1)
                            own.add()
                        else:
                            ins.then_inc(sem("mod_summed"), 1)
                if half == 1:
                    sum_n.add()

            def norm(l, which, n_t):
                sqn = T_("sq")
                mt = modt[l][:].rearrange("p (m c) -> p m c", c=2)
                m0 = 8 if which == 1 else 32
                for k in range(1, KD):
                    dve.wait_ge(sem("sq_ready"), sqn.n + k + 1)
                    if k >= 2:
                        dve.wait_ge(sem("acc_added"), T_("acc").n + k - 1)
                    v.tensor_tensor(tmp[2][:, 0:n_t], tmp[0][:, 0:n_t] if k == 1 else tmp[2][:, 0:n_t],
                                    tmp[k % 2][:, 0:n_t], ALU.add).then_inc(sem("acc_added"), 1)
                sqn.add(KD)
                T_("acc").add(KD - 1)
                if l == 0 and which == 1:
                    for r in range(2):
                        dve.wait_ge(sem("mod_used"), FIRST_MODS // 2 * (r + 1))
                        v.tensor_copy(mod_rows[0:2, r * 1024:(r + 1) * 1024],
                                      ps[0:2, r * 1024:(r + 1) * 1024]).then_inc(sem("mod_rows_ready"), 1)
                    dve.wait_ge(sem("mod_cols"), 1)
                    v.tensor_tensor(modt[0][:, 0:4 * FIRST_MODS].rearrange("p (m c) -> p m c", c=2),
                                    bank(6, 0, 4 * FIRST_MODS).rearrange("p (m c) -> p m c", c=2),
                                    bc(lvec(0, LV_BMOD, 2 * FIRST_MODS), 2), ALU.add).then_inc(sem("mod_out"), 1)
                dve.wait_ge(sem("mod_out"), mod_n.at(1))
                step(v.scalar_tensor_tensor(gs[:], mt[:, m0:m0 + KD, :], 1.0,
                                            bc(lvec(l, LV_G1 if which == 1 else LV_G2, KD), 2), ALU.add, ALU.mult))
                dve.wait_ge(sem("rstd_ready"), T_("rstd").add())

                def low(k):
                    dve.wait_ge(sem("h_hi_ready"), T_("hhi").add())
                    v.tensor_tensor(h_lo[:, k, 0:n_t], tmp[4 + k % 2][:, 0:n_t], h_hi[:, k, 0:n_t].bitcast(F32),
                                    ALU.subtract).then_inc(sem("h_ready"), 1)
                for k in range(KD):
                    if k >= 2:
                        dve.wait_ge(sem("h_full"), T_("hf").n + k - 1)
                    v.tensor_tensor(tmp[k % 2][:, 0:n_t], xT[:, k, 0:n_t], tmp[3][:, 0:n_t],
                                    ALU.mult).then_inc(sem("t_ready"), 1)
                    if k == 0 and l == 0 and which == 1:
                        make_masks()
                    if k >= 1:
                        low(k - 1)
                low(KD - 1)
                T_("hf").add(KD)

            def in_proj(l):
                for s in range(IN_SLOTS):
                    has_mod = mod_after(l, s) is not None
                    for m in range(2):
                        g = 2 * s + m
                        if has_mod:
                            mod_sum(m)
                        if g == FEATS:
                            continue
                        big.add()
                        if g < FEATS:
                            continue
                        dve.wait_ge(sem("big_done"), big.at(0))
                        j0, n = token_tiles(l, s, m)
                        src = pair(g, 0, n * 256).rearrange("p (j c) -> p j c", j=n)
                        if s == 7:
                            dst = v_ab[:, j0:j0 + n, :]
                        elif s == 8:
                            dst = vc[:, j0:j0 + n, :]
                        elif s == 9:
                            dst = vd1[:, j0:j0 + n, :, 0:64]
                            src = pair(g, 0, n * 256).rearrange("p (j h c) -> p j h c", j=n, h=4)
                        else:
                            dst = ro[:, j0:j0 + n, (s - 10) * 256:(s - 9) * 256]
                        v.tensor_copy(dst, src).then_inc(sem("vt_ready"), 1)
                    if has_mod:
                        mod_out(0, mod_after(l, s))
                v.memset(vd1[:, :, :, 64:65], 1.0)

            def prep_ab(l):
                dve.wait_ge(sem("lay_landed"), 32 * (l + 1))
                v.tensor_scalar(nsink[:], rowc[:, 0:4], -1.0, None, ALU.mult)
                for i in range(6):
                    gi = LV_GQK + (0, 0, 1, 2, 2, 3)[i]
                    if i >= 1:
                        dve.wait_ge(sem("rot_done"), T_("rot").n + i)
                    v.tensor_scalar(gswap[:], swap, lvec(l, gi), None, ALU.mult).then_inc(sem("gswap_ready"), 1)
                T_("rot").add(6)
                dve.wait_ge(sem("rot_done"), T_("rot").n)
                lat, ctx_ = slice(0, SEQ), slice(SEQ, T)
                for i in range(6):
                    g = lvec(l, LV_GQK + (0, 0, 1, 2, 2, 3)[i])
                    rot = bank(4 + i % 4) if i < 4 else bank(i - 4)
                    step(v.scalar_tensor_tensor(rt[0][:], ft[i][:, lat], g, cos, ALU.mult, ALU.mult))
                    step(v.tensor_tensor(rt[1][:], rot, sin, ALU.mult))
                    step(v.tensor_tensor(rt[0][:], rt[0][:], rt[1][:], ALU.add))
                    dve.wait_ge(sem("rab_ready"), T_("rab").add())
                    if i in (2, 5):
                        k1 = kb1[i // 3]
                        a, b = slice(0, 64), slice(64, 128)
                        v.memset(k1[a, :], 0.0)
                        v.tensor_tensor(k1[b, lat], rt[0][b, :], rab[b, i, lat], ALU.mult)
                        step(v.scalar_tensor_tensor(k1[b, ctx_], ft[i][b, ctx_], g[b, :], rab[b, i, ctx_],
                                                    ALU.mult, ALU.mult))
                        v.tensor_tensor(ft[i][a, lat], rt[0][a, :], rab[a, i, lat], ALU.mult)
                        v.scalar_tensor_tensor(ft[i][a, ctx_], ft[i][a, ctx_], g[a, :], rab[a, i, ctx_],
                                               ALU.mult, ALU.mult)
                        v.memset(ft[i][b, :], 0.0).then_inc(sem("qk_ready"), 1)
                    else:
                        ins = v.tensor_tensor(ft[i][:, lat], rt[0][:], rab[:, i, lat], ALU.mult)
                        if n_q(l) == T:
                            ins = v.scalar_tensor_tensor(ft[i][:, ctx_], ft[i][:, ctx_], g, rab[:, i, ctx_],
                                                         ALU.mult, ALU.mult)
                        ins.then_inc(sem("qk_ready"), 1)
                    dve.wait_ge(sem("qk_ready"), T_("qk").add())

            def attention(l):
                units = att_units(l)
                s0, p0 = T_("sc").n, T_("pv").n
                e0 = T_("exp").n

                def tile_out(jj):
                    m, j, _ = units[4 * jj]
                    jp = jj % 2
                    dve.wait_ge(sem("pv_done"), p0 + 4 * jj + 4)
                    dve.wait_ge(sem("exp_done"), e0 + 4 * jj + 4)
                    if m == 1:
                        dve.wait_ge(sem("es_ready"), T_("es").add())
                        step(v.tensor_tensor(psum_e[:, jp, :], psum_e[:, jp, :], es[:, jp, :], ALU.add))
                    step(v.reciprocal(rs[:, jp, :], psum_e[:, jp, :]))
                    v.tensor_tensor(y[:, j, m * 256:m * 256 + 256].rearrange("p (h c) -> p h c", h=4),
                                    bank(6 + jp, 0, 256).rearrange("p (h c) -> p h c", h=4),
                                    bc(rs[:, jp, :], 64), ALU.mult).then_inc(sem("yab_ready"), 1)

                for u, (m, j, h) in enumerate(units):
                    lo, keys, _ = key_span(m, j)
                    jp = u // 4 % 2
                    dve.wait_ge(sem("sc_done"), s0 + u + 1)
                    step(v.tensor_reduce(mx[:, u % 2:u % 2 + 1], pair(u, lo, T - lo), AX_X, ALU.max))
                    if m == 0:
                        v.tensor_scalar(nb[:, jp, h:h + 1], mx[:, u % 2:u % 2 + 1], -HD ** -0.5, None,
                                        ALU.mult).then_inc(sem("nb_ready"), 1)
                    else:
                        step(v.tensor_scalar(nb[:, jp, h:h + 1], mx[:, u % 2:u % 2 + 1], -HD ** -0.5,
                                             nsink[:, h:h + 1], ALU.mult, ALU.min))
                        v.tensor_tensor(se[:, jp, h:h + 1], nb[:, jp, h:h + 1], rowc[:, h:h + 1],
                                        ALU.add).then_inc(sem("nb_ready"), 1)
                    if h == 2 and u >= 4:
                        tile_out(u // 4 - 1)
                tile_out(len(units) // 4 - 1)
                T_("sc").add(len(units)), T_("pv").add(len(units)), T_("exp").add(len(units))

            def gla(l):
                qc, kc, gates = ft[6], ft[7], ft[12]
                for d in range(2):
                    dve.wait_ge(sem("pre_ready"), T_("pre").add())
                    v.scalar_tensor_tensor(ls[:, d, :], pre[d][:], -1.0, pre[d][:], ALU.mult,
                                           ALU.min).then_inc(sem("abs_ready"), 1)
                v.scalar_tensor_tensor(ls[:, 2, :], gates[:], -1.0, gates[:], ALU.mult,
                                       ALU.min).then_inc(sem("abs_ready"), 1)
                v.memset(snap[:, 0, ORDER[0][0], :], 0.0)
                v.memset(snap[:, 1, ORDER[1][0], :], 0.0)
                dve.wait_ge(sem("softplus_ready"), T_("sp").add())
                for d in range(2):
                    step(v.scalar_tensor_tensor(pre[d][:], pre[d][:], 0.0, ls[:, d, :], ALU.min, ALU.subtract))
                step(v.scalar_tensor_tensor(gates[64:128, :], gates[64:128, :], 0.0, ls[64:128, 2, :],
                                            ALU.min, ALU.subtract))
                one = ones[:, 0:1].to_broadcast([P, P])
                for j in range(TILES):
                    v.tensor_tensor_scan(bb[0][:, cols(j)], one, pre[0][:, cols(j)], 0.0, ALU.mult, ALU.add)
                    last = v.tensor_tensor_scan(bb[1][:, cols(j)][:, ::-1], one, pre[1][:, cols(j)][:, ::-1], 0.0,
                                                ALU.mult, ALU.add)
                step(last)
                ends = [bb[0][:].rearrange("p (j t) -> p j t", t=P)[:, :, P - 1],
                        bb[1][:].rearrange("p (j t) -> p j t", t=P)[:, :, 0]]
                for d in range(2):
                    v.tensor_copy(dex[:, d, :], ends[d])
                    last = v.tensor_tensor(ex[:, d, :].rearrange("p (j t) -> p j t", t=P), bc(ends[d], P),
                                           bb[d][:].rearrange("p (j t) -> p j t", t=P), ALU.subtract)
                last.then_inc(sem("ex_raw"), 1)
                dve.wait_ge(sem("ex_ready"), T_("ex").add(2))
                for d in range(2):
                    v.tensor_tensor(kdec[d][:], kc[:], ex[:, d, :], ALU.mult).then_inc(sem("kdec_ready"), 1)
                for s in range(TILES - 1):
                    dve.wait_ge(sem("u_done"), T_("u").add())
                    step(v.tensor_tensor(umask[:].rearrange("p d (h c) -> p (d h) c", c=64),
                                         bank(4 + s % 2).rearrange("p (h c) -> p h c", c=64), bc(hm8, 64), ALU.mult))
                    for d in range(2):
                        a, b = ORDER[d][s], ORDER[d][s + 1]
                        last = v.scalar_tensor_tensor(snap[:, d, b, :], snap[:, d, a, :], dex[:, d, a:a + 1],
                                                      umask[:, d, :], ALU.mult, ALU.add)
                    last.then_inc(sem("snap_ready"), 1)
                    dve.wait_ge(sem("snap_ready"), T_("snap").add())
                dve.wait_ge(sem("ex_ready"), T_("ex").add(2))
                for d in range(2):
                    v.tensor_tensor(qe[d][:, 0:n_q(l)], qc[:, 0:n_q(l)], ex[:, d, 0:n_q(l)], ALU.mult).then_inc(sem("qe_ready"), 1)
                dve.wait_ge(sem("qe_ready"), T_("qe").add(2))
                v.memset(qbd[0][:], 0.0)
                v.memset(qbd[1][:], 0.0)
                step(v.memset(sacc[:], 0.0))

                seq = [(hf, li, j0, nt) for hf, (j0, nt) in enumerate(halves(l)) for li in range(8)]

                def exponents(it):
                    hf, li, j0, nt = seq[it]
                    if li == 0:
                        return
                    h = LEVELS[li - 1]
                    b = it % 2
                    tok = slice(j0 * P, (j0 + nt) * P)
                    b0 = bb[0][:, tok].rearrange("p (n w h) -> p n w h", w=2, h=h)
                    b1 = bb[1][:, tok].rearrange("p (n w h) -> p n w h", w=2, h=h)
                    eq = eqk[b][:, 0, 0:nt * P].rearrange("p (n w h) -> p n w h", w=2, h=h)
                    ek = eqk[b][:, 1, 0:nt * P].rearrange("p (n w h) -> p n w h", w=2, h=h)
                    ref0, ref1 = bc(b0[:, :, 0, h - 1], h), bc(b1[:, :, 1, 0], h)
                    v.tensor_tensor(eq[:, :, 1, :], b0[:, :, 1, :], ref0, ALU.subtract)
                    v.tensor_tensor(eq[:, :, 0, :], b1[:, :, 0, :], ref1, ALU.subtract)
                    v.tensor_tensor(ek[:, :, 0, :], ref0, b0[:, :, 0, :], ALU.subtract)
                    v.tensor_tensor(ek[:, :, 1, :], ref1, b1[:, :, 1, :], ALU.subtract).then_inc(sem("e_raw"), 1)

                def factors(it):
                    hf, li, j0, nt = seq[it]
                    b = it % 2
                    tok = slice(j0 * P, (j0 + nt) * P)
                    if it >= 2:
                        done = sum(q[3] for q in seq[:it - 1])
                        dve.wait_ge(sem("lev_done"), T_("lev").n + done)
                    if li > 0:
                        dve.wait_ge(sem("e_ready"), T_("er").add())
                        v.tensor_tensor(kl[b][:, 0:nt * P], kc[:, tok], eqk[b][:, 1, 0:nt * P], ALU.mult)
                    for h in range(4):
                        r = slice(32 * h, 32 * h + 32)
                        src = qc[r, tok].rearrange("p (j t) -> p j t", t=P)
                        if li > 0:
                            last = v.tensor_tensor(qbd[b][r, 0:nt, h, :], src,
                                                   eqk[b][r, 0, 0:nt * P].rearrange("p (j t) -> p j t", t=P), ALU.mult)
                        else:
                            last = v.tensor_scalar(qbd[b][r, 0:nt, h, :], src, 2.0, None, ALU.mult)
                    last.then_inc(sem("lev_factors"), 1)
                    dve.wait_ge(sem("lev_factors"), T_("lf").add())

                def merge(it):
                    hf, li, j0, nt = seq[it]
                    if li == 0 and hf == 1:
                        dve.wait_ge(sem("oc_done"), T_("oc").n + 3)
                    if it >= 1:
                        dve.wait_ge(sem("lev_merged"), T_("mm").n)
                    for t in range(nt):
                        k = T_("mm").n
                        dve.wait_ge(sem("lev_done"), T_("lev").n + T_("mm").add() - T_("mm0").n)
                        v.copy_predicated(sacc[:, t], lmask[:, li, :].unsqueeze(1).to_broadcast([P, 4, P]),
                                          bank(k % 4).rearrange("p (h t) -> p h t", h=4)).then_inc(sem("lev_merged"), 1)

                T_("mm0").n = T_("mm").n
                exponents(0)
                for it in range(len(seq)):
                    if it + 1 < len(seq):
                        exponents(it + 1)
                    factors(it)
                    if it >= 1:
                        merge(it - 1)
                merge(len(seq) - 1)
                n_mm = sum(q[3] for q in seq)
                T_("lev").add(n_mm)
                T_("oc").add(sum(nt for _, nt in halves(l)))

            def mlstm(l):
                gates = ft[12]
                v.memset(qdb[:], 0.0).then_inc(sem("qdb_zero"), 1)
                v.memset(cst_d[:], 0.0)
                v.memset(mrun[:], 0.0)
                v.memset(r1[:], 0.0)
                v.memset(r2[:], 0.0)
                v.memset(mp[:], 0.0)
                v.memset(mend[:], 0.0)
                v.memset(dec[:], 0.0)
                step(v.memset(fcum[:], 0.0))
                one = ones[64:68, 0:1].to_broadcast([4, P])
                one1 = ones[96:100, 0:1].to_broadcast([4, P])
                for j in range(TILES):
                    v.tensor_tensor_scan(fcum[0:4, cols(j)], one, gates[64:68, cols(j)], 0.0, ALU.mult, ALU.add)
                    last = v.tensor_tensor_scan(fcum[32:36, cols(j)][:, ::-1], one1, gates[96:100, cols(j)][:, ::-1],
                                                0.0, ALU.mult, ALU.add)
                step(last)
                R = slice(0, 36)
                step(v.tensor_tensor(arow[R, :], gates[R, :], fcum[R, :], ALU.subtract))
                for s in range(TILES):
                    for d in range(2):
                        j = ORDER[d][s]
                        r = slice(32 * d, 32 * d + 4)
                        a_, m_ = arow[r, cols(j)], mrun[r, cols(j)]
                        if d == 1:
                            a_, m_ = a_[:, ::-1], m_[:, ::-1]
                        last = v.tensor_tensor_scan(m_, a_, a_, mp[r, j:j + 1], ALU.max, ALU.max)
                    step(last)
                    if s < TILES - 1:
                        for d in range(2):
                            j, jn = ORDER[d][s], ORDER[d][s + 1]
                            r = slice(32 * d, 32 * d + 4)
                            e = j * P + (P - 1 if d == 0 else 0)
                            last = v.tensor_tensor(mp[r, jn:jn + 1], fcum[r, e:e + 1], mrun[r, e:e + 1], ALU.add)
                        step(last)
                mr = mrun[:].rearrange("p (j t) -> p j t", t=P)
                v.tensor_copy(mend[0:4, :], mr[0:4, :, P - 1])
                step(v.tensor_copy(mend[32:36, :], mr[32:36, :, 0]))

                def tt(ap):
                    return ap.rearrange("p (j t) -> p j t", t=P)
                v.tensor_copy(r1[R, :], arow[R, :])
                v.tensor_tensor(tt(r1[64:100, :]), tt(arow[R, :]), bc(mend[R, :], P), ALU.subtract)
                v.tensor_tensor(tt(r2[R, :]), bc(mp[R, :], P), tt(mrun[R, :]), ALU.subtract)
                v.scalar_tensor_tensor(r2[64:100, :], fcum[R, :], -1.0, mrun[R, :], ALU.mult, ALU.subtract)
                v.tensor_tensor(dec[R, :], mp[R, :], mend[R, :], ALU.subtract).then_inc(sem("r_raw"), 1)
                for q in range(2):
                    dve.wait_ge(sem("r_trans"), T_("rtr").add())
                    last = v.tensor_copy(col[:, :, q, :, :], pair(q, 0, T).rearrange(
                        "p (j a b) -> p j a b", j=TILES, a=4)[:, :, :, 0:4])
                last.then_inc(sem("col_ready"), 1)
                dve.wait_ge(sem("dec_done"), T_("decd").add())
                v.tensor_copy(dcb[:], bank(4, 0, 24).rearrange("p (a j) -> p a j", a=4)).then_inc(sem("dcb_ready"), 1)
                dve.wait_ge(sem("dcb_ready"), T_("dcb").add())
                dve.wait_ge(sem("col_ready"), T_("col").add())
                seen = set()
                for s in range(TILES):
                    cur_, nxt = s % 2, (s + 1) % 2
                    for d in range(2):
                        j = ORDER[d][s]
                        if s < TILES - 1:
                            if s >= 1:
                                dve.wait_ge(sem("ud_done"), T_("udv").add())
                            v.tensor_tensor(vw[:, d], vd1[:, j], bc(col[:, j, 0, 2 + d, :], 65),
                                            ALU.mult).then_inc(sem("vw_ready"), 1)
                    if s == TILES - 1:
                        T_("udv").add(2)
                    outs = [d for d in range(2) if not (l == DEPTH - 1 and ORDER[d][s] >= LAT_TILES)]
                    for d in outs:
                        dve.wait_ge(sem("w_ready"), T_("w").add())
                        dve.wait_ge(sem("qk_done"), T_("qkd").add())
                        v.tensor_tensor(wb[s % 2][:, d], wb[s % 2][:, d],
                                        bank(2 + d).rearrange("p (h t) -> p h t", h=4),
                                        ALU.mult).then_inc(sem("p_ready"), 1)
                    for d in range(2):
                        j = ORDER[d][s]
                        if s < TILES - 1:
                            dve.wait_ge(sem("ud_done"), T_("ud").add())
                            for p_ in range(2):
                                last = v.scalar_tensor_tensor(
                                    cst_d[:, d, nxt, p_, :], cst_d[:, d, cur_, p_, :], dcb[:, 2 * d + p_, j:j + 1],
                                    bank(d, p_ * 65, 65), ALU.mult, ALU.add)
                            last.then_inc(sem("state_ready"), 1)
                            dve.wait_ge(sem("state_ready"), T_("st").add())
                    for d in outs:
                        j = ORDER[d][s]
                        dve.wait_ge(sem("num_done"), T_("num").add())
                        inter = bank(6 + d, 0, 260).rearrange("p (h c) -> p h c", h=4)
                        intra = bank(4 + d, 0, 260).rearrange("p (h c) -> p h c", h=4)
                        step(v.tensor_tensor(t1[:, d], inter, bc(col[:, j, 1, d, :], 65), ALU.mult))
                        step(v.tensor_tensor(t2[:, d], t1[:, d], intra, ALU.add))
                        step(v.scalar_tensor_tensor(dd[:, d, :], t2[:, d, :, 64], -1.0, t2[:, d, :, 64],
                                                    ALU.mult, ALU.max))
                        step(v.tensor_tensor(dd[:, d, :], dd[:, d, :], col[:, j, 1, 2 + d, :], ALU.max))
                        step(v.reciprocal(rd[:, d, :], dd[:, d, :]))
                        dst = y[:, j, 768:1024].rearrange("p (h c) -> p h c", h=4)
                        if j in seen:
                            step(v.tensor_tensor(hh[:, d], t2[:, d, :, 0:64], bc(rd[:, d, :], 64), ALU.mult))
                            v.tensor_tensor(dst, dst, hh[:, d], ALU.add).then_inc(sem("yd_ready"), 1)
                        else:
                            seen.add(j)
                            v.tensor_tensor(dst, t2[:, d, :, 0:64], bc(rd[:, d, :], 64),
                                            ALU.mult).then_inc(sem("yd_ready"), 1)
                        dve.wait_ge(sem("yd_ready"), T_("yd").add())

            def finish(l):
                nj = TILES if l == 0 else LAT_TILES
                dve.wait_ge(sem("sqy_ready"), T_("sqy").add())
                v.tensor_reduce(ms8[:, 0:nj * 8], sqy[:, 0:nj, :].rearrange("p j (h c) -> p (j h) c", c=64),
                                AX_X, ALU.add).then_inc(sem("ms8_ready"), 1)
                dve.wait_ge(sem("sig_raw"), T_("sigr").add())
                sg = sig[:, 0:nj, :]
                step(v.tensor_scalar(sg, sg, 1.0, None, ALU.add))
                step(v.reciprocal(sg, sg))
                step(v.tensor_tensor(sig[:, 0:nj, 0:256], sig[:, 0:nj, 0:256], ro[:, 0:nj, 0:256], ALU.mult))
                yg = y[:, 0:nj, 512:1024]
                step(v.tensor_tensor(sg, sg, rowc[:, 4:516].unsqueeze(1).to_broadcast([P, nj, 512]), ALU.mult))
                step(v.tensor_tensor(yg, yg, sg, ALU.mult))
                dve.wait_ge(sem("rstd8_ready"), T_("r8").add())
                for j in range(nj):
                    yj = y[:, j, 512:1024].rearrange("p (h c) -> p h c", c=64)
                    v.tensor_tensor(yj, yj, bc(ms8[:, 8 * j:8 * j + 8], 64), ALU.mult).then_inc(sem("y_ready"), 1)
                for j in range(nj):
                    dve.wait_ge(sem("yt_hi"), T_("yth").add())
                    v.tensor_tensor(yT_lo[:, :, cols(j)], pair(j).rearrange("p (k t) -> p k t", k=KD),
                                    yT_hi[:, :, cols(j)].bitcast(F32), ALU.subtract).then_inc(sem("yt_ready"), 1)

            def residual(l, n_t, k, ga):
                mt = modt[l][:].rearrange("p (m c) -> p m c", c=2)
                dve.wait_ge(sem("big_done"), big.add())
                v_ = T_("xd")
                for c_i, a, b in [(0, 0, SEQ)] + ([(1, SEQ, T)] if n_t == T else []):
                    ins = v.scalar_tensor_tensor(xT[:, k, a:b], pair(k, a, b - a), mt[:, ga + k, c_i:c_i + 1],
                                                 xT[:, k, a:b], ALU.mult, ALU.add)
                ins.then_inc(sem("x_done"), 1)
                v_.add()

            def mlp_quarter(l, n_t, i):
                def hid_low(m):
                    dve.wait_ge(sem("hid_hi_ready"), T_("hh2").add())
                    v.tensor_tensor(hid_lo[:, m, 0:n_t], tmp[2 + m % 2][:, 0:n_t],
                                    hid_hi[:, m, 0:n_t].bitcast(F32), ALU.subtract).then_inc(sem("hid_ready"), 1)
                dve.wait_ge(sem("x_done"), T_("xd").at(0))
                for s in range(QW1 + QW2):
                    has_mod = l == 0 and s < Q_MODS
                    for m in range(2):
                        g = 2 * s + m
                        if has_mod:
                            mod_sum(m)
                        if s < QW1:
                            big.add()
                            dve.wait_ge(sem("relu_done"), T_("relu").add())
                            if g >= 2:
                                dve.wait_ge(sem("hid_ready"), T_("hh2").at(0))
                            v.tensor_tensor(tmp[2 + g % 2][:, 0:n_t], tmp[6 + g % 2][:, 0:n_t],
                                            tmp[6 + g % 2][:, 0:n_t], ALU.mult).then_inc(sem("sq2_ready"), 1)
                            if g >= 1:
                                hid_low(g - 1)
                        else:
                            residual(l, n_t, g - 2 * QW1, 40)
                    if s == QW1 - 1:
                        hid_low(2 * QW1 - 1)
                    if has_mod:
                        mod_out(1, s, i)

            for l in range(DEPTH):
                n_t = T if l == 0 else SEQ
                norm(l, 1, T)
                in_proj(l)
                stage_end()
                prep_ab(l)
                attention(l)
                stage_end()
                gla(l)
                stage_end()
                mlstm(l)
                stage_end()
                finish(l)
                for s in range(OUT_SLOTS):
                    has_mod = mod_after(l, IN_SLOTS + s) is not None
                    for m in range(2):
                        if has_mod:
                            mod_sum(m)
                        if s == 0 and m == 0:
                            dve.wait_ge(sem("mod_out"), mod_n.at(1))
                        residual(l, n_t, 2 * s + m, 16)
                    if has_mod:
                        mod_out(0, mod_after(l, IN_SLOTS + s))
                norm(l, 2, n_t)
                n_loop = QUARTERS if l < DEPTH - 1 else QUARTERS - 1
                looped = [(big, 16), (T_("relu"), 8), (T_("hh2"), 8), (T_("xd"), 8),
                          (mod_n, Q_MODS if l == 0 else 0), (sum_n, Q_MODS if l == 0 else 0),
                          (own, Q_MODS * 2 * (KD - 1) if l == 0 else 0)]
                with dve.Fori(0, n_loop) as i:
                    for t, per in looped:
                        t.enter(i, per)
                    mlp_quarter(l, n_t, i)
                for t, per in looped:
                    t.leave(n_loop)
                if l == DEPTH - 1:
                    mlp_quarter(l, n_t, None)
            for j in range(LAT_TILES):
                dve.wait_ge(sem("out_trans"), j + 1)
                if j >= 2:
                    dve.wait_ge(sem(f"out_stored{j % 2}"), 16 * (j // 2))
                v.tensor_copy(xout[j % 2][:], pair(j)).then_inc(sem("out_ready"), 1)

        @blk.tensor
        def _(pe):
            c = {}

            def T_(name):
                return c.setdefault(name, Tally())

            mm = nc.tensor.matmul
            stage_n = [0]

            def stage_end():
                pe.drain().then_inc(sem("stage_done"), 1)
                stage_n[0] += 3
                pe.wait_ge(sem("stage_done"), stage_n[0])

            pe.wait_ge(sem("c_landed"), 48)
            nc.tensor.transpose(bank(7, P, LV), vin1[0:LV, :], ident[0:LV, 0:LV])
            nc.tensor.transpose(bank(7, 0, V_ALL), vin[0:V_ALL, :], ident[0:V_ALL, 0:V_ALL]).then_inc(sem("v_trans"), 1)

            for j in range(TILES):
                pe.wait_ge(sem(f"x_landed{j}"), 16)
                if j >= 2:
                    pe.wait_ge(sem("x_in"), j - 1)
                for k in range(KD):
                    ins = nc.tensor.transpose(pair(j, k * P, P), xin[j][:, k * P:(k + 1) * P], ident)
                ins.then_inc(sem("x_trans"), 1)

            mods, wts = Tally(), Tally()

            def first_mods(a, b):
                for j in range(a, b):
                    pe.wait_ge(sem(f"first_mod_landed{j}"), 16)
                    for k in range(KD):
                        ins = mm(ps[0:2, j * WC:(j + 1) * WC], cs[:, k, :], first_mod[j][:, k, :],
                                 start=(k == 0), stop=(k == KD - 1))
                    ins.then_inc(sem("mod_used"), 1)

            def first_mods_columns():
                pe.wait_ge(sem("mod_rows_ready"), 2)
                for m in range(2 * FIRST_MODS):
                    ins = nc.tensor.transpose(bank(6, 2 * m, 2), mod_rows[0:2, m * P:(m + 1) * P], ident[0:2, 0:2])
                ins.then_inc(sem("mod_cols"), 1)

            def mod_slot():
                pe.wait_ge(sem("mod_summed"), mods.add(2))
                pe.wait_ge(sem("mod_out"), mods_out.add())
                for m in range(2):
                    for c_i in range(2):
                        ins = mm(bank(6, 2 * m + c_i, 1), mod_acc[:, c_i, m * P:(m + 1) * P], ones[:, 0:1],
                                 start=True, stop=True)
                ins.then_inc(sem("mod_used"), 1)

            mods_out = Tally()

            def passes(r):
                return ((w_hi[r], 0), (w_hi[r], 1), (w_lo[r], 0))

            def feature_pair(g, r, mov, n_t, ready):
                spans = [(0, SEQ)] + ([(SEQ, T)] if n_t == T else [])
                for k in range(KD):
                    pe.wait_ge(ready[0], ready[1] + k + 1)
                    for m in range(2):
                        for q, (w, hl) in enumerate(passes(r)):
                            for a, b in spans:
                                ins = mm(pair(g + m, a, b - a), w[:, k, m * P:(m + 1) * P], mov[hl][:, k, a:b],
                                         start=(k == 0 and q == 0), stop=(k == KD - 1 and q == 2))
                        if k == KD - 1:
                            ins.then_inc(sem("big_done"), 1)

            def feature_group(g, r, m, mov, n_t, ready=None):
                spans = [(0, SEQ)] + ([(SEQ, T)] if n_t == T else [])
                for k in range(KD):
                    if ready is not None:
                        pe.wait_ge(ready[0], ready[1] + k + 1)
                    for q, (w, hl) in enumerate(passes(r)):
                        for a, b in spans:
                            ins = mm(pair(g, a, b - a), w[:, k, m * P:(m + 1) * P], mov[hl][:, k, a:b],
                                     start=(k == 0 and q == 0), stop=(k == KD - 1 and q == 2))
                ins.then_inc(sem("big_done"), 1)

            def norm_sum(n_t):
                pe.wait_ge(sem("acc_added"), T_("acc").add(KD - 1))
                ins = mm(bank(4), ones[:], tmp[2][:, 0:SEQ], start=True, stop=True)
                if n_t == T:
                    ins = mm(bank(5, 0, CTX), ones[:], tmp[2][:, SEQ:T], start=True, stop=True)
                ins.then_inc(sem("ms_ready"), 1)

            def in_proj(l):
                ft0, vt0, h0 = T_("ft").n, T_("vt").n, T_("h").n
                for s in range(IN_SLOTS):
                    r = wts.n % 2
                    pe.wait_ge(sem("lo_ready"), wts.add())
                    for m in range(2):
                        g = 2 * s + m
                        if g == FEATS:
                            continue
                        if 2 <= g <= FEATS + 1:
                            pe.wait_ge(sem("ft_ready"), ft0 + min(g - 1, FEATS))
                        elif g > FEATS + 1:
                            n = g - FEATS - 2
                            if n >= 1:
                                pe.wait_ge(sem("vt_ready"), vt0 + n)
                        if g == 0:
                            feature_pair(0, r, (h_hi, h_lo), n_q(l), (sem("h_ready"), h0))
                        elif g == 1:
                            continue
                        elif g < FEATS:
                            feature_group(g, r, m, (h_hi, h_lo), n_q(l) if g in Q_FEATS else T)
                        else:
                            j0, n = token_tiles(l, s, m)
                            for j in range(j0, j0 + n):
                                for k in range(KD):
                                    for q, (w, hl) in enumerate(passes(r)):
                                        ins = mm(pair(g, (j - j0) * 256, 256), (h_hi, h_lo)[hl][:, k, cols(j)],
                                                 w[:, k, :], start=(k == 0 and q == 0),
                                                 stop=(k == KD - 1 and q == 2))
                            ins.then_inc(sem("big_done"), 1)
                    if mod_after(l, s) is not None:
                        mod_slot()
                T_("ft").add(FEATS), T_("vt").add(10), T_("h").add(KD)

            def prep_ab(l):
                for i in range(6):
                    pe.wait_ge(sem("sqab_ready"), T_("sqab").add())
                    if i >= 2:
                        pe.wait_ge(sem("lnab_done"), T_("lnab").n + i - 1)
                    ins = mm(pair(i, 0, SEQ), block, rab[:, i, 0:SEQ], start=True, stop=True)
                    if n_q(l) == T or i not in Q_FEATS:
                        ins = mm(pair(i, SEQ, CTX), block, rab[:, i, SEQ:T], start=True, stop=True)
                    ins.then_inc(sem("msab_ready"), 1)
                T_("lnab").add(6)
                pe.wait_ge(sem("lnab_done"), T_("lnab").n)
                for i in range(6):
                    pe.wait_ge(sem("gswap_ready"), T_("gsw").add())
                    mm(bank(4 + i % 4) if i < 4 else bank(i - 4), gswap[:], ft[i][:, 0:SEQ], start=True,
                       stop=True).then_inc(sem("rot_done"), 1)

            def attention(l):
                units = att_units(l)
                n = len(units)
                e0, q0, y0, pt0 = T_("exp").n, T_("qk").n, T_("yab").n, T_("pt").n
                pe.wait_ge(sem("qk_ready"), T_("qk").add(6))

                def scores(u):
                    m, j, h = units[u]
                    lo, keys, masks = key_span(m, j)
                    if u >= 2:
                        pe.wait_ge(sem("exp_done"), e0 + u - 1)
                    q = ft[3 * m + h % 2][:, cols(j)]
                    k_ = ft[3 * m + 2] if h < 2 else kb1[m]
                    if lo < 512:
                        mm(pair(u, lo, 512 - lo), q, k_[:, keys[0] * P:keys[0] * P + 512 - lo], start=True,
                           stop=not masks)
                        for x_, (mk, at) in enumerate(masks):
                            mm(pair(u, at, P), ident_b[:], mk[:], start=False, stop=(x_ == len(masks) - 1))
                    mm(pair(u, 512, CTX), q, k_[:, SEQ:T], start=True, stop=True).then_inc(sem("sc_done"), 1)

                def transposes(u):
                    m, j, h = units[u]
                    _, keys, _ = key_span(m, j)
                    pe.wait_ge(sem("exp_done"), e0 + u + 1)
                    if u >= 1:
                        pe.wait_ge(sem("pt_ready"), pt0 + u)
                    for t in range(len(keys)):
                        ins = nc.tensor.transpose(bank(4, t * P, P), prob[u % 2][:, cols(t)], ident)
                    ins.then_inc(sem("tr_done"), 1)

                def values(u):
                    m, j, h = units[u]
                    _, keys, _ = key_span(m, j)
                    jj = u // 4
                    pe.wait_ge(sem("pt_ready"), pt0 + u + 1)
                    if h == 0 and jj >= 2:
                        pe.wait_ge(sem("yab_ready"), y0 + jj - 1)
                    for t, kt in enumerate(keys):
                        ins = mm(bank(6 + jj % 2, h * 64, 64), probT[u % 2][:, cols(t)],
                                 v_ab[:, kt, m * P + (h // 2) * 64:m * P + (h // 2) * 64 + 64],
                                 start=(t == 0), stop=(t == len(keys) - 1))
                    ins.then_inc(sem("pv_done"), 1)

                scores(0)
                for u in range(n):
                    if u + 1 < n:
                        scores(u + 1)
                    if u >= 1:
                        values(u - 1)
                    transposes(u)
                values(n - 1)
                T_("exp").add(n), T_("yab").add(n // 4), T_("pt").add(n)

            def gla(l):
                for d in range(2):
                    pe.wait_ge(sem("lay_landed"), 32 * (l + 1))
                    mm(pair(d, 0, SEQ), wg[:, d, :], ft[12][:, 0:SEQ], start=True, stop=True)
                    mm(pair(d, SEQ, CTX), wg[:, d, :], ft[12][:, SEQ:T], start=True, stop=True)\
                        .then_inc(sem("pre_done"), 1)
                for d in range(2):
                    pe.wait_ge(sem("kdec_ready"), T_("kdec").add())
                    for j in range(TILES):
                        ins = nc.tensor.transpose(pair(d, j * P, P), kdec[d][:, cols(j)], ident)
                    ins.then_inc(sem("kt_done"), 1)
                pe.wait_ge(sem("ktc_ready"), T_("ktc").add(2))
                for s in range(TILES - 1):
                    if s >= 2:
                        pe.wait_ge(sem("snap_ready"), T_("snap").n + s - 1)
                    for d in range(2):
                        j = ORDER[d][s]
                        ins = mm(bank(4 + s % 2, d * 256, 256), ktc[d][:, cols(j)], vc[:, j, :], start=True, stop=True)
                    ins.then_inc(sem("u_done"), 1)
                T_("snap").add(TILES - 1)
                n_oc = 0
                for hf, (j0, nt) in enumerate(halves(l)):
                    for li in range(8):
                        b = (hf * 8 + li) % 2
                        pe.wait_ge(sem("lev_factors"), T_("lf").add())
                        for t in range(nt):
                            k = T_("mm").n
                            if k - T_("mm0").n >= 4:
                                pe.wait_ge(sem("lev_merged"), T_("mg").n + k - T_("mm0").n - 3)
                            kk = ft[7][:, cols(j0 + t)] if li == 0 else kl[b][:, cols(t)]
                            mm(bank(k % 4), kk, qbd[b][:, t], start=True, stop=True).then_inc(sem("lev_done"), 1)
                            T_("mm").add()
                    pe.wait_ge(sem("lev_merged"), T_("mg").n + T_("mm").n - T_("mm0").n)
                    if hf == 0:
                        pe.wait_ge(sem("qe_ready"), T_("qe").add(2))
                        pe.wait_ge(sem("snap_ready"), T_("snap").n)
                    for t in range(nt):
                        j = j0 + t
                        if n_oc >= 2:
                            pe.wait_ge(sem("yc_ready"), T_("yc").n + n_oc - 1)
                        ob = 4 + j % 2
                        mm(bank(ob, 0, 256), qe[0][:, cols(j)], snap[:, 0, j, :], start=True, stop=False)
                        mm(bank(ob, 0, 256), qe[1][:, cols(j)], snap[:, 1, j, :], start=False, stop=False)
                        for h in range(4):
                            ins = mm(bank(ob, h * 64, 64), sacc[:, t, h, :], vc[:, j, h * 64:h * 64 + 64],
                                     start=False, stop=(h == 3))
                        ins.then_inc(sem("oc_done"), 1)
                        n_oc += 1
                T_("mg").add(T_("mm").n - T_("mm0").n)
                T_("mm0").n = T_("mm").n
                T_("yc").add(n_oc)

            def mlstm(l):
                for a, n in ((0, 4), (4, 2)):
                    for j in range(a, a + n):
                        for p_ in range(2):
                            ins = nc.tensor.transpose(pair(a // 4, (j - a) * 256 + p_ * P, P),
                                                      ft[10 + p_][:, cols(j)], ident)
                    ins.then_inc(sem("kd_done"), 1)
                pe.wait_ge(sem("ktd_ready"), T_("ktd").add(2))
                pe.wait_ge(sem("r_ready"), T_("r").add(3))
                for q in range(2):
                    for j in range(TILES):
                        ins = nc.tensor.transpose(pair(q, j * P, P), (r1, r2)[q][:, cols(j)], ident)
                    ins.then_inc(sem("r_trans"), 1)
                for d in range(2):
                    for p_ in range(2):
                        for hf in range(2):
                            h = 4 * d + 2 * p_ + hf
                            a = 4 * 512 + (2 * d + p_) * TILES
                            ins = mm(ps[64 * hf:64 * hf + 64, a:a + TILES], sel[:, h:h + 1].to_broadcast([P, 64]),
                                     dec[:], start=True, stop=True)
                ins.then_inc(sem("dec_done"), 1)
                pe.wait_ge(sem("qdb_ready"), T_("qdb").add(4))
                pe.wait_ge(sem("col_ready"), T_("col").add())
                pe.wait_ge(sem("dcb_ready"), T_("dcb").add())
                st0 = T_("st").n
                for s in range(TILES):
                    cur_ = s % 2
                    outs = [d for d in range(2) if not (l == DEPTH - 1 and ORDER[d][s] >= LAT_TILES)]
                    if s >= 1:
                        pe.wait_ge(sem("state_ready"), st0 + 2 * s)
                    for d in outs:
                        j = ORDER[d][s]
                        mk = (p_after, p_before)[d]
                        mm(bank(d), ident_b[:], mk[:].unsqueeze(1).to_broadcast([P, 4, P]), start=True, stop=False)
                        for h in range(4):
                            ins = mm(bank(d, h * P, P), sel[:, 4 * d + h:4 * d + h + 1].to_broadcast([P, P]),
                                     mrun[:, cols(j)], start=False, stop=(h == 3))
                        ins.then_inc(sem("mb_done"), 1)
                        if T_("pk").n >= 1:
                            pe.wait_ge(sem("p_ready"), T_("pr").n)
                        for p_ in range(2):
                            ins = mm(bank(2 + d, p_ * 256, 256), ft[10 + p_][:, cols(j)],
                                     qdb[:, 2 * p_:2 * p_ + 2, cols(j)], start=True, stop=True)
                        ins.then_inc(sem("qk_done"), 1)
                    if s < TILES - 1:
                        for d in range(2):
                            j = ORDER[d][s]
                            pe.wait_ge(sem("vw_ready"), T_("vw").add())
                            if d in outs:
                                pe.wait_ge(sem("w_ready"), T_("w").add())
                            for h in range(4):
                                hf = h % 2
                                a = d * 512 + (h // 2) * 65
                                ins = mm(ps[64 * hf:64 * hf + 64, a:a + 65], ktd[:, j, h * 64:h * 64 + 64],
                                         vw[:, d, h, :], start=True, stop=True)
                            ins.then_inc(sem("ud_done"), 1)
                    else:
                        T_("w").add(len(outs))
                    for d in outs:
                        j = ORDER[d][s]
                        pe.wait_ge(sem("p_ready"), T_("pr").add())
                        if T_("ydn").n >= 2:
                            pe.wait_ge(sem("yd_ready"), T_("ydn").n - 1)
                        T_("ydn").add()
                        T_("pk").add()
                        for h in range(4):
                            mm(bank(6 + d, h * 65, 65), qdb[:, h, cols(j)], cst_d[:, d, cur_, h // 2, :],
                               start=True, stop=True)
                        for h in range(4):
                            ins = mm(bank(4 + d, h * 65, 65), wb[s % 2][:, d, h, :], vd1[:, j, h, :],
                                     start=True, stop=True)
                        ins.then_inc(sem("num_done"), 1)
                T_("st").add(2 * (TILES - 1))

            def finish(l):
                nj = TILES if l == 0 else LAT_TILES
                lo0 = T_("ytl").n
                for j in range(nj):
                    pe.wait_ge(sem("y_ready"), T_("y").add())
                    if j >= 2:
                        pe.wait_ge(sem("yt_ready"), lo0 + j - 1)
                    for k in range(KD):
                        ins = nc.tensor.transpose(pair(j, k * P, P), y[:, j, k * P:(k + 1) * P], ident)
                    ins.then_inc(sem("yt_done"), 1)
                T_("ytl").add(nj)
                pe.wait_ge(sem("yt_ready"), T_("ytl").n)

            def out_proj(l, n_t):
                for s in range(OUT_SLOTS):
                    r = wts.n % 2
                    pe.wait_ge(sem("lo_ready"), wts.add())
                    for m in range(2):
                        k = 2 * s + m
                        if k >= 2:
                            pe.wait_ge(sem("x_done"), T_("xd").n - 1)
                        feature_group(k, r, m, (yT_hi, yT_lo), n_t)
                        T_("xd").add()
                    if mod_after(l, IN_SLOTS + s) is not None:
                        mod_slot()

            def mlp_quarter(l, n_t):
                for s in range(QW1 + QW2):
                    r = s % 2
                    pe.wait_ge(sem("lo_ready"), wts.add())
                    for m in range(2):
                        g = 2 * s + m
                        if g < 2:
                            if g == 0:
                                pe.wait_ge(sem("x_done"), T_("xd").at(0))
                        elif g < 10:
                            pe.wait_ge(sem("relu_done"), T_("relu").at(g - 9 if s >= QW1 else -1))
                        else:
                            pe.wait_ge(sem("x_done"), T_("xd").at(-1))
                        if s < QW1:
                            if g == 0:
                                feature_pair(0, r, (h_hi, h_lo), n_t, (sem("h_ready"), T_("h").n - KD))
                            elif g >= 2:
                                feature_group(g, r, m, (h_hi, h_lo), n_t)
                            T_("relu").add()
                        else:
                            if g == 2 * QW1:
                                feature_group(g, r, m, (hid_hi, hid_lo), n_t, (sem("hid_ready"), T_("hid").at(0)))
                                T_("hid").add(8)
                            else:
                                feature_group(g, r, m, (hid_hi, hid_lo), n_t)
                            T_("xd").add()
                    if l == 0 and s < Q_MODS:
                        mod_slot()

            for l in range(DEPTH):
                n_t = T if l == 0 else SEQ
                if l == 0:
                    pe.wait_ge(sem("cs_ready"), 1)
                    pe.wait_ge(sem("x_in"), TILES)
                    first_mods(0, 4)
                norm_sum(T)
                if l == 0:
                    first_mods(4, FIRST_MODS)
                    first_mods_columns()
                in_proj(l)
                stage_end()
                prep_ab(l)
                attention(l)
                stage_end()
                gla(l)
                stage_end()
                mlstm(l)
                stage_end()
                finish(l)
                out_proj(l, n_t)
                norm_sum(n_t)
                T_("h").add(KD)
                n_loop = QUARTERS if l < DEPTH - 1 else QUARTERS - 1
                looped = [(wts, 8), (T_("relu"), 8), (T_("hid"), 8), (T_("xd"), 8), (mods, 2 * Q_MODS if l == 0 else 0),
                          (mods_out, Q_MODS if l == 0 else 0)]
                with pe.Fori(0, n_loop) as i:
                    for t, per in looped:
                        t.enter(i, per)
                    mlp_quarter(l, n_t)
                for t, per in looped:
                    t.leave(n_loop)
                if l == DEPTH - 1:
                    mlp_quarter(l, n_t)
            pe.wait_ge(sem("x_done"), T_("xd").n)
            for j in range(LAT_TILES):
                if j >= 2:
                    pe.wait_ge(sem("out_ready"), j - 1)
                for k in range(KD):
                    ins = nc.tensor.transpose(pair(j, k * P, P), xT[:, k, cols(j)], ident)
                ins.then_inc(sem("out_trans"), 1)


def _slots(w, widths=WC):
    k, m = w.shape
    return w.reshape(k // P, P, m // widths, widths).transpose(2, 1, 0, 3).reshape(m // widths, P, -1)


def _in_columns():
    gw, kw, gk = 256, 128, 128
    names = [("qa", gw), ("ka", kw), ("va", kw), ("qb", gw), ("kb", kw), ("vb", kw), ("qc", gk), ("kc", gk),
             ("vc", gw), ("rc", gw), ("gc", 32), ("qd", gw), ("kd", gw), ("vd", gw), ("od", gw), ("id", 8), ("fd", 8)]
    at, c = {}, 0
    for n, w in names:
        at[n] = np.arange(c, c + w)
        c += w

    def q_pair(n, p):
        return np.concatenate([at[n][64 * p:64 * p + 64], at[n][64 * (p + 2):64 * (p + 2) + 64]])
    gates = -np.ones(P, dtype=np.int64)
    gates[0:4] = at["id"][0:4]
    gates[32:36] = at["id"][4:8]
    gates[16:32] = at["gc"][0:16]
    gates[48:64] = at["gc"][16:32]
    gates[64:68] = at["fd"][0:4]
    gates[96:100] = at["fd"][4:8]
    return np.concatenate([q_pair("qa", 0), q_pair("qa", 1), at["ka"], q_pair("qb", 0), q_pair("qb", 1), at["kb"],
                           at["qc"], at["kc"], at["qd"], at["kd"], gates, -np.ones(P, dtype=np.int64),
                           at["va"], at["vb"], at["vc"], at["vd"], at["rc"], at["od"]])


def _constants():
    c = np.zeros((P, C_ALL), np.float32)
    p = np.arange(P)
    c[:, C_IDENT:C_IDENT + P] = np.eye(P)
    c[:, C_BLOCK:C_BLOCK + P] = (p[:, None] // HD == p[None, :] // HD)
    sw = np.zeros((P, P), np.float32)
    e = np.arange(0, P, 2)
    sw[e + 1, e] = -1.0
    sw[e, e + 1] = 1.0
    c[:, C_SWAP:C_SWAP + P] = sw
    t = np.arange(SEQ)
    n_freq = HD // 4
    inv = np.float32(ROPE_THETA) ** (-np.arange(n_freq, dtype=np.float32) / np.float32(n_freq))
    row = (t // GRID_W).astype(np.float32)
    col = (t % GRID_W).astype(np.float32)
    ang = np.concatenate([row[:, None] * inv, col[:, None] * inv], axis=-1).astype(np.float32)
    idx = (p % HD) // 2
    c[:, C_COS:C_COS + SEQ] = np.cos(ang).T[idx]
    c[:, C_SIN:C_SIN + SEQ] = np.sin(ang).T[idx]
    for d in range(2):
        for h in range(4):
            c[32 * d + h, C_SEL + 4 * d + h] = 1.0
            c[32 * h:32 * h + 32, C_HM + 4 * d + h] = 1.0
    s_, t_ = p[:, None], p[None, :]
    c[:, C_LEVEL:C_LEVEL + P] = np.eye(P)
    for i, h in enumerate(LEVELS):
        same = (s_ // (2 * h)) == (t_ // (2 * h))
        c[:, C_LEVEL + (i + 1) * P:C_LEVEL + (i + 2) * P] = same & ((s_ // h) != (t_ // h))
    c[:, C_LEFT:C_LEFT + P] = t_ < s_
    c[:, C_RIGHT:C_RIGHT + P] = t_ > s_
    return c


def kernel(**inputs):
    import concourse.bacc as _bacc
    from concourse.bass_utils import run_bass_kernel_spmd as _run

    a = {k: np.ascontiguousarray(v) for k, v in inputs.items()}
    cols_ = _in_columns()
    slots, mods, vrows, gate, row_list = [], [], [a["c"][0].reshape(KD, P), a["c_ctx"].reshape(KD, P)], [], []
    for l in range(DEPTH):
        mods.append(_slots(a["w_mod"][l]))
        w_in = np.zeros((D_MODEL, len(cols_)), a["w_in"].dtype)
        w_in[:, cols_ >= 0] = a["w_in"][l][:, cols_[cols_ >= 0]]
        slots.append(_slots(w_in))
        slots.append(_slots(a["w_out"][l]))
        for q in range(QUARTERS):
            w = D_MODEL
            slots.append(_slots(a["w_mlp1"][l][:, q * w:(q + 1) * w]))
            slots.append(_slots(a["w_mlp2"][l][q * w:(q + 1) * w, :]))
        gb = np.zeros((1, P), np.float32)
        gb[0, 0:4], gb[0, 32:36] = a["b_mlstm_i"][l]
        gb[0, 64:68], gb[0, 96:100] = a["b_mlstm_f"][l]
        vrows += [a["b_mod"][l].reshape(48, P), a["g_norm1"][l].reshape(KD, P), a["g_norm2"][l].reshape(KD, P), gb]
        vrows += [np.tile(a[n][l], 2)[None] for n in ("g_q_a", "g_k_a", "g_q_b", "g_k_b")]
        vrows.append(a["b_gla_gate"][l])
        g = np.zeros((P, 2, P), np.float32)
        g[16:32, 0] = a["w_gla_gate"][l, 0]
        g[48:64, 1] = a["w_gla_gate"][l, 1]
        gate.append(g)
        row_list.append(np.concatenate([a["sink_b"][l], np.tile(a["g_gla_out"][l], 4), np.tile(a["g_mlstm_out"][l], 4)]))
    arrays = {
        "x_in": a["x"][0], "ctx_in": a["ctx"][0], "w_big": np.concatenate(slots), "w_modl": np.concatenate(mods),
        "vecs": np.concatenate(vrows), "consts": _constants(), "gla_gate": np.stack(gate), "rows": np.stack(row_list),
    }
    nc = _bacc.Bacc("TRN2", target_bir_lowering=False, num_devices=1)
    args = [nc.dram_tensor(n, v.shape, F32, kind="ExternalInput").ap() for n, v in arrays.items()]
    out = nc.dram_tensor("out", (SEQ, D_MODEL), F32, kind="ExternalOutput").ap()
    build(nc, *args, out)
    r = _run(nc, [arrays], core_ids=[0])
    return r.results[0]["out"][None]
```

```python
import numpy as np
import concourse.bass as bass
from concourse import mybir

F32 = mybir.dt.float32
F32R = mybir.dt.float32r
BF16 = mybir.dt.bfloat16
U8 = mybir.dt.uint8
ALU = mybir.AluOpType
ACT = mybir.ActivationFunctionType
AX_X = mybir.AxisListType.X

P = 128
D_MODEL = 1024
SEQ = 512
CTX = 256
T = SEQ + CTX
DEPTH = 2
GRID_W = 64
HD = 64
KD = D_MODEL // P
TILES = T // P
LAT_TILES = SEQ // P
GLA_DK = 32
GATE_RANK = 16
GLA_TAU = 16.0
ROPE_THETA = 10000.0
EPS = 1e-6
BIG = 1e30
N_MOD = 6
WC = 256
MOD_SLOTS = N_MOD * D_MODEL // WC
IN_SLOTS = 12
OUT_SLOTS = D_MODEL // WC
QUARTERS = 4
QW1 = 4
QW2 = 4
LAYER_SLOTS = IN_SLOTS + OUT_SLOTS + QUARTERS * (QW1 + QW2)
FIRST_MODS = 8
FEATS = 13
ONE_RAW = LAYER_SLOTS + 2
G_OF = (0, 0, 1, 2, 2, 3)
GATE_SLOT = 7
Q_FEATS = (0, 1, 3, 4, 6, 8, 9)
ORDER = ((4, 5, 0, 1, 2, 3), (5, 4, 3, 2, 1, 0))
LEVELS = (64, 32, 16, 8, 4, 2, 1)

C_IDENT, C_BLOCK, C_SWAP = 0, P, 2 * P
C_COS = 3 * P
C_SIN = C_COS + SEQ
C_SEL = C_SIN + SEQ
C_HM = C_SEL + 8
C_KEEP = C_HM + 8
C_LEVEL = C_KEEP
C_LEFT = C_LEVEL + 8 * P
C_RIGHT = C_LEFT + P
C_ALL = C_RIGHT + P

V_C = 0
V_CC = KD
V_L = 2 * KD
LV_BMOD, LV_G1, LV_G2, LV_GB = 0, 48, 56, 64
LV_GQK = 65
LV_BG = 69
LV = 71
V_ALL = V_L + LV


class Tally:

    def __init__(self):
        self.n = 0
        self.term = None

    def add(self, k=1):
        self.n += k
        return self.at(0)

    def at(self, back):
        v = self.n + back
        return v if self.term is None else self.term + v

    def enter(self, i, per):
        self.start, self.per = self.n, per
        if i is not None:
            self.term = i * per

    def leave(self, times):
        assert self.n - self.start == self.per, (self.n, self.start, self.per)
        self.n = self.start + self.per * times
        self.term = None


def build(nc, x_in, ctx_in, w_big, w_mod, vecs, consts, gla_gate, rows, out):
    def place(name, off, shape, dt=F32):
        return nc.alloc_sbuf_tensor_at(name, [P] + list(shape), dt, offset=off)

    base = (nc.sbuf_base + 63) // 64 * 64
    cur = [base]

    def keep(name, shape, dt=F32):
        size = int(np.prod(shape)) * {F32: 4, F32R: 4, BF16: 2, U8: 1}[dt]
        off = cur[0]
        cur[0] += (size + 31) // 32 * 32
        return place(name, off, shape, dt)

    xT = keep("xT", [KD, T])
    raw = [keep(f"raw{r}", [KD, WC]) for r in range(2)]
    w_hi = [keep(f"w_hi{r}", [KD, WC], F32R) for r in range(2)]
    w_lo = [keep(f"w_lo{r}", [KD, WC], F32R) for r in range(2)]
    cst = keep("cst", [C_KEEP])
    ones = keep("ones", [1])
    lmask = keep("lmask", [8, P], U8)
    ident_b = keep("ident_b", [P], BF16)
    m_left = keep("m_left", [P], BF16)
    m_right = keep("m_right", [P], BF16)
    p_after = keep("p_after", [P], BF16)
    p_before = keep("p_before", [P], BF16)
    vcol = [keep("vcol0", [V_ALL]), keep("vcol1", [LV])]
    cs = keep("cs", [KD, 2])
    modt = [keep(f"modt{l}", [2 * 48]) for l in range(DEPTH)]
    gs = keep("gs", [KD, 2])
    mod_acc_at = cur[0]
    mod_acc = keep("mod_acc", [2, WC])
    wg = keep("wg", [2, P])
    rowc = keep("rowc", [4 + 2 * 256])
    nsink = keep("nsink", [4])
    eps = keep("eps", [1])
    mx = keep("mx", [2])
    nb = keep("nb", [2, 4])
    se = keep("se", [2, 4])
    es = keep("es", [2, 4])
    psum_e = keep("psum_e", [2, 4])
    rs = keep("rs", [2, 4])
    dex = keep("dex", [2, TILES])
    mp = keep("mp", [TILES])
    mend = keep("mend", [TILES])
    dec = keep("dec", [TILES])
    dcb = keep("dcb", [4, TILES])
    col = keep("col", [TILES, 2, 4, 4])
    ident = cst[:, C_IDENT:C_IDENT + P]
    block = cst[:, C_BLOCK:C_BLOCK + P]
    swap = cst[:, C_SWAP:C_SWAP + P]
    cos = cst[:, C_COS:C_COS + SEQ]
    sin = cst[:, C_SIN:C_SIN + SEQ]
    sel = cst[:, C_SEL:C_SEL + 8]
    hm8 = cst[:, C_HM:C_HM + 8]

    TB = T * 4
    RH = cur[0]
    RS = RH + KD * TB
    RU = RS + KD * TB
    RV = RU + 16 * TB
    END = RV + 6 * 260 * 4 + 6 * 256 * 4 + 6 * 512 * 4
    assert END <= nc.sbuf_usable_end, (END, nc.sbuf_usable_end)

    h_hi = place("h_hi", RH, [KD, T], F32R)
    h_lo = place("h_lo", RS, [KD, T], F32R)
    y = place("y", RH, [TILES, 4 * 256])
    SLOT = KD * WC * 4
    xin = [place(f"xin{j}", RU + j * D_MODEL * 4, [D_MODEL]) for j in range(TILES)]
    first_at = [RS + j * SLOT for j in range(3)] + [RU + (3 + j) * SLOT for j in range(3)] + [RH, RH + SLOT]
    first_mod = [place(f"first_mod{j}", a, [KD, WC]) for j, a in enumerate(first_at)]
    mod_rows = place("mod_rows", RV + 5 * T * 4, [FIRST_MODS * WC])
    cload = place("cload", RH + 2 * SLOT, [C_ALL - C_KEEP])
    vin = place("vin", RH + 2 * SLOT + (C_ALL - C_KEEP) * 4, [P])
    vin1 = place("vin1", RH + 2 * SLOT + (C_ALL - C_KEEP) * 4 + P * 4, [P])
    xout = [place(f"xout{i}", RH + i * 4096, [D_MODEL]) for i in range(2)]
    tmp = [place(f"tmp{i}", RV + i * TB, [T]) for i in range(8)]
    ft = [None] * FEATS
    v_ab = place("v_ab", RU + 6 * TB, [TILES, 256])
    for i in range(6):
        ft[i] = place(f"ft{i}", RU + i * TB, [T])
    for i in range(6, FEATS):
        ft[i] = place(f"ft{i}", RU + (i + 2) * TB, [T])
    SPARE = RU + 15 * TB
    vd1 = place("vd1", RV, [TILES, 4, 65])
    sig_r = place("sig_r", RV + 6 * 260 * 4, [TILES, 256])
    vc = place("vc", RV + 6 * 260 * 4, [TILES, 256])
    ro = place("ro", RV + 6 * 516 * 4, [TILES, 512])
    yT_hi = place("yT_hi", RU, [KD, T], F32R)
    yT_lo = place("yT_lo", RU + KD * TB, [KD, T], F32R)
    hid_hi = place("hid_hi", RU, [KD, T], F32R)
    hid_lo = place("hid_lo", RU + KD * TB, [KD, T], F32R)
    gswap = place("gswap", mod_acc_at, [P])
    ms8 = place("ms8", mod_acc_at + 512, [TILES * 8])
    rab = place("rab", RS, [6, T])
    kb1 = [place(f"kb1_{m}", RS + (6 + m) * TB, [T]) for m in range(2)]
    rt = [place(f"rt{i}", RH + i * 2048, [SEQ]) for i in range(8)]
    prob = [place(f"prob{i}", RS + i * TB, [T]) for i in range(2)]
    probT = [place(f"probT{i}", RS + (2 + i) * TB, [T]) for i in range(2)]
    bb = [place(f"bb{d}", RS + d * TB, [T]) for d in range(2)]
    snap = place("snap", RS + 2 * TB, [2, TILES, 256])
    qe = [place(f"qe{d}", RS + (6 + d) * TB, [T]) for d in range(2)]
    ls = place("ls", RU, [2, T])
    pre = [place(f"pre{d}", RU + (3 + d) * TB, [T]) for d in range(2)]
    ex = place("ex", RU + 5 * TB, [2, T])
    kdec = [place(f"kdec{d}", RU + d * TB, [T]) for d in range(2)]
    ktc = [place(f"ktc{d}", RU + (2 + d) * TB, [T]) for d in range(2)]
    umask = place("umask", RU + 7 * TB, [2, 256])
    HT = 3 * P
    sacc = place("sacc", RU, [3, 4, P])
    eqk = [place(f"eqk{b}", RU + (2 + b) * TB, [2, HT]) for b in range(2)]
    qbd = [place(f"qbd{b}", RU + (4 + 2 * b) * TB, [3, 4, P]) for b in range(2)]
    kl = [place(f"kl{b}", SPARE + b * HT * 4, [HT]) for b in range(2)]
    qdb = place("qdb", RS, [4, T])
    ktd = place("ktd", RS + 4 * TB, [TILES, 256])
    o = RU
    wb = [place(f"wb{b}", o + b * 4096, [2, 4, P]) for b in range(2)]
    o += 8192
    vw = place("vw", o, [2, 4, 65])
    o += 2080
    t1 = place("t1", o, [2, 4, 65])
    t2 = place("t2", o + 2080, [2, 4, 65])
    hh = place("hh", o + 4160, [2, 4, 64])
    cst_d = place("cst_d", o + 6208, [2, 2, 2, 65])
    dd = place("dd", o + 8288, [2, 4])
    rd = place("rd", o + 8320, [2, 4])
    assert o + 8352 <= RU + 10 * TB
    lsf = place("lsf", SPARE, [T])
    r1 = place("r1", RV, [T])
    r2 = place("r2", RV + TB, [T])
    sqy = place("sqy", RS, [TILES, 512])

    ps = nc.alloc_psum_tensor("ps", [P, 4096], F32)

    def bank(b, a=0, n=512):
        return ps[:, b * 512 + a:b * 512 + a + n]

    def pair(g, a=0, n=1024):
        return bank(2 * (g % 2), a, n)

    S = {}

    def sem(name):
        if name not in S:
            S[name] = nc.alloc_semaphore(name)
        return S[name]

    def cols(j, n=1):
        return slice(j * P, (j + n) * P)

    def bc(ap, n):
        return ap.unsqueeze(2).to_broadcast([ap.shape[0], ap.shape[1], n])

    def mod_after(l, s):
        if l == 0 and s < IN_SLOTS + OUT_SLOTS:
            return FIRST_MODS + s
        return None

    Q_MODS = MOD_SLOTS // QUARTERS
    N_W = DEPTH * LAYER_SLOTS

    def lvec(l, i, n=1):
        b = (V_L if l == 0 else 0) + i
        return vcol[l][:, b:b + n]

    def att_units(l):
        js = range(TILES) if l == 0 else range(LAT_TILES)
        return [(m, j, h) for m in range(2) for j in js for h in range(4)]

    def key_span(m, j):
        if j >= LAT_TILES:
            return 512, [4, 5], []
        if m == 0:
            return 0, [0, 1, 2, 3, 4, 5], []
        k0, k1 = max(0, j - 1), min(LAT_TILES - 1, j + 1)
        n = k1 - k0 + 1
        lo = 512 - n * P
        masks = []
        if j > 0:
            masks.append((m_left, lo))
        if j < LAT_TILES - 1:
            masks.append((m_right, 512 - P))
        return lo, list(range(k0, k1 + 1)) + [4, 5], masks

    def raw_of(w):
        return 0 if w < ONE_RAW else 1 - w % 2

    def landed(w):
        if w < ONE_RAW:
            return sem("w_landed0"), 16 * (w + 1)
        n = (w - ONE_RAW) // 2 + 1
        return (sem("w_landed1"), 16 * n) if raw_of(w) else (sem("w_landed0"), 16 * (ONE_RAW + n))

    def n_q(l):
        return T if l < DEPTH - 1 else SEQ

    def token_tiles(l, s, m):
        if l == DEPTH - 1 and s in (GATE_SLOT, GATE_SLOT + 1):
            return 2 * m, 2
        return ((0, 4), (4, 2))[m]

    def halves(l):
        return [(0, 3), (3, 3 if l == 0 else 1)]

    def levels(l):
        return [(hf, li, j0, nt) for hf, (j0, nt) in enumerate(halves(l)) for li in range(8)]

    blk = nc.Block()
    with blk:
        @blk.sync
        def _(sp):
            sp.dma_start(vin[0:V_ALL, :], vecs[0:V_ALL, :]).then_inc(sem("c_landed"), 16)
            sp.dma_start(vin1[0:LV, :], vecs[V_ALL:V_ALL + LV, :]).then_inc(sem("c_landed"), 16)
            sp.dma_start(cst[:], consts[:, 0:C_KEEP]).then_inc(sem("c_landed"), 16)
            for j in range(TILES):
                src = x_in[cols(j), :] if j < LAT_TILES else ctx_in[cols(j - LAT_TILES), :]
                sp.dma_start(xin[j][:], src).then_inc(sem(f"x_landed{j}"), 16)
            mods = Tally()
            wts = Tally()

            def load_mod(idx):
                if mods.term is not None or mods.n > 0:
                    sp.wait_ge(sem("mod_summed"), mods.at(0))
                sp.dma_start(raw[1][:], idx).then_inc(sem("mod_landed"), 16)
                mods.add(2)

            def load_w(idx, w):
                if w == ONE_RAW:
                    sp.wait_ge(sem("mod_summed"), 2 * (DEPTH * MOD_SLOTS - FIRST_MODS))
                elif w > 0:
                    sp.wait_ge(sem("lo_ready"), wts.at(0 if w < ONE_RAW else -1))
                sp.dma_start(raw[raw_of(w)][:], idx).then_inc(landed(w)[0], 16)
                wts.add()

            def wslot(n):
                return w_big[n].rearrange("p (k m) -> p k m", k=KD)

            def mslot(n):
                return w_mod[n].rearrange("p (k m) -> p k m", k=KD)

            for j in range(FIRST_MODS):
                sp.dma_start(first_mod[j][:], mslot(j)).then_inc(sem(f"first_mod_landed{j}"), 16)
            sp.dma_start(cload[:], consts[:, C_KEEP:C_ALL]).then_inc(sem("masks_landed"), 16)
            load_w(wslot(0), 0)
            load_mod(mslot(FIRST_MODS))
            load_w(wslot(1), 1)
            for l in range(DEPTH):
                sp.dma_start(rowc[:], rows[l:l + 1, :].to_broadcast([P, rows.shape[1]])).then_inc(sem("lay_landed"), 16)
                sp.dma_start(wg[:], gla_gate[l]).then_inc(sem("lay_landed"), 16)
                w0 = l * LAYER_SLOTS
                for s in range(IN_SLOTS + OUT_SLOTS):
                    if mod_after(l, s) is not None and s > 0:
                        load_mod(mslot(mod_after(l, s)))
                    load_w(wslot(w0 + s + 2), w0 + s + 2)
                q0 = w0 + IN_SLOTS + OUT_SLOTS
                n_loop = QUARTERS if l < DEPTH - 1 else QUARTERS - 1
                mods_per = Q_MODS if l == 0 else 0
                with sp.Fori(0, n_loop) as i:
                    wts.enter(i, 8)
                    mods.enter(i, 2 * mods_per)
                    for s in range(QW1 + QW2):
                        if s < mods_per:
                            load_mod(w_mod[bass.ds(i * Q_MODS + (MOD_SLOTS + s), 1)]
                                     .rearrange("o p (k m) -> p (o k) m", k=KD))
                        load_w(w_big[bass.ds(i * 8 + (q0 + s + 2), 1)].rearrange("o p (k m) -> p (o k) m", k=KD),
                               q0 + s + 2)
                wts.leave(n_loop)
                mods.leave(n_loop)
                if l == DEPTH - 1:
                    for s in range(QW1 + QW2 - 2):
                        load_w(wslot(q0 + 8 * n_loop + s + 2), q0 + 8 * n_loop + s + 2)
                if l == 0:
                    sp.wait_ge(sem("x_done"), 8 * (1 + QUARTERS))
            for j in range(LAT_TILES):
                sp.wait_ge(sem("out_ready"), j + 1)
                sp.dma_start(out[cols(j), :], xout[j % 2][:]).then_inc(sem(f"out_stored{j % 2}"), 16)
            for r in range(2):
                sp.wait_ge(sem(f"out_stored{r}"), 16 * (LAT_TILES // 2))

        @blk.gpsimd
        def _(gp):
            def low(n, r, raw_r):
                gp.wait_ge(sem("hi_ready"), n)
                nc.gpsimd.tensor_tensor(w_lo[r][:], raw[raw_r][:], w_hi[r][:].bitcast(F32),
                                        ALU.subtract).then_inc(sem("lo_ready"), 1)
            def lows(a, b):
                with gp.Fori(0, (b - a) // 2) as i:
                    low(i * 2 + (a + 1), 0, raw_of(a))
                    low(i * 2 + (a + 2), 1, raw_of(a + 1))

            c = {}

            def T_(name):
                return c.setdefault(name, Tally())

            def gla_levels(l):
                seq = levels(l)
                n_lev = [q[3] for q in seq]
                bl0 = T_("lb").n

                def exponents(it):
                    hf, li, j0, nt = seq[it]
                    if li == 0:
                        return
                    h, b = LEVELS[li - 1], it % 2
                    tok = slice(j0 * P, (j0 + nt) * P)
                    b0 = bb[0][:, tok].rearrange("p (n w h) -> p n w h", w=2, h=h)
                    b1 = bb[1][:, tok].rearrange("p (n w h) -> p n w h", w=2, h=h)
                    eq = eqk[b][:, 0, 0:nt * P].rearrange("p (n w h) -> p n w h", w=2, h=h)
                    ek = eqk[b][:, 1, 0:nt * P].rearrange("p (n w h) -> p n w h", w=2, h=h)
                    ref0, ref1 = bc(b0[:, :, 0, h - 1], h), bc(b1[:, :, 1, 0], h)
                    if it >= 2:
                        gp.wait_ge(sem("lev_blocks"), bl0 + it - 1)
                        if T_("kl").n:
                            gp.wait_ge(sem("kl_ready"), T_("kl").n)
                    tt = nc.gpsimd.tensor_tensor
                    tt(eq[:, :, 1, :], b0[:, :, 1, :], ref0, ALU.subtract)
                    tt(eq[:, :, 0, :], b1[:, :, 0, :], ref1, ALU.subtract)
                    tt(ek[:, :, 0, :], ref0, b0[:, :, 0, :], ALU.subtract)
                    tt(ek[:, :, 1, :], ref1, b1[:, :, 1, :], ALU.subtract).then_inc(sem("e_raw"), 1)

                gp.wait_ge(sem("lev_start"), l + 1)
                for it in range(len(seq)):
                    hf, li, j0, nt = seq[it]
                    if it + 1 < len(seq):
                        exponents(it + 1)
                    if li > 0:
                        b = it % 2
                        gp.wait_ge(sem("e_ready"), T_("er").add())
                        if it >= 2:
                            gp.wait_ge(sem("lev_done"), T_("lev").n + sum(n_lev[:it - 1]))
                        nc.gpsimd.tensor_tensor(kl[b][:, 0:nt * P], ft[7][:, j0 * P:(j0 + nt) * P],
                                                eqk[b][:, 1, 0:nt * P], ALU.mult).then_inc(sem("kl_ready"), 1)
                        T_("kl").add()
                T_("lb").add(len(seq))
                T_("lev").add(sum(n_lev))

            lows(0, IN_SLOTS + 2)
            gla_levels(0)
            lows(IN_SLOTS + 2, ONE_RAW)
            lows(ONE_RAW, LAYER_SLOTS + IN_SLOTS + 2)
            gla_levels(1)
            lows(LAYER_SLOTS + IN_SLOTS + 2, N_W)

        @blk.scalar
        def _(act):
            big = Tally()
            w_n = Tally()
            c = {}

            def T_(name):
                return c.setdefault(name, Tally())

            w_groups = []
            for l in range(DEPTH):
                for s in range(LAYER_SLOTS):
                    w_groups.append((w_groups[-1] if w_groups else 0) + (1 if s == 6 else 2))

            def split_hi(w, i=None, per=0):
                if w >= N_W:
                    return
                land, n = landed(w)
                if i is None:
                    act.wait_ge(land, n)
                    if w >= 2:
                        act.wait_ge(sem("big_done"), w_groups[w - 2])
                else:
                    act.wait_ge(land, i * (128 if w < ONE_RAW else 64) + n)
                    act.wait_ge(sem("big_done"), i * 16 + w_groups[w - 2])
                nc.scalar.activation(w_hi[w % 2][:], raw[raw_of(w)][:], ACT.Copy).then_inc(sem("hi_ready"), 1)

            stage_n = [0]

            def stage_end():
                act.drain().then_inc(sem("stage_done"), 1)
                stage_n[0] += 3
                act.wait_ge(sem("stage_done"), stage_n[0])

            own = Tally()

            def step(ins):
                ins.then_inc(sem("act_step"), 1)
                act.wait_ge(sem("act_step"), own.add())

            act.wait_ge(sem("v_cols"), 1)
            nc.scalar.activation(cs[:, :, 0], vcol[0][:, V_C:V_C + KD], ACT.Exp, scale=-1.0)
            nc.scalar.activation(cs[:, :, 1], vcol[0][:, V_CC:V_CC + KD], ACT.Exp,
                                 scale=-1.0).then_inc(sem("c_exp"), 1)
            for j in range(TILES):
                act.wait_ge(sem("x_trans"), j + 1)
                nc.scalar.activation(xT[:, :, cols(j)], pair(j).rearrange("p (k t) -> p k t", k=KD),
                                     ACT.Copy).then_inc(sem("x_in"), 1)

            def norm(l, which, n_t, x_total):
                parts = [(0, 0, SEQ)] + ([(1, SEQ, T)] if n_t == T else [])
                sqn, accn, hn = T_("sq"), T_("acc"), T_("h")
                t_n, hh_n = T_("t"), T_("h_hi")
                for k in range(KD):
                    act.wait_ge(sem("x_done"), x_total - KD + k + 1) if x_total else \
                        act.wait_ge(sem("x_in"), TILES)
                    if k >= 2:
                        act.wait_ge(sem("acc_added"), accn.n + max(1, k - 2))
                    nc.scalar.activation(tmp[k % 2][:, 0:n_t], xT[:, k, 0:n_t],
                                         ACT.Square).then_inc(sem("sq_ready"), 1)
                accn.add(KD - 1)
                act.wait_ge(sem("ms_ready"), T_("ms").add())
                step(nc.scalar.activation(tmp[3][:, 0:n_t], bank(4, 0, n_t), ACT.Ln, bias=eps[:, 0:1],
                                          scale=1.0 / D_MODEL))
                nc.scalar.activation(tmp[3][:, 0:n_t], tmp[3][:, 0:n_t], ACT.Exp,
                                     scale=-0.5).then_inc(sem("rstd_ready"), 1)
                if x_total == 0:
                    split_hi(0)
                sh = modt[l][:].rearrange("p (m c) -> p m c", c=2)
                m0 = 0 if which == 1 else 24
                for k in range(KD):
                    act.wait_ge(sem("t_ready"), t_n.add())
                    if k >= 2:
                        act.wait_ge(sem("h_ready"), hn.n + k - 1)
                    for c_i, a, b in parts:
                        ins = nc.scalar.activation(tmp[4 + k % 2][:, a:b], tmp[k % 2][:, a:b], ACT.Identity,
                                                   bias=sh[:, m0 + k, c_i:c_i + 1], scale=gs[:, k, c_i:c_i + 1])
                    ins.then_inc(sem("h_full"), 1)
                    act.wait_ge(sem("h_full"), hh_n.add())
                    nc.scalar.activation(h_hi[:, k, 0:n_t], tmp[4 + k % 2][:, 0:n_t],
                                         ACT.Copy).then_inc(sem("h_hi_ready"), 1)
                if x_total == 0:
                    split_hi(1)
                hn.add(KD)

            def in_proj(l):
                scale = {6: GLA_DK ** -0.5, 10: HD ** -0.5, 11: HD ** -0.5}
                for s in range(IN_SLOTS):
                    w = l * LAYER_SLOTS + s
                    for m in range(2):
                        g = 2 * s + m
                        if g < FEATS:
                            n = n_q(l) if g in Q_FEATS else T
                            act.wait_ge(sem("big_done"), big.add())
                            if g == 12:
                                ins = nc.scalar.activation(ft[g][:], pair(g, 0, T), ACT.Identity,
                                                           bias=lvec(l, LV_GB), scale=1.0)
                            else:
                                ins = nc.scalar.activation(ft[g][:, 0:n], pair(g, 0, n), ACT.Copy,
                                                           scale=scale.get(g, 1.0))
                            ins.then_inc(sem("ft_ready"), 1)
                        elif g > FEATS:
                            big.add()
                    if s == GATE_SLOT:
                        act.wait_ge(sem("absf_ready"), l + 1)
                        step(nc.scalar.activation(lsf[64:128, :], lsf[64:128, :], ACT.Exp))
                        nc.scalar.activation(lsf[64:128, :], lsf[64:128, :], ACT.Ln,
                                             bias=1.0).then_inc(sem("softplusf_ready"), 1)
                    if s == GATE_SLOT + 3:
                        act.wait_ge(sem("r_raw"), l + 1)
                        nc.scalar.activation(r1[64:128, :], r1[64:128, :], ACT.Exp).then_inc(sem("r_ready"), 1)
                        nc.scalar.activation(r2[:], r2[:], ACT.Exp).then_inc(sem("r_ready"), 1)
                        nc.scalar.activation(dec[:], dec[:], ACT.Exp).then_inc(sem("r_ready"), 1)
                    if s in (GATE_SLOT + 1, GATE_SLOT + 2):
                        which, nj = s - GATE_SLOT - 1, n_q(l) // P
                        src = ro[:, 0:nj, which * 256:(which + 1) * 256]
                        act.wait_ge(sem("vt_ready"), 10 * l + 2 * (which + 1))
                        e = (sig_r[:, 0:nj, :], src)[which]
                        step(nc.scalar.activation(e, src, ACT.Exp, scale=-1.0))
                        step(nc.scalar.activation(e, e, ACT.Ln, bias=1.0))
                        nc.scalar.activation(e, e, ACT.Exp, scale=-1.0).then_inc(sem("sigmoid_ready"), 1)
                    split_hi(w + 2)

            def prep_ab(l):
                n_i = [n_q(l) if i in Q_FEATS else T for i in range(6)]
                for i, n in enumerate(n_i):
                    nc.scalar.activation(rab[:, i, 0:n], ft[i][:, 0:n], ACT.Square).then_inc(sem("sqab_ready"), 1)
                for i, n in enumerate(n_i):
                    act.wait_ge(sem("msab_ready"), T_("msab").add())
                    nc.scalar.activation(rab[:, i, 0:n], pair(i, 0, n), ACT.Ln, bias=eps[:, 0:1],
                                         scale=1.0 / HD).then_inc(sem("lnab_done"), 1)
                for i, n in enumerate(n_i):
                    act.wait_ge(sem("lnab_done"), T_("lnab").add())
                    nc.scalar.activation(rab[:, i, 0:n], rab[:, i, 0:n], ACT.Exp,
                                         scale=-0.5).then_inc(sem("rab_ready"), 1)

            def attention(l):
                units = att_units(l)
                n = len(units)
                e0, t0, p0 = T_("nb").n, T_("tr").n, T_("pv").n

                def evac(u):
                    _, j, _ = units[u]
                    m = units[u][0]
                    _, keys, _ = key_span(m, j)
                    act.wait_ge(sem("tr_done"), t0 + u + 1)
                    if u >= 2:
                        act.wait_ge(sem("pv_done"), p0 + u - 1)
                    nc.scalar.activation(probT[u % 2][:, 0:len(keys) * P], bank(4, 0, len(keys) * P),
                                         ACT.Copy).then_inc(sem("pt_ready"), 1)

                for u, (m, j, h) in enumerate(units):
                    lo, keys, _ = key_span(m, j)
                    jj = u // 4
                    act.wait_ge(sem("nb_ready"), e0 + u + 1)
                    if u >= 2:
                        act.wait_ge(sem("tr_done"), t0 + u - 1)
                    nc.scalar.activation(prob[u % 2][:, 0:T - lo], pair(u, lo, T - lo), ACT.Exp,
                                         bias=nb[:, jj % 2, h:h + 1], scale=HD ** -0.5,
                                         accum_out=psum_e[:, jj % 2, h:h + 1]).then_inc(sem("exp_done"), 1)
                    if m == 1 and h == 3:
                        nc.scalar.activation(es[:, jj % 2, :], se[:, jj % 2, :],
                                             ACT.Exp).then_inc(sem("es_ready"), 1)
                    if u >= 1:
                        evac(u - 1)
                evac(n - 1)
                T_("nb").add(n), T_("tr").add(n), T_("pv").add(n)

            def gla(l):
                for d in range(2):
                    act.wait_ge(sem("pre_done"), T_("pre").add())
                    nc.scalar.activation(pre[d][:], pair(d, 0, T), ACT.Identity, bias=lvec(l, LV_BG + d),
                                         scale=1.0).then_inc(sem("pre_ready"), 1)
                act.wait_ge(sem("abs_ready"), T_("abs").add(2))
                step(nc.scalar.activation(ls[:], ls[:], ACT.Exp))
                nc.scalar.activation(ls[:], ls[:], ACT.Ln, bias=1.0).then_inc(sem("softplus_ready"), 1)
                act.wait_ge(sem("ex_raw"), T_("exr").add())
                nc.scalar.activation(ex[:], ex[:], ACT.Exp, scale=1.0 / GLA_TAU).then_inc(sem("ex_ready"), 1)
                nc.scalar.activation(dex[:], dex[:], ACT.Exp, scale=1.0 / GLA_TAU).then_inc(sem("ex_ready"), 1)
                for d in range(2):
                    act.wait_ge(sem("kt_done"), T_("kt").add())
                    nc.scalar.activation(ktc[d][:], pair(d, 0, T), ACT.Copy).then_inc(sem("ktc_ready"), 1)
                act.wait_ge(sem("kdec_ready"), T_("kdec").add(2))
                for d in range(2):
                    nc.scalar.activation(ex[:, d, :], bb[d][:], ACT.Exp,
                                         scale=1.0 / GLA_TAU).then_inc(sem("ex_ready"), 1)
                n_lev = [nt for _, nt in halves(l) for _ in range(8)]

                def level_exp(it, nt):
                    b = it % 2
                    act.wait_ge(sem("e_raw"), T_("er").add())
                    nc.scalar.activation(eqk[b][:, :, 0:nt * P], eqk[b][:, :, 0:nt * P], ACT.Exp,
                                         scale=1.0 / GLA_TAU).then_inc(sem("e_ready"), 1)

                def level_blocks(it, j0, nt):
                    b, li = it % 2, it % 8
                    if li > 0:
                        act.wait_ge(sem("lev_q"), T_("lq").add())
                    if it >= 2:
                        act.wait_ge(sem("lev_done"), T_("lev").n + sum(n_lev[:it - 1]))
                    src = eqk[b][:, 0, 0:nt * P] if li > 0 else ft[6][:, j0 * P:(j0 + nt) * P]
                    for h in range(4):
                        r = slice(32 * h, 32 * h + 32)
                        ins = nc.scalar.activation(qbd[b][r, 0:nt, h, :], src[r, :].rearrange("p (j t) -> p j t", t=P),
                                                   ACT.Copy, scale=1.0 if li > 0 else 2.0)
                    ins.then_inc(sem("lev_blocks"), 1)

                for hf, (j0, nt) in enumerate(halves(l)):
                    for li in range(8):
                        it = hf * 8 + li
                        if it == 0:
                            act.wait_ge(sem("qbd_zero"), T_("qbz").add())
                        if li < 7:
                            level_exp(it + 1, nt)
                        level_blocks(it, j0, nt)
                    for t in range(nt):
                        act.wait_ge(sem("oc_done"), T_("oc").add())
                        nc.scalar.activation(y[:, j0 + t, 512:768], bank(4 + (j0 + t) % 2, 0, 256),
                                             ACT.Copy).then_inc(sem("yc_ready"), 1)
                T_("lev").add(sum(n_lev))

            def mlstm(l):
                for a, n in ((0, 4), (4, 2)):
                    act.wait_ge(sem("kd_done"), T_("kd").add())
                    nc.scalar.activation(ktd[:, a:a + n, :], pair(a // 4, 0, n * 256).rearrange(
                        "p (j c) -> p j c", j=n), ACT.Copy).then_inc(sem("ktd_ready"), 1)
                for p_ in range(2):
                    for hf in range(2):
                        rr = slice(64 * hf, 64 * hf + 64)
                        nc.scalar.activation(qdb[rr, 2 * p_ + hf, 0:n_q(l)], ft[8 + p_][rr, 0:n_q(l)],
                                             ACT.Copy).then_inc(sem("qdb_ready"), 1)
                k = 0
                for s in range(TILES):
                    for d in range(2):
                        j = ORDER[d][s]
                        if l == DEPTH - 1 and j >= LAT_TILES:
                            continue
                        act.wait_ge(sem("mb_done"), T_("mb").add())
                        if k >= 4:
                            act.wait_ge(sem("num_done"), T_("num").n + k - 3)
                        for h in range(4):
                            ins = nc.scalar.activation(wb[s % 2][:, d, h, :], bank(d, h * P, P), ACT.Exp,
                                                       bias=col[:, j, 0, d, h:h + 1], scale=-1.0)
                        ins.then_inc(sem("w_ready"), 1)
                        k += 1
                T_("num").add(k)

            def finish(l):
                nj = TILES if l == 0 else LAT_TILES
                for j in range(nj):
                    nc.scalar.activation(sqy[:, j, :], y[:, j, 512:1024], ACT.Square).then_inc(sem("sqy_ready"), 1)
                act.wait_ge(sem("ms8_ready"), T_("ms8").add())
                step(nc.scalar.activation(ms8[:, 0:nj * 8], ms8[:, 0:nj * 8], ACT.Ln, bias=eps[:, 0:1],
                                          scale=1.0 / HD))
                nc.scalar.activation(ms8[:, 0:nj * 8], ms8[:, 0:nj * 8], ACT.Exp,
                                     scale=-0.5).then_inc(sem("rstd8_ready"), 1)
                for j in range(nj):
                    act.wait_ge(sem("yt_done"), T_("yt").add())
                    nc.scalar.activation(yT_hi[:, :, cols(j)], pair(j).rearrange("p (k t) -> p k t", k=KD),
                                         ACT.Copy).then_inc(sem("yt_hi"), 1)

            def mlp_quarter(l, n_t, w0, i, last):
                def hid_high(m):
                    act.wait_ge(sem("sq2_ready"), T_("sq2").add())
                    nc.scalar.activation(hid_hi[:, m, 0:n_t], tmp[2 + m % 2][:, 0:n_t],
                                         ACT.Copy).then_inc(sem("hid_hi_ready"), 1)
                for s in range(QW1 + QW2):
                    for m in range(2):
                        g = 2 * s + m
                        big.add()
                        if s < QW1:
                            act.wait_ge(sem("big_done"), big.at(0))
                            if g >= 2:
                                act.wait_ge(sem("sq2_ready"), T_("sq2").at(0))
                            nc.scalar.activation(tmp[6 + g % 2][:, 0:n_t], pair(g, 0, n_t),
                                                 ACT.Relu).then_inc(sem("relu_done"), 1)
                            if g >= 1:
                                hid_high(g - 1)
                    if s == QW1 - 1:
                        hid_high(2 * QW1 - 1)
                    if not (last and s >= QW1 + QW2 - 2):
                        split_hi(w0 + s + 2, i)

            x_total = 0
            for l in range(DEPTH):
                n_t = T if l == 0 else SEQ
                w0 = l * LAYER_SLOTS
                norm(l, 1, T, x_total)
                in_proj(l)
                stage_end()
                prep_ab(l)
                attention(l)
                stage_end()
                gla(l)
                stage_end()
                mlstm(l)
                stage_end()
                finish(l)
                for s in range(OUT_SLOTS):
                    big.add(2)
                    split_hi(w0 + IN_SLOTS + s + 2)
                x_total += KD
                norm(l, 2, n_t, x_total)
                n_loop = QUARTERS if l < DEPTH - 1 else QUARTERS - 1
                q0 = w0 + IN_SLOTS + OUT_SLOTS
                with act.Fori(0, n_loop) as i:
                    big.enter(i, 16)
                    T_("sq2").enter(i, 8)
                    mlp_quarter(l, n_t, q0, i, False)
                big.leave(n_loop)
                T_("sq2").leave(n_loop)
                if l == DEPTH - 1:
                    mlp_quarter(l, n_t, q0 + 8 * n_loop, None, True)
                x_total += KD * QUARTERS

        @blk.vector
        def _(dve):
            c = {}

            def T_(name):
                return c.setdefault(name, Tally())

            big = Tally()
            own = Tally()

            def step(ins):
                ins.then_inc(sem("dve_step"), 1)
                dve.wait_ge(sem("dve_step"), own.add())

            stage_n = [0]

            def stage_end():
                dve.drain().then_inc(sem("stage_done"), 1)
                stage_n[0] += 3
                dve.wait_ge(sem("stage_done"), stage_n[0])

            v = nc.vector

            v.memset(ones[:], 1.0)
            v.memset(eps[:], EPS).then_inc(sem("ones_ready"), 1)
            dve.wait_ge(sem("v_trans"), 1)
            v.tensor_copy(vcol[1][:], bank(7, P, LV))
            v.tensor_copy(vcol[0][:], bank(7, 0, V_ALL)).then_inc(sem("v_cols"), 1)
            dve.wait_ge(sem("v_cols"), 1)
            dve.wait_ge(sem("c_exp"), 1)
            step(v.tensor_scalar(cs[:], cs[:], 1.0, None, ALU.add))
            step(v.reciprocal(cs[:], cs[:]))
            v.tensor_tensor(cs[:, :, 0], cs[:, :, 0], vcol[0][:, V_C:V_C + KD], ALU.mult)
            v.tensor_tensor(cs[:, :, 1], cs[:, :, 1], vcol[0][:, V_CC:V_CC + KD], ALU.mult).then_inc(sem("cs_ready"), 1)

            def make_masks():
                dve.wait_ge(sem("masks_landed"), 16)
                dve.wait_ge(sem("c_landed"), 48)
                v.tensor_copy(lmask[:], cload[:, 0:8 * P].rearrange("p (a b) -> p a b", a=8))
                v.tensor_copy(ident_b[:], ident)
                v.tensor_scalar(m_left[:], cload[:, C_LEFT - C_KEEP:C_LEFT - C_KEEP + P], -BIG, None, ALU.mult)
                v.tensor_scalar(m_right[:], cload[:, C_RIGHT - C_KEEP:C_RIGHT - C_KEEP + P], -BIG, None, ALU.mult)
                v.tensor_scalar(p_after[:], cload[:, C_LEFT - C_KEEP:C_LEFT - C_KEEP + P], BIG, None, ALU.mult)
                v.tensor_scalar(p_before[:], cload[:, C_RIGHT - C_KEEP:C_RIGHT - C_KEEP + P], BIG, None,
                                ALU.mult).then_inc(sem("masks_ready"), 1)

            mod_n = Tally()
            sum_n = Tally()

            def mod_out(l, s, i=None):
                dve.wait_ge(sem("mod_used"), mod_n.at(FIRST_MODS + 1))
                mod_n.add()
                if i is None:
                    a, b = modt[l][:, 4 * s:4 * s + 4], lvec(l, LV_BMOD + 2 * s, 2)
                else:
                    a = modt[l][:, bass.ds(i * (4 * Q_MODS) + 4 * s, 4)]
                    b = vcol[l][:, bass.ds(i * (2 * Q_MODS) + (LV_BMOD + 2 * s), 2)]
                v.tensor_tensor(a.rearrange("p (m c) -> p m c", c=2), bank(6, 0, 4).rearrange("p (m c) -> p m c", c=2),
                                bc(b, 2), ALU.add).then_inc(sem("mod_out"), 1)

            def mod_sum(half):
                if half == 0:
                    dve.wait_ge(sem("mod_landed"), sum_n.at(1) * 16)
                    dve.wait_ge(sem("mod_used"), sum_n.at(FIRST_MODS))
                for k in range(4 * half, 4 * half + 4):
                    for c_i in range(2):
                        if k == 0:
                            ins = v.tensor_scalar(mod_acc[:, c_i, :], raw[1][:, k, :], cs[:, k, c_i:c_i + 1], None,
                                                  ALU.mult)
                        else:
                            dve.wait_ge(sem("dve_step"), own.at(0 if (k, c_i) == (KD - 1, 1) else -1))
                            ins = v.scalar_tensor_tensor(mod_acc[:, c_i, :], raw[1][:, k, :], cs[:, k, c_i:c_i + 1],
                                                         mod_acc[:, c_i, :], ALU.mult, ALU.add)
                        if k < KD - 1:
                            ins.then_inc(sem("dve_step"), 1)
                            own.add()
                        else:
                            ins.then_inc(sem("mod_summed"), 1)
                if half == 1:
                    sum_n.add()

            def norm(l, which, n_t):
                sqn = T_("sq")
                mt = modt[l][:].rearrange("p (m c) -> p m c", c=2)
                m0 = 8 if which == 1 else 32
                for k in range(1, KD):
                    dve.wait_ge(sem("sq_ready"), sqn.n + k + 1)
                    if k >= 2:
                        dve.wait_ge(sem("acc_added"), T_("acc").n + k - 1)
                    v.tensor_tensor(tmp[2][:, 0:n_t], tmp[0][:, 0:n_t] if k == 1 else tmp[2][:, 0:n_t],
                                    tmp[k % 2][:, 0:n_t], ALU.add).then_inc(sem("acc_added"), 1)
                sqn.add(KD)
                T_("acc").add(KD - 1)
                if l == 0 and which == 1:
                    for r in range(2):
                        dve.wait_ge(sem("mod_used"), FIRST_MODS // 2 * (r + 1))
                        v.tensor_copy(mod_rows[0:2, r * 1024:(r + 1) * 1024],
                                      ps[0:2, r * 1024:(r + 1) * 1024]).then_inc(sem("mod_rows_ready"), 1)
                    dve.wait_ge(sem("mod_cols"), 1)
                    v.tensor_tensor(modt[0][:, 0:4 * FIRST_MODS].rearrange("p (m c) -> p m c", c=2),
                                    bank(6, 0, 4 * FIRST_MODS).rearrange("p (m c) -> p m c", c=2),
                                    bc(lvec(0, LV_BMOD, 2 * FIRST_MODS), 2), ALU.add).then_inc(sem("mod_out"), 1)
                dve.wait_ge(sem("mod_out"), mod_n.at(1))
                step(v.scalar_tensor_tensor(gs[:], mt[:, m0:m0 + KD, :], 1.0,
                                            bc(lvec(l, LV_G1 if which == 1 else LV_G2, KD), 2), ALU.add, ALU.mult))
                dve.wait_ge(sem("rstd_ready"), T_("rstd").add())

                def low(k):
                    dve.wait_ge(sem("h_hi_ready"), T_("hhi").add())
                    v.tensor_tensor(h_lo[:, k, 0:n_t], tmp[4 + k % 2][:, 0:n_t], h_hi[:, k, 0:n_t].bitcast(F32),
                                    ALU.subtract).then_inc(sem("h_ready"), 1)
                for k in range(KD):
                    if k >= 2:
                        dve.wait_ge(sem("h_full"), T_("hf").n + k - 1)
                    v.tensor_tensor(tmp[k % 2][:, 0:n_t], xT[:, k, 0:n_t], tmp[3][:, 0:n_t],
                                    ALU.mult).then_inc(sem("t_ready"), 1)
                    if k == 0 and l == 0 and which == 1:
                        make_masks()
                    if k >= 1:
                        low(k - 1)
                low(KD - 1)
                T_("hf").add(KD)

            def in_proj(l):
                for s in range(IN_SLOTS):
                    has_mod = mod_after(l, s) is not None
                    for m in range(2):
                        g = 2 * s + m
                        if has_mod:
                            mod_sum(m)
                        if m == 0 and s >= GATE_SLOT:
                            mlstm_gates(l, s - GATE_SLOT)
                        if m == 0 and s == GATE_SLOT + 1:
                            gate(l, 0)
                        if m == 0 and s == GATE_SLOT + 2:
                            gate(l, 1)
                        if g == FEATS:
                            continue
                        big.add()
                        if g < FEATS:
                            continue
                        dve.wait_ge(sem("big_done"), big.at(0))
                        j0, n = token_tiles(l, s, m)
                        src = pair(g, 0, n * 256).rearrange("p (j c) -> p j c", j=n)
                        if s == GATE_SLOT + 2:
                            dst = v_ab[:, j0:j0 + n, :]
                        elif s == GATE_SLOT + 3:
                            dst = vc[:, j0:j0 + n, :]
                        elif s == GATE_SLOT + 4:
                            dst = vd1[:, j0:j0 + n, :, 0:64]
                            src = pair(g, 0, n * 256).rearrange("p (j h c) -> p j h c", j=n, h=4)
                        else:
                            dst = ro[:, j0:j0 + n, (s - GATE_SLOT) * 256:(s - GATE_SLOT + 1) * 256]
                        v.tensor_copy(dst, src).then_inc(sem("vt_ready"), 1)
                    if has_mod:
                        mod_out(0, mod_after(l, s))
                v.memset(vd1[:, :, :, 64:65], 1.0)

            def mlstm_gates(l, part):
                gates = ft[12]
                R, F = slice(0, 36), slice(64, 100)

                def tt(ap):
                    return ap.rearrange("p (j t) -> p j t", t=P)

                if part == 0:
                    dve.wait_ge(sem("ft_ready"), FEATS * (l + 1))
                    f = gates[64:128, :]
                    v.scalar_tensor_tensor(lsf[64:128, :], f, -1.0, f, ALU.mult, ALU.min).then_inc(sem("absf_ready"), 1)
                    v.memset(r1[:], 0.0)
                    v.memset(r2[:], 0.0)
                    v.memset(mp[:], 0.0)
                    v.memset(mend[:], 0.0)
                    step(v.memset(dec[:], 0.0))
                elif part == 1:
                    dve.wait_ge(sem("softplusf_ready"), l + 1)
                    f = gates[64:128, :]
                    step(v.scalar_tensor_tensor(f, f, 0.0, lsf[64:128, :], ALU.min, ALU.subtract))
                    one = ones[64:68, 0:1].to_broadcast([4, P])
                    one1 = ones[96:100, 0:1].to_broadcast([4, P])
                    for j in range(TILES):
                        f0, f1 = gates[64:68, cols(j)], gates[96:100, cols(j)][:, ::-1]
                        v.tensor_tensor_scan(f0, one, f0, 0.0, ALU.mult, ALU.add)
                        last = v.tensor_tensor_scan(f1, one1, f1, 0.0, ALU.mult, ALU.add)
                    step(last)
                elif part in (2, 3):
                    if part == 2:
                        step(v.tensor_tensor(r1[R, :], gates[R, :], gates[F, :], ALU.subtract))
                    for s in range(TILES // 2 * (part - 2), TILES // 2 * (part - 1)):
                        for d in range(2):
                            j = ORDER[d][s]
                            r = slice(32 * d, 32 * d + 4)
                            a_, m_ = r1[r, cols(j)], gates[r, cols(j)]
                            if d == 1:
                                a_, m_ = a_[:, ::-1], m_[:, ::-1]
                            last = v.tensor_tensor_scan(m_, a_, a_, mp[r, j:j + 1], ALU.max, ALU.max)
                        step(last)
                        if s < TILES - 1:
                            for d in range(2):
                                j, jn = ORDER[d][s], ORDER[d][s + 1]
                                r = slice(32 * d, 32 * d + 4)
                                f = slice(64 + 32 * d, 68 + 32 * d)
                                e = j * P + (P - 1 if d == 0 else 0)
                                last = v.tensor_tensor(mp[r, jn:jn + 1], gates[f, e:e + 1], gates[r, e:e + 1], ALU.add)
                            step(last)
                if part == 3:
                    v.tensor_copy(mend[0:4, :], tt(gates[0:4, :])[:, :, P - 1])
                    step(v.tensor_copy(mend[32:36, :], tt(gates[32:36, :])[:, :, 0]))
                    v.tensor_tensor(tt(r1[64:100, :]), tt(r1[R, :]), bc(mend[R, :], P), ALU.subtract)
                    v.tensor_tensor(tt(r2[R, :]), bc(mp[R, :], P), tt(gates[R, :]), ALU.subtract)
                    v.scalar_tensor_tensor(r2[64:100, :], gates[F, :], -1.0, gates[R, :], ALU.mult, ALU.subtract)
                    v.tensor_tensor(dec[R, :], mp[R, :], mend[R, :], ALU.subtract).then_inc(sem("r_raw"), 1)
                elif part == 4:
                    for q in range(2):
                        dve.wait_ge(sem("r_trans"), T_("rtr").add())
                        v.tensor_copy(col[:, :, q, :, :], bank(4, 0, T).rearrange(
                            "p (j a b) -> p j a b", j=TILES, a=4)[:, :, :, 0:4]).then_inc(sem("col_ready"), 1)
                    dve.wait_ge(sem("dec_done"), T_("decd").add())
                    v.tensor_copy(dcb[:], bank(7, 0, 24).rearrange("p (a j) -> p a j",
                                                                   a=4)).then_inc(sem("dcb_ready"), 1)

            def gate(l, which):
                nj = n_q(l) // P
                half = ro[:, 0:nj, which * 256:(which + 1) * 256]
                e = (sig_r[:, 0:nj, :], half)[which]
                gain = rowc[:, 4 + 256 * which:260 + 256 * which].unsqueeze(1).to_broadcast([P, nj, 256])
                dve.wait_ge(sem("lay_landed"), 32 * (l + 1))
                dve.wait_ge(sem("sigmoid_ready"), T_("sig").add())
                if which == 0:
                    step(v.tensor_tensor(half, half, e, ALU.mult))
                v.tensor_tensor(half, half, gain, ALU.mult).then_inc(sem("gate_ready"), 1)

            def prep_ab(l):
                v.tensor_scalar(nsink[:], rowc[:, 0:4], -1.0, None, ALU.mult)
                for m in range(2):
                    v.memset(kb1[m][0:64, :], 0.0)
                for i in range(7):
                    if i >= 1:
                        dve.wait_ge(sem("rot_done"), T_("rot").n + i)
                    if i < 6:
                        v.tensor_scalar(gswap[:], swap, lvec(l, LV_GQK + G_OF[i]), None,
                                        ALU.mult).then_inc(sem("gswap_ready"), 1)
                    if i >= 1:
                        v.scalar_tensor_tensor(rt[i - 1][:], ft[i - 1][:, 0:SEQ], lvec(l, LV_GQK + G_OF[i - 1]), cos,
                                               ALU.mult, ALU.mult)
                        step(v.tensor_tensor(rt[6 + i % 2][:], bank(4 + (i - 1) % 4), sin, ALU.mult))
                        v.tensor_tensor(rt[i - 1][:], rt[i - 1][:], rt[6 + i % 2][:],
                                        ALU.add).then_inc(sem("turned"), 1)
                T_("rot").add(6)
                for i in range(3):
                    normed(l, i)

            lat, ctx_ = slice(0, SEQ), slice(SEQ, T)

            def normed(l, i):
                g = lvec(l, LV_GQK + G_OF[i])
                dve.wait_ge(sem("turned"), 6 * (l + 1))
                dve.wait_ge(sem("rab_ready"), T_("rab").add())
                if i in (2, 5):
                    k1 = kb1[i // 3]
                    a, b = slice(0, 64), slice(64, 128)
                    v.tensor_tensor(k1[b, lat], rt[i][b, :], rab[b, i, lat], ALU.mult)
                    step(v.scalar_tensor_tensor(k1[b, ctx_], ft[i][b, ctx_], g[b, :], rab[b, i, ctx_],
                                                ALU.mult, ALU.mult))
                    v.memset(ft[i][b, :], 0.0)
                    v.tensor_tensor(ft[i][a, lat], rt[i][a, :], rab[a, i, lat], ALU.mult)
                    ins = v.scalar_tensor_tensor(ft[i][a, ctx_], ft[i][a, ctx_], g[a, :], rab[a, i, ctx_],
                                                 ALU.mult, ALU.mult)
                else:
                    ins = v.tensor_tensor(ft[i][:, lat], rt[i][:], rab[:, i, lat], ALU.mult)
                    if n_q(l) == T:
                        ins = v.scalar_tensor_tensor(ft[i][:, ctx_], ft[i][:, ctx_], g, rab[:, i, ctx_],
                                                     ALU.mult, ALU.mult)
                ins.then_inc(sem("qk_ready"), 1)

            def attention(l):
                units = att_units(l)
                s0, p0 = T_("sc").n, T_("pv").n
                e0 = T_("exp").n

                def tile_out(jj):
                    m, j, _ = units[4 * jj]
                    jp = jj % 2
                    dve.wait_ge(sem("pv_done"), p0 + 4 * jj + 4)
                    dve.wait_ge(sem("exp_done"), e0 + 4 * jj + 4)
                    if m == 1:
                        dve.wait_ge(sem("es_ready"), T_("es").add())
                        step(v.tensor_tensor(psum_e[:, jp, :], psum_e[:, jp, :], es[:, jp, :], ALU.add))
                    step(v.reciprocal(rs[:, jp, :], psum_e[:, jp, :]))
                    v.tensor_tensor(y[:, j, m * 256:m * 256 + 256].rearrange("p (h c) -> p h c", h=4),
                                    bank(6 + jp, 0, 256).rearrange("p (h c) -> p h c", h=4),
                                    bc(rs[:, jp, :], 64), ALU.mult).then_inc(sem("yab_ready"), 1)

                for u, (m, j, h) in enumerate(units):
                    lo, keys, _ = key_span(m, j)
                    jp = u // 4 % 2
                    dve.wait_ge(sem("sc_done"), s0 + u + 1)
                    step(v.tensor_reduce(mx[:, u % 2:u % 2 + 1], pair(u, lo, T - lo), AX_X, ALU.max))
                    if m == 0:
                        v.tensor_scalar(nb[:, jp, h:h + 1], mx[:, u % 2:u % 2 + 1], -HD ** -0.5, None,
                                        ALU.mult).then_inc(sem("nb_ready"), 1)
                    else:
                        step(v.tensor_scalar(nb[:, jp, h:h + 1], mx[:, u % 2:u % 2 + 1], -HD ** -0.5,
                                             nsink[:, h:h + 1], ALU.mult, ALU.min))
                        v.tensor_tensor(se[:, jp, h:h + 1], nb[:, jp, h:h + 1], rowc[:, h:h + 1],
                                        ALU.add).then_inc(sem("nb_ready"), 1)
                    if u in (1, 3, 5):
                        normed(l, 3 + u // 2)
                    if h == 2 and u >= 4:
                        tile_out(u // 4 - 1)
                tile_out(len(units) // 4 - 1)
                T_("sc").add(len(units)), T_("pv").add(len(units)), T_("exp").add(len(units))

            def gla(l):
                qc, kc = ft[6], ft[7]
                for d in range(2):
                    dve.wait_ge(sem("pre_ready"), T_("pre").add())
                    v.scalar_tensor_tensor(ls[:, d, :], pre[d][:], -1.0, pre[d][:], ALU.mult,
                                           ALU.min).then_inc(sem("abs_ready"), 1)
                v.memset(snap[:, 0, ORDER[0][0], :], 0.0)
                v.memset(snap[:, 1, ORDER[1][0], :], 0.0)
                dve.wait_ge(sem("softplus_ready"), T_("sp").add())
                for d in range(2):
                    step(v.scalar_tensor_tensor(pre[d][:], pre[d][:], 0.0, ls[:, d, :], ALU.min, ALU.subtract))
                one = ones[:, 0:1].to_broadcast([P, P])
                for j in range(TILES):
                    v.tensor_tensor_scan(bb[0][:, cols(j)], one, pre[0][:, cols(j)], 0.0, ALU.mult, ALU.add)
                    last = v.tensor_tensor_scan(bb[1][:, cols(j)][:, ::-1], one, pre[1][:, cols(j)][:, ::-1], 0.0,
                                                ALU.mult, ALU.add)
                step(last)
                ends = [bb[0][:].rearrange("p (j t) -> p j t", t=P)[:, :, P - 1],
                        bb[1][:].rearrange("p (j t) -> p j t", t=P)[:, :, 0]]
                for d in range(2):
                    v.tensor_copy(dex[:, d, :], ends[d])
                    last = v.tensor_tensor(ex[:, d, :].rearrange("p (j t) -> p j t", t=P), bc(ends[d], P),
                                           bb[d][:].rearrange("p (j t) -> p j t", t=P), ALU.subtract)
                last.then_inc(sem("ex_raw"), 1)
                dve.wait_ge(sem("ex_ready"), T_("ex").add(2))
                for d in range(2):
                    v.tensor_tensor(kdec[d][:], kc[:], ex[:, d, :], ALU.mult).then_inc(sem("kdec_ready"), 1)
                for s in range(TILES - 1):
                    dve.wait_ge(sem("u_done"), T_("u").add())
                    step(v.tensor_tensor(umask[:].rearrange("p d (h c) -> p (d h) c", c=64),
                                         bank(4 + s % 2).rearrange("p (h c) -> p h c", c=64), bc(hm8, 64), ALU.mult))
                    for d in range(2):
                        a, b = ORDER[d][s], ORDER[d][s + 1]
                        last = v.scalar_tensor_tensor(snap[:, d, b, :], snap[:, d, a, :], dex[:, d, a:a + 1],
                                                      umask[:, d, :], ALU.mult, ALU.add)
                    last.then_inc(sem("snap_ready"), 1)
                    dve.wait_ge(sem("snap_ready"), T_("snap").add())
                dve.wait_ge(sem("ex_ready"), T_("ex").add(2))
                for d in range(2):
                    v.tensor_tensor(qe[d][:, 0:n_q(l)], qc[:, 0:n_q(l)], ex[:, d, 0:n_q(l)], ALU.mult).then_inc(sem("qe_ready"), 1)
                dve.wait_ge(sem("qe_ready"), T_("qe").add(2))
                v.tensor_copy(mx[:, 0:1], eps[:]).then_inc(sem("lev_start"), 1)
                v.memset(qbd[0][:], 0.0)
                v.memset(qbd[1][:], 0.0).then_inc(sem("qbd_zero"), 1)
                step(v.memset(sacc[:], 0.0))
                seq = levels(l)

                def decayed_q(it):
                    hf, li, j0, nt = seq[it]
                    if li > 0:
                        e = eqk[it % 2][:, 0, 0:nt * P]
                        dve.wait_ge(sem("e_ready"), T_("er").add())
                        v.tensor_tensor(e, qc[:, j0 * P:(j0 + nt) * P], e, ALU.mult).then_inc(sem("lev_q"), 1)

                def merge(it):
                    hf, li, j0, nt = seq[it]
                    if li == 0 and hf == 1:
                        dve.wait_ge(sem("oc_done"), T_("oc").n + 3)
                    if it >= 1:
                        dve.wait_ge(sem("lev_merged"), T_("mm").n)
                    for t in range(nt):
                        k = T_("mm").n
                        dve.wait_ge(sem("lev_done"), T_("lev").n + T_("mm").add() - T_("mm0").n)
                        v.copy_predicated(sacc[:, t], lmask[:, li, :].unsqueeze(1).to_broadcast([P, 4, P]),
                                          bank(k % 4).rearrange("p (h t) -> p h t", h=4)).then_inc(sem("lev_merged"), 1)

                T_("mm0").n = T_("mm").n
                for it in range(len(seq)):
                    decayed_q(it)
                    if it >= 1:
                        merge(it - 1)
                merge(len(seq) - 1)
                n_mm = sum(q[3] for q in seq)
                T_("lev").add(n_mm)
                T_("oc").add(sum(nt for _, nt in halves(l)))

            def mlstm(l):
                for h in range(4):
                    a = 64 - 64 * (h % 2)
                    v.memset(qdb[a:a + 64, h, 0:n_q(l)], 0.0)
                v.memset(cst_d[:], 0.0).then_inc(sem("qdb_zero"), 1)
                dve.wait_ge(sem("qdb_zero"), l + 1)
                seen = set()
                for s in range(TILES):
                    cur_, nxt = s % 2, (s + 1) % 2
                    for d in range(2):
                        j = ORDER[d][s]
                        if s < TILES - 1:
                            if s >= 1:
                                dve.wait_ge(sem("ud_done"), T_("udv").add())
                            v.tensor_tensor(vw[:, d], vd1[:, j], bc(col[:, j, 0, 2 + d, :], 65),
                                            ALU.mult).then_inc(sem("vw_ready"), 1)
                    if s == TILES - 1:
                        T_("udv").add(2)
                    outs = [d for d in range(2) if not (l == DEPTH - 1 and ORDER[d][s] >= LAT_TILES)]
                    for d in outs:
                        dve.wait_ge(sem("w_ready"), T_("w").add())
                        dve.wait_ge(sem("qk_done"), T_("qkd").add())
                        v.tensor_tensor(wb[s % 2][:, d], wb[s % 2][:, d],
                                        bank(2 + d).rearrange("p (h t) -> p h t", h=4),
                                        ALU.mult).then_inc(sem("p_ready"), 1)
                    for d in range(2):
                        j = ORDER[d][s]
                        if s < TILES - 1:
                            dve.wait_ge(sem("ud_done"), T_("ud").add())
                            for p_ in range(2):
                                last = v.scalar_tensor_tensor(
                                    cst_d[:, d, nxt, p_, :], cst_d[:, d, cur_, p_, :], dcb[:, 2 * d + p_, j:j + 1],
                                    bank(d, p_ * 65, 65), ALU.mult, ALU.add)
                            last.then_inc(sem("state_ready"), 1)
                            dve.wait_ge(sem("state_ready"), T_("st").add())
                    for d in outs:
                        j = ORDER[d][s]
                        dve.wait_ge(sem("num_done"), T_("num").add())
                        inter = bank(6 + d, 0, 260).rearrange("p (h c) -> p h c", h=4)
                        intra = bank(4 + d, 0, 260).rearrange("p (h c) -> p h c", h=4)
                        step(v.tensor_tensor(t1[:, d], inter, bc(col[:, j, 1, d, :], 65), ALU.mult))
                        step(v.tensor_tensor(t2[:, d], t1[:, d], intra, ALU.add))
                        step(v.scalar_tensor_tensor(dd[:, d, :], t2[:, d, :, 64], -1.0, t2[:, d, :, 64],
                                                    ALU.mult, ALU.max))
                        step(v.tensor_tensor(dd[:, d, :], dd[:, d, :], col[:, j, 1, 2 + d, :], ALU.max))
                        step(v.reciprocal(rd[:, d, :], dd[:, d, :]))
                        dst = y[:, j, 768:1024].rearrange("p (h c) -> p h c", h=4)
                        if j in seen:
                            step(v.tensor_tensor(hh[:, d], t2[:, d, :, 0:64], bc(rd[:, d, :], 64), ALU.mult))
                            v.tensor_tensor(dst, dst, hh[:, d], ALU.add).then_inc(sem("yd_ready"), 1)
                        else:
                            seen.add(j)
                            v.tensor_tensor(dst, t2[:, d, :, 0:64], bc(rd[:, d, :], 64),
                                            ALU.mult).then_inc(sem("yd_ready"), 1)
                        dve.wait_ge(sem("yd_ready"), T_("yd").add())

            def finish(l):
                nj = TILES if l == 0 else LAT_TILES
                for j in range(nj):
                    dve.wait_ge(sem("sqy_ready"), T_("sqy").add())
                    ins = v.tensor_reduce(ms8[:, 8 * j:8 * j + 8], sqy[:, j, :].rearrange("p (h c) -> p h c", c=64),
                                          AX_X, ALU.add)
                ins.then_inc(sem("ms8_ready"), 1)
                dve.wait_ge(sem("gate_ready"), 2 * (l + 1))
                for j in range(nj):
                    yg = y[:, j, 512:1024]
                    ins = v.tensor_tensor(yg, yg, ro[:, j, :], ALU.mult)
                step(ins)
                dve.wait_ge(sem("rstd8_ready"), T_("r8").add())

                def low(j):
                    dve.wait_ge(sem("yt_hi"), T_("yth").add())
                    v.tensor_tensor(yT_lo[:, :, cols(j)], pair(j).rearrange("p (k t) -> p k t", k=KD),
                                    yT_hi[:, :, cols(j)].bitcast(F32), ALU.subtract).then_inc(sem("yt_ready"), 1)
                for j in range(nj):
                    yj = y[:, j, 512:1024].rearrange("p (h c) -> p h c", c=64)
                    v.tensor_tensor(yj, yj, bc(ms8[:, 8 * j:8 * j + 8], 64), ALU.mult).then_inc(sem("y_ready"), 1)
                    if j >= 1:
                        low(j - 1)
                low(nj - 1)

            def residual(l, n_t, k, ga):
                mt = modt[l][:].rearrange("p (m c) -> p m c", c=2)
                dve.wait_ge(sem("big_done"), big.add())
                v_ = T_("xd")
                for c_i, a, b in [(0, 0, SEQ)] + ([(1, SEQ, T)] if n_t == T else []):
                    ins = v.scalar_tensor_tensor(xT[:, k, a:b], pair(k, a, b - a), mt[:, ga + k, c_i:c_i + 1],
                                                 xT[:, k, a:b], ALU.mult, ALU.add)
                ins.then_inc(sem("x_done"), 1)
                v_.add()

            def mlp_quarter(l, n_t, i):
                def hid_low(m):
                    dve.wait_ge(sem("hid_hi_ready"), T_("hh2").add())
                    v.tensor_tensor(hid_lo[:, m, 0:n_t], tmp[2 + m % 2][:, 0:n_t],
                                    hid_hi[:, m, 0:n_t].bitcast(F32), ALU.subtract).then_inc(sem("hid_ready"), 1)
                dve.wait_ge(sem("x_done"), T_("xd").at(0))
                for s in range(QW1 + QW2):
                    has_mod = l == 0 and s < Q_MODS
                    for m in range(2):
                        g = 2 * s + m
                        if has_mod:
                            mod_sum(m)
                        if s < QW1:
                            big.add()
                            dve.wait_ge(sem("relu_done"), T_("relu").add())
                            if g >= 2:
                                dve.wait_ge(sem("hid_ready"), T_("hh2").at(0))
                            v.tensor_tensor(tmp[2 + g % 2][:, 0:n_t], tmp[6 + g % 2][:, 0:n_t],
                                            tmp[6 + g % 2][:, 0:n_t], ALU.mult).then_inc(sem("sq2_ready"), 1)
                            if g >= 1:
                                hid_low(g - 1)
                        else:
                            residual(l, n_t, g - 2 * QW1, 40)
                    if s == QW1 - 1:
                        hid_low(2 * QW1 - 1)
                    if has_mod:
                        mod_out(1, s, i)

            for l in range(DEPTH):
                n_t = T if l == 0 else SEQ
                norm(l, 1, T)
                in_proj(l)
                stage_end()
                prep_ab(l)
                attention(l)
                stage_end()
                gla(l)
                stage_end()
                mlstm(l)
                stage_end()
                finish(l)
                for s in range(OUT_SLOTS):
                    has_mod = mod_after(l, IN_SLOTS + s) is not None
                    for m in range(2):
                        if has_mod:
                            mod_sum(m)
                        if s == 0 and m == 0:
                            dve.wait_ge(sem("mod_out"), mod_n.at(1))
                        residual(l, n_t, 2 * s + m, 16)
                    if has_mod:
                        mod_out(0, mod_after(l, IN_SLOTS + s))
                norm(l, 2, n_t)
                n_loop = QUARTERS if l < DEPTH - 1 else QUARTERS - 1
                looped = [(big, 16), (T_("relu"), 8), (T_("hh2"), 8), (T_("xd"), 8),
                          (mod_n, Q_MODS if l == 0 else 0), (sum_n, Q_MODS if l == 0 else 0),
                          (own, Q_MODS * 2 * (KD - 1) if l == 0 else 0)]
                with dve.Fori(0, n_loop) as i:
                    for t, per in looped:
                        t.enter(i, per)
                    mlp_quarter(l, n_t, i)
                for t, per in looped:
                    t.leave(n_loop)
                if l == DEPTH - 1:
                    mlp_quarter(l, n_t, None)
            for j in range(LAT_TILES):
                dve.wait_ge(sem("out_trans"), j + 1)
                if j >= 2:
                    dve.wait_ge(sem(f"out_stored{j % 2}"), 16 * (j // 2))
                v.tensor_copy(xout[j % 2][:], pair(j)).then_inc(sem("out_ready"), 1)

        @blk.tensor
        def _(pe):
            c = {}

            def T_(name):
                return c.setdefault(name, Tally())

            mm = nc.tensor.matmul
            stage_n = [0]

            def stage_end():
                pe.drain().then_inc(sem("stage_done"), 1)
                stage_n[0] += 3
                pe.wait_ge(sem("stage_done"), stage_n[0])

            pe.wait_ge(sem("c_landed"), 48)
            nc.tensor.transpose(bank(7, P, LV), vin1[0:LV, :], ident[0:LV, 0:LV])
            nc.tensor.transpose(bank(7, 0, V_ALL), vin[0:V_ALL, :], ident[0:V_ALL, 0:V_ALL]).then_inc(sem("v_trans"), 1)

            for j in range(TILES):
                pe.wait_ge(sem(f"x_landed{j}"), 16)
                if j >= 2:
                    pe.wait_ge(sem("x_in"), j - 1)
                for k in range(KD):
                    ins = nc.tensor.transpose(pair(j, k * P, P), xin[j][:, k * P:(k + 1) * P], ident)
                ins.then_inc(sem("x_trans"), 1)

            mods, wts = Tally(), Tally()

            def first_mods(a, b):
                for j in range(a, b):
                    pe.wait_ge(sem(f"first_mod_landed{j}"), 16)
                    for k in range(KD):
                        ins = mm(ps[0:2, j * WC:(j + 1) * WC], cs[:, k, :], first_mod[j][:, k, :],
                                 start=(k == 0), stop=(k == KD - 1))
                    ins.then_inc(sem("mod_used"), 1)

            def first_mods_columns():
                pe.wait_ge(sem("mod_rows_ready"), 2)
                for m in range(2 * FIRST_MODS):
                    ins = nc.tensor.transpose(bank(6, 2 * m, 2), mod_rows[0:2, m * P:(m + 1) * P], ident[0:2, 0:2])
                ins.then_inc(sem("mod_cols"), 1)

            def mod_slot():
                pe.wait_ge(sem("mod_summed"), mods.add(2))
                pe.wait_ge(sem("mod_out"), mods_out.add())
                for m in range(2):
                    for c_i in range(2):
                        ins = mm(bank(6, 2 * m + c_i, 1), mod_acc[:, c_i, m * P:(m + 1) * P], ones[:, 0:1],
                                 start=True, stop=True)
                ins.then_inc(sem("mod_used"), 1)

            mods_out = Tally()

            def passes(r):
                return ((w_hi[r], 0), (w_hi[r], 1), (w_lo[r], 0))

            def feature_pair(g, r, mov, n_t, ready):
                spans = [(0, SEQ)] + ([(SEQ, T)] if n_t == T else [])
                for k in range(KD):
                    pe.wait_ge(ready[0], ready[1] + k + 1)
                    for m in range(2):
                        for q, (w, hl) in enumerate(passes(r)):
                            for a, b in spans:
                                ins = mm(pair(g + m, a, b - a), w[:, k, m * P:(m + 1) * P], mov[hl][:, k, a:b],
                                         start=(k == 0 and q == 0), stop=(k == KD - 1 and q == 2))
                        if k == KD - 1:
                            ins.then_inc(sem("big_done"), 1)

            def feature_group(g, r, m, mov, n_t, ready=None):
                spans = [(0, SEQ)] + ([(SEQ, T)] if n_t == T else [])
                for k in range(KD):
                    if ready is not None:
                        pe.wait_ge(ready[0], ready[1] + k + 1)
                    for q, (w, hl) in enumerate(passes(r)):
                        for a, b in spans:
                            ins = mm(pair(g, a, b - a), w[:, k, m * P:(m + 1) * P], mov[hl][:, k, a:b],
                                     start=(k == 0 and q == 0), stop=(k == KD - 1 and q == 2))
                ins.then_inc(sem("big_done"), 1)

            def norm_sum(n_t):
                pe.wait_ge(sem("acc_added"), T_("acc").add(KD - 1))
                all_ones = ones[:, 0:1].to_broadcast([P, P])
                ins = mm(bank(4), all_ones, tmp[2][:, 0:SEQ], start=True, stop=True)
                if n_t == T:
                    ins = mm(bank(5, 0, CTX), all_ones, tmp[2][:, SEQ:T], start=True, stop=True)
                ins.then_inc(sem("ms_ready"), 1)

            def gate_columns(q):
                if q == 0:
                    pe.wait_ge(sem("r_ready"), T_("r").add(3))
                else:
                    pe.wait_ge(sem("col_ready"), T_("r").n // 3 * 2 - 1)
                for j in range(TILES):
                    ins = nc.tensor.transpose(bank(4, j * P, P), (r1, r2)[q][:, cols(j)], ident)
                ins.then_inc(sem("r_trans"), 1)
                if q == 1:
                    for d in range(2):
                        for p_ in range(2):
                            for hf in range(2):
                                h = 4 * d + 2 * p_ + hf
                                a = 7 * 512 + (2 * d + p_) * TILES
                                ins = mm(ps[64 * hf:64 * hf + 64, a:a + TILES], sel[:, h:h + 1].to_broadcast([P, 64]),
                                         dec[:], start=True, stop=True)
                    ins.then_inc(sem("dec_done"), 1)

            def in_proj(l):
                ft0, vt0, h0 = T_("ft").n, T_("vt").n, T_("h").n
                for s in range(IN_SLOTS):
                    r = wts.n % 2
                    pe.wait_ge(sem("lo_ready"), wts.add())
                    for m in range(2):
                        g = 2 * s + m
                        if g == FEATS:
                            continue
                        if 2 <= g <= FEATS + 1:
                            pe.wait_ge(sem("ft_ready"), ft0 + min(g - 1, FEATS))
                        elif g > FEATS + 1:
                            n = g - FEATS - 2
                            if n >= 1:
                                pe.wait_ge(sem("vt_ready"), vt0 + n)
                        if g == 0:
                            feature_pair(0, r, (h_hi, h_lo), n_q(l), (sem("h_ready"), h0))
                        elif g == 1:
                            continue
                        elif g < FEATS:
                            feature_group(g, r, m, (h_hi, h_lo), n_q(l) if g in Q_FEATS else T)
                        else:
                            if s == IN_SLOTS - 1:
                                gate_columns(m)
                            j0, n = token_tiles(l, s, m)
                            for j in range(j0, j0 + n):
                                for k in range(KD):
                                    for q, (w, hl) in enumerate(passes(r)):
                                        ins = mm(pair(g, (j - j0) * 256, 256), (h_hi, h_lo)[hl][:, k, cols(j)],
                                                 w[:, k, :], start=(k == 0 and q == 0),
                                                 stop=(k == KD - 1 and q == 2))
                            ins.then_inc(sem("big_done"), 1)
                    if mod_after(l, s) is not None:
                        mod_slot()
                T_("ft").add(FEATS), T_("vt").add(10), T_("h").add(KD)

            def prep_ab(l):
                def mean_squares(i):
                    pe.wait_ge(sem("sqab_ready"), T_("sqab").add())
                    if i >= 2:
                        pe.wait_ge(sem("lnab_done"), T_("lnab").n + i - 1)
                    ins = mm(pair(i, 0, SEQ), block, rab[:, i, 0:SEQ], start=True, stop=True)
                    if n_q(l) == T or i not in Q_FEATS:
                        ins = mm(pair(i, SEQ, CTX), block, rab[:, i, SEQ:T], start=True, stop=True)
                    ins.then_inc(sem("msab_ready"), 1)

                def turn(i):
                    pe.wait_ge(sem("gswap_ready"), T_("gsw").add())
                    mm(bank(4 + i % 4), gswap[:], ft[i][:, 0:SEQ], start=True, stop=True).then_inc(sem("rot_done"), 1)

                for what, i in ((mean_squares, 0), (turn, 0), (mean_squares, 1), (turn, 1), (turn, 2),
                                (mean_squares, 2), (turn, 3), (mean_squares, 3), (turn, 4), (mean_squares, 4),
                                (turn, 5), (mean_squares, 5)):
                    what(i)
                T_("lnab").add(6)

            def attention(l):
                units = att_units(l)
                n = len(units)
                e0, y0, pt0 = T_("exp").n, T_("yab").n, T_("pt").n
                pe.wait_ge(sem("lnab_done"), T_("lnab").n)
                pe.wait_ge(sem("qk_ready"), T_("qk").add(3))

                def scores(u):
                    m, j, h = units[u]
                    lo, keys, masks = key_span(m, j)
                    if u == n // 2:
                        pe.wait_ge(sem("qk_ready"), T_("qk").add(3))
                    if u >= 2:
                        pe.wait_ge(sem("exp_done"), e0 + u - 1)
                    q = ft[3 * m + h % 2][:, cols(j)]
                    k_ = ft[3 * m + 2] if h < 2 else kb1[m]
                    if lo < 512:
                        mm(pair(u, lo, 512 - lo), q, k_[:, keys[0] * P:keys[0] * P + 512 - lo], start=True,
                           stop=not masks)
                        for x_, (mk, at) in enumerate(masks):
                            mm(pair(u, at, P), ident_b[:], mk[:], start=False, stop=(x_ == len(masks) - 1))
                    mm(pair(u, 512, CTX), q, k_[:, SEQ:T], start=True, stop=True).then_inc(sem("sc_done"), 1)

                def transposes(u):
                    m, j, h = units[u]
                    _, keys, _ = key_span(m, j)
                    pe.wait_ge(sem("exp_done"), e0 + u + 1)
                    if u >= 1:
                        pe.wait_ge(sem("pt_ready"), pt0 + u)
                    for t in range(len(keys)):
                        ins = nc.tensor.transpose(bank(4, t * P, P), prob[u % 2][:, cols(t)], ident)
                    ins.then_inc(sem("tr_done"), 1)

                def values(u):
                    m, j, h = units[u]
                    _, keys, _ = key_span(m, j)
                    jj = u // 4
                    pe.wait_ge(sem("pt_ready"), pt0 + u + 1)
                    if h == 0 and jj >= 2:
                        pe.wait_ge(sem("yab_ready"), y0 + jj - 1)
                    for t, kt in enumerate(keys):
                        ins = mm(bank(6 + jj % 2, h * 64, 64), probT[u % 2][:, cols(t)],
                                 v_ab[:, kt, m * P + (h // 2) * 64:m * P + (h // 2) * 64 + 64],
                                 start=(t == 0), stop=(t == len(keys) - 1))
                    ins.then_inc(sem("pv_done"), 1)

                scores(0)
                for u in range(n):
                    if u + 1 < n:
                        scores(u + 1)
                    if u >= 1:
                        values(u - 1)
                    transposes(u)
                values(n - 1)
                T_("exp").add(n), T_("yab").add(n // 4), T_("pt").add(n)

            def gla(l):
                for d in range(2):
                    pe.wait_ge(sem("lay_landed"), 32 * (l + 1))
                    mm(pair(d, 0, SEQ), wg[:, d, :], ft[12][:, 0:SEQ], start=True, stop=True)
                    mm(pair(d, SEQ, CTX), wg[:, d, :], ft[12][:, SEQ:T], start=True, stop=True)\
                        .then_inc(sem("pre_done"), 1)
                for d in range(2):
                    pe.wait_ge(sem("kdec_ready"), T_("kdec").add())
                    for j in range(TILES):
                        ins = nc.tensor.transpose(pair(d, j * P, P), kdec[d][:, cols(j)], ident)
                    ins.then_inc(sem("kt_done"), 1)
                pe.wait_ge(sem("ktc_ready"), T_("ktc").add(2))
                for s in range(TILES - 1):
                    if s >= 2:
                        pe.wait_ge(sem("snap_ready"), T_("snap").n + s - 1)
                    for d in range(2):
                        j = ORDER[d][s]
                        ins = mm(bank(4 + s % 2, d * 256, 256), ktc[d][:, cols(j)], vc[:, j, :], start=True, stop=True)
                    ins.then_inc(sem("u_done"), 1)
                T_("snap").add(TILES - 1)
                n_oc = 0
                for hf, (j0, nt) in enumerate(halves(l)):
                    for li in range(8):
                        b = (hf * 8 + li) % 2
                        pe.wait_ge(sem("lev_blocks"), T_("lb").add())
                        if li > 0:
                            pe.wait_ge(sem("kl_ready"), T_("kl").add())
                        for t in range(nt):
                            k = T_("mm").n
                            if k - T_("mm0").n >= 4:
                                pe.wait_ge(sem("lev_merged"), T_("mg").n + k - T_("mm0").n - 3)
                            kk = ft[7][:, cols(j0 + t)] if li == 0 else kl[b][:, cols(t)]
                            mm(bank(k % 4), kk, qbd[b][:, t], start=True, stop=True).then_inc(sem("lev_done"), 1)
                            T_("mm").add()
                    pe.wait_ge(sem("lev_merged"), T_("mg").n + T_("mm").n - T_("mm0").n)
                    if hf == 0:
                        pe.wait_ge(sem("qe_ready"), T_("qe").add(2))
                        pe.wait_ge(sem("snap_ready"), T_("snap").n)
                    for t in range(nt):
                        j = j0 + t
                        if n_oc >= 2:
                            pe.wait_ge(sem("yc_ready"), T_("yc").n + n_oc - 1)
                        ob = 4 + j % 2
                        mm(bank(ob, 0, 256), qe[0][:, cols(j)], snap[:, 0, j, :], start=True, stop=False)
                        mm(bank(ob, 0, 256), qe[1][:, cols(j)], snap[:, 1, j, :], start=False, stop=False)
                        for h in range(4):
                            ins = mm(bank(ob, h * 64, 64), sacc[:, t, h, :], vc[:, j, h * 64:h * 64 + 64],
                                     start=False, stop=(h == 3))
                        ins.then_inc(sem("oc_done"), 1)
                        n_oc += 1
                T_("mg").add(T_("mm").n - T_("mm0").n)
                T_("mm0").n = T_("mm").n
                T_("yc").add(n_oc)

            def mlstm(l):
                for a, n in ((0, 4), (4, 2)):
                    for j in range(a, a + n):
                        for p_ in range(2):
                            ins = nc.tensor.transpose(pair(a // 4, (j - a) * 256 + p_ * P, P),
                                                      ft[10 + p_][:, cols(j)], ident)
                    ins.then_inc(sem("kd_done"), 1)
                pe.wait_ge(sem("ktd_ready"), T_("ktd").add(2))
                pe.wait_ge(sem("qdb_ready"), T_("qdb").add(4))
                pe.wait_ge(sem("qdb_zero"), l + 1)
                st0 = T_("st").n
                for s in range(TILES):
                    cur_ = s % 2
                    outs = [d for d in range(2) if not (l == DEPTH - 1 and ORDER[d][s] >= LAT_TILES)]
                    if s >= 1:
                        pe.wait_ge(sem("state_ready"), st0 + 2 * s)
                    for d in outs:
                        j = ORDER[d][s]
                        mk = (p_after, p_before)[d]
                        mm(bank(d), ident_b[:], mk[:].unsqueeze(1).to_broadcast([P, 4, P]), start=True, stop=False)
                        for h in range(4):
                            ins = mm(bank(d, h * P, P), sel[:, 4 * d + h:4 * d + h + 1].to_broadcast([P, P]),
                                     ft[12][:, cols(j)], start=False, stop=(h == 3))
                        ins.then_inc(sem("mb_done"), 1)
                        if T_("pk").n >= 1:
                            pe.wait_ge(sem("p_ready"), T_("pr").n)
                        for p_ in range(2):
                            ins = mm(bank(2 + d, p_ * 256, 256), ft[10 + p_][:, cols(j)],
                                     qdb[:, 2 * p_:2 * p_ + 2, cols(j)], start=True, stop=True)
                        ins.then_inc(sem("qk_done"), 1)
                    if s < TILES - 1:
                        for d in range(2):
                            j = ORDER[d][s]
                            pe.wait_ge(sem("vw_ready"), T_("vw").add())
                            if d in outs:
                                pe.wait_ge(sem("w_ready"), T_("w").add())
                            for h in range(4):
                                hf = h % 2
                                a = d * 512 + (h // 2) * 65
                                ins = mm(ps[64 * hf:64 * hf + 64, a:a + 65], ktd[:, j, h * 64:h * 64 + 64],
                                         vw[:, d, h, :], start=True, stop=True)
                            ins.then_inc(sem("ud_done"), 1)
                    else:
                        T_("w").add(len(outs))
                    for d in outs:
                        j = ORDER[d][s]
                        pe.wait_ge(sem("p_ready"), T_("pr").add())
                        if T_("ydn").n >= 2:
                            pe.wait_ge(sem("yd_ready"), T_("ydn").n - 1)
                        T_("ydn").add()
                        T_("pk").add()
                        for h in range(4):
                            mm(bank(6 + d, h * 65, 65), qdb[:, h, cols(j)], cst_d[:, d, cur_, h // 2, :],
                               start=True, stop=True)
                        for h in range(4):
                            ins = mm(bank(4 + d, h * 65, 65), wb[s % 2][:, d, h, :], vd1[:, j, h, :],
                                     start=True, stop=True)
                        ins.then_inc(sem("num_done"), 1)
                T_("st").add(2 * (TILES - 1))

            def finish(l):
                nj = TILES if l == 0 else LAT_TILES
                lo0 = T_("ytl").n
                for j in range(nj):
                    pe.wait_ge(sem("y_ready"), T_("y").add())
                    if j >= 2:
                        pe.wait_ge(sem("yt_ready"), lo0 + j - 1)
                    for k in range(KD):
                        ins = nc.tensor.transpose(pair(j, k * P, P), y[:, j, k * P:(k + 1) * P], ident)
                    ins.then_inc(sem("yt_done"), 1)
                T_("ytl").add(nj)
                pe.wait_ge(sem("yt_ready"), T_("ytl").n)

            def out_proj(l, n_t):
                for s in range(OUT_SLOTS):
                    r = wts.n % 2
                    pe.wait_ge(sem("lo_ready"), wts.add())
                    for m in range(2):
                        k = 2 * s + m
                        if k >= 2:
                            pe.wait_ge(sem("x_done"), T_("xd").n - 1)
                        feature_group(k, r, m, (yT_hi, yT_lo), n_t)
                        T_("xd").add()
                    if mod_after(l, IN_SLOTS + s) is not None:
                        mod_slot()

            def mlp_quarter(l, n_t):
                for s in range(QW1 + QW2):
                    r = s % 2
                    pe.wait_ge(sem("lo_ready"), wts.add())
                    for m in range(2):
                        g = 2 * s + m
                        if g < 2:
                            if g == 0:
                                pe.wait_ge(sem("x_done"), T_("xd").at(0))
                        elif g < 10:
                            pe.wait_ge(sem("relu_done"), T_("relu").at(g - 9 if s >= QW1 else -1))
                        else:
                            pe.wait_ge(sem("x_done"), T_("xd").at(-1))
                        if s < QW1:
                            if g == 0:
                                feature_pair(0, r, (h_hi, h_lo), n_t, (sem("h_ready"), T_("h").n - KD))
                            elif g >= 2:
                                feature_group(g, r, m, (h_hi, h_lo), n_t)
                            T_("relu").add()
                        else:
                            if g == 2 * QW1:
                                feature_group(g, r, m, (hid_hi, hid_lo), n_t, (sem("hid_ready"), T_("hid").at(0)))
                                T_("hid").add(8)
                            else:
                                feature_group(g, r, m, (hid_hi, hid_lo), n_t)
                            T_("xd").add()
                    if l == 0 and s < Q_MODS:
                        mod_slot()

            for l in range(DEPTH):
                n_t = T if l == 0 else SEQ
                if l == 0:
                    pe.wait_ge(sem("cs_ready"), 1)
                    pe.wait_ge(sem("x_in"), TILES)
                    first_mods(0, 4)
                norm_sum(T)
                if l == 0:
                    first_mods(4, FIRST_MODS)
                    first_mods_columns()
                in_proj(l)
                stage_end()
                prep_ab(l)
                attention(l)
                stage_end()
                gla(l)
                stage_end()
                mlstm(l)
                stage_end()
                finish(l)
                out_proj(l, n_t)
                norm_sum(n_t)
                T_("h").add(KD)
                n_loop = QUARTERS if l < DEPTH - 1 else QUARTERS - 1
                looped = [(wts, 8), (T_("relu"), 8), (T_("hid"), 8), (T_("xd"), 8), (mods, 2 * Q_MODS if l == 0 else 0),
                          (mods_out, Q_MODS if l == 0 else 0)]
                with pe.Fori(0, n_loop) as i:
                    for t, per in looped:
                        t.enter(i, per)
                    mlp_quarter(l, n_t)
                for t, per in looped:
                    t.leave(n_loop)
                if l == DEPTH - 1:
                    mlp_quarter(l, n_t)
            pe.wait_ge(sem("x_done"), T_("xd").n)
            for j in range(LAT_TILES):
                if j >= 2:
                    pe.wait_ge(sem("out_ready"), j - 1)
                for k in range(KD):
                    ins = nc.tensor.transpose(pair(j, k * P, P), xT[:, k, cols(j)], ident)
                ins.then_inc(sem("out_trans"), 1)


def _slots(w, widths=WC):
    k, m = w.shape
    return w.reshape(k // P, P, m // widths, widths).transpose(2, 1, 0, 3).reshape(m // widths, P, -1)


def _in_columns():
    gw, kw, gk = 256, 128, 128
    names = [("qa", gw), ("ka", kw), ("va", kw), ("qb", gw), ("kb", kw), ("vb", kw), ("qc", gk), ("kc", gk),
             ("vc", gw), ("rc", gw), ("gc", 32), ("qd", gw), ("kd", gw), ("vd", gw), ("od", gw), ("id", 8), ("fd", 8)]
    at, c = {}, 0
    for n, w in names:
        at[n] = np.arange(c, c + w)
        c += w

    def q_pair(n, p):
        return np.concatenate([at[n][64 * p:64 * p + 64], at[n][64 * (p + 2):64 * (p + 2) + 64]])
    gates = -np.ones(P, dtype=np.int64)
    gates[0:4] = at["id"][0:4]
    gates[32:36] = at["id"][4:8]
    gates[16:32] = at["gc"][0:16]
    gates[48:64] = at["gc"][16:32]
    gates[64:68] = at["fd"][0:4]
    gates[96:100] = at["fd"][4:8]
    return np.concatenate([q_pair("qa", 0), q_pair("qa", 1), at["ka"], q_pair("qb", 0), q_pair("qb", 1), at["kb"],
                           at["qc"], at["kc"], at["qd"], at["kd"], gates, -np.ones(P, dtype=np.int64),
                           at["rc"], at["od"], at["va"], at["vb"], at["vc"], at["vd"]])


def _constants():
    c = np.zeros((P, C_ALL), np.float32)
    p = np.arange(P)
    c[:, C_IDENT:C_IDENT + P] = np.eye(P)
    c[:, C_BLOCK:C_BLOCK + P] = (p[:, None] // HD == p[None, :] // HD)
    sw = np.zeros((P, P), np.float32)
    e = np.arange(0, P, 2)
    sw[e + 1, e] = -1.0
    sw[e, e + 1] = 1.0
    c[:, C_SWAP:C_SWAP + P] = sw
    t = np.arange(SEQ)
    n_freq = HD // 4
    inv = np.float32(ROPE_THETA) ** (-np.arange(n_freq, dtype=np.float32) / np.float32(n_freq))
    row = (t // GRID_W).astype(np.float32)
    col = (t % GRID_W).astype(np.float32)
    ang = np.concatenate([row[:, None] * inv, col[:, None] * inv], axis=-1).astype(np.float32)
    idx = (p % HD) // 2
    c[:, C_COS:C_COS + SEQ] = np.cos(ang).T[idx]
    c[:, C_SIN:C_SIN + SEQ] = np.sin(ang).T[idx]
    for d in range(2):
        for h in range(4):
            c[32 * d + h, C_SEL + 4 * d + h] = 1.0
            c[32 * h:32 * h + 32, C_HM + 4 * d + h] = 1.0
    s_, t_ = p[:, None], p[None, :]
    c[:, C_LEVEL:C_LEVEL + P] = np.eye(P)
    for i, h in enumerate(LEVELS):
        same = (s_ // (2 * h)) == (t_ // (2 * h))
        c[:, C_LEVEL + (i + 1) * P:C_LEVEL + (i + 2) * P] = same & ((s_ // h) != (t_ // h))
    c[:, C_LEFT:C_LEFT + P] = t_ < s_
    c[:, C_RIGHT:C_RIGHT + P] = t_ > s_
    return c


def kernel(**inputs):
    import concourse.bacc as _bacc
    from concourse.bass_utils import run_bass_kernel_spmd as _run

    a = {k: np.ascontiguousarray(v) for k, v in inputs.items()}
    cols_ = _in_columns()
    slots, mods, vrows, gate, row_list = [], [], [a["c"][0].reshape(KD, P), a["c_ctx"].reshape(KD, P)], [], []
    for l in range(DEPTH):
        mods.append(_slots(a["w_mod"][l]))
        w_in = np.zeros((D_MODEL, len(cols_)), a["w_in"].dtype)
        w_in[:, cols_ >= 0] = a["w_in"][l][:, cols_[cols_ >= 0]]
        slots.append(_slots(w_in))
        slots.append(_slots(a["w_out"][l]))
        for q in range(QUARTERS):
            w = D_MODEL
            slots.append(_slots(a["w_mlp1"][l][:, q * w:(q + 1) * w]))
            slots.append(_slots(a["w_mlp2"][l][q * w:(q + 1) * w, :]))
        gb = np.zeros((1, P), np.float32)
        gb[0, 0:4], gb[0, 32:36] = a["b_mlstm_i"][l]
        gb[0, 64:68], gb[0, 96:100] = a["b_mlstm_f"][l]
        vrows += [a["b_mod"][l].reshape(48, P), a["g_norm1"][l].reshape(KD, P), a["g_norm2"][l].reshape(KD, P), gb]
        vrows += [np.tile(a[n][l], 2)[None] for n in ("g_q_a", "g_k_a", "g_q_b", "g_k_b")]
        vrows.append(a["b_gla_gate"][l])
        g = np.zeros((P, 2, P), np.float32)
        g[16:32, 0] = a["w_gla_gate"][l, 0]
        g[48:64, 1] = a["w_gla_gate"][l, 1]
        gate.append(g)
        row_list.append(np.concatenate([a["sink_b"][l], np.tile(a["g_gla_out"][l], 4), np.tile(a["g_mlstm_out"][l], 4)]))
    arrays = {
        "x_in": a["x"][0], "ctx_in": a["ctx"][0], "w_big": np.concatenate(slots), "w_modl": np.concatenate(mods),
        "vecs": np.concatenate(vrows), "consts": _constants(), "gla_gate": np.stack(gate), "rows": np.stack(row_list),
    }
    nc = _bacc.Bacc("TRN2", target_bir_lowering=False, num_devices=1)
    args = [nc.dram_tensor(n, v.shape, F32, kind="ExternalInput").ap() for n, v in arrays.items()]
    out = nc.dram_tensor("out", (SEQ, D_MODEL), F32, kind="ExternalOutput").ap()
    build(nc, *args, out)
    r = _run(nc, [arrays], core_ids=[0])
    return r.results[0]["out"][None]
```
